# Optimizing a Trainium2 kernel written in Bass

```python
import math
import jax, jax.numpy as jnp
from jax import lax
import numpy as np

D_MODEL = 1024
BATCH = 1
SEQ = 256
DEPTH = 1

N_HEADS_ATTN = 8
HEAD_DIM = 64
D_ATTN = N_HEADS_ATTN * HEAD_DIM
Q_BLOCK = 128
D_SSM = D_MODEL // 2
SSM_GROUP = 16
N_SSM_GROUPS = D_SSM // SSM_GROUP
SSM_STATE = 64
DT_MIN = 1e-3
DT_MAX = 1e-1
N_EXPERT_GROUPS = 4
EXPERTS_PER_GROUP = 8
N_EXPERTS = N_EXPERT_GROUPS * EXPERTS_PER_GROUP
TOP_K = 2
D_EXPERT = D_MODEL // 4
D_IN_PROJ = 3 * D_ATTN + N_HEADS_ATTN + D_SSM + 2 * D_MODEL
EPS = 1e-6
NEG_INF = -1e30


def _rmsnorm(x, g):
    xf = x.astype(jnp.float32)
    y = xf * lax.rsqrt(jnp.mean(xf * xf, axis=-1, keepdims=True) + EPS)
    return (y * g.astype(jnp.float32)).astype(x.dtype)

def _forgetting_attention(q, k, v, f_logit):
    b, s, h, d = q.shape
    n_blk = s // Q_BLOCK
    log_f = jax.nn.log_sigmoid(f_logit.astype(jnp.float32))
    cum = jnp.cumsum(log_f, axis=1).transpose(0, 2, 1)
    qf = q.astype(jnp.float32).transpose(0, 2, 1, 3) * (d ** -0.5)
    kf = k.astype(jnp.float32).transpose(0, 2, 1, 3)
    vf = v.astype(jnp.float32).transpose(0, 2, 1, 3)
    q_blk = qf.reshape(b, h, n_blk, Q_BLOCK, d).transpose(2, 0, 1, 3, 4)
    c_blk = cum.reshape(b, h, n_blk, Q_BLOCK).transpose(2, 0, 1, 3)
    pos = jnp.arange(s, dtype=jnp.int32)
    p_blk = pos.reshape(n_blk, Q_BLOCK)

    def one_block(args):
        qb, cb, pb = args
        logits = jnp.einsum('bhqd,bhkd->bhqk', qb, kf) + cb[..., :, None] - cum[:, :, None, :]
        causal = pos[None, :] <= pb[:, None]
        logits = jnp.where(causal, logits, NEG_INF)
        p = jax.nn.softmax(logits, axis=-1)
        return jnp.einsum('bhqk,bhkd->bhqd', p, vf)

    o = lax.map(one_block, (q_blk, c_blk, p_blk))
    return o.transpose(1, 0, 3, 2, 4).reshape(b, s, h, d).astype(v.dtype)

def _linear_combine(a, b):
    a1, b1 = a
    a2, b2 = b
    return a2 * a1, a2 * b1 + b2

def _s5(u, A_re, A_im, log_dt, B_re, B_im, C_re, C_im, D_skip, w_glu):
    f32 = jnp.float32
    b, s, _ = u.shape
    uf = u.astype(f32).reshape(b, s, N_SSM_GROUPS, SSM_GROUP)
    A = lax.complex(A_re.astype(f32), A_im.astype(f32))
    dt = jnp.exp(log_dt.astype(f32))[:, None]
    A_bar = jnp.exp(A * dt)
    Bm = lax.complex(B_re.astype(f32), B_im.astype(f32))
    B_bar = ((A_bar - 1.0) / A)[..., None] * Bm
    Bu = jnp.einsum('bsgc,gpc->bsgp', uf.astype(jnp.complex64), B_bar)
    A_seq = jnp.broadcast_to(A_bar, Bu.shape)
    _, state = lax.associative_scan(_linear_combine, (A_seq, Bu), axis=1)
    Cm = lax.complex(C_re.astype(f32), C_im.astype(f32))
    y = jnp.real(jnp.einsum('gcp,bsgp->bsgc', Cm, state))
    y = y + D_skip.astype(f32).reshape(N_SSM_GROUPS, SSM_GROUP) * uf
    y = jax.nn.gelu(y.reshape(b, s, D_SSM))
    y = y * jax.nn.sigmoid(y @ w_glu.astype(f32))
    return y.astype(u.dtype)

def _hier_moe(x, w_rg, b_rg, w_re, b_re, w_gate, w_up, w_down):
    f32 = jnp.float32
    b, s, d = x.shape
    t = b * s
    xt = x.reshape(t, d)
    g_prob = jax.nn.softmax((xt @ w_rg).astype(f32) + b_rg.astype(f32), axis=-1)
    g_top, g_sel = lax.top_k(g_prob, 1)
    e_logits = ((xt @ w_re).astype(f32) + b_re.astype(f32)).reshape(t, N_EXPERT_GROUPS, EXPERTS_PER_GROUP)
    idx = jnp.broadcast_to(g_sel[:, :, None], (t, 1, EXPERTS_PER_GROUP))
    e_in = jnp.take_along_axis(e_logits, idx, axis=1)[:, 0]
    e_prob = jax.nn.softmax(e_in, axis=-1)
    e_top, e_idx = lax.top_k(e_prob, TOP_K)
    w = g_top * e_top / jnp.sum(e_top, axis=-1, keepdims=True)
    expert_id = g_sel * EXPERTS_PER_GROUP + e_idx
    combine = jnp.sum(jax.nn.one_hot(expert_id, N_EXPERTS, dtype=f32) * w[..., None], axis=1).astype(x.dtype)
    y = jnp.zeros_like(xt)
    for e in range(N_EXPERTS):
        h = jax.nn.silu(xt @ w_gate[e]) * (xt @ w_up[e])
        y = y + combine[:, e:e + 1] * (h @ w_down[e])
    return y.reshape(b, s, d)

def first_inputs(seed: int = 0) -> dict:
    key = jax.random.key(seed)
    ks = jax.random.split(key, 32)
    f32 = jnp.float32
    nrm = lambda k, shape, scale: (jax.random.normal(k, shape, f32) * scale)
    L = DEPTH
    x = jax.random.normal(ks[0], (BATCH, SEQ, D_MODEL), f32)
    norm_mix_g = 1.0 + nrm(ks[1], (L, D_MODEL), 0.02)
    w_in = nrm(ks[2], (L, D_MODEL, D_IN_PROJ), D_MODEL ** -0.5)
    b_forget = jnp.broadcast_to(jnp.linspace(1.0, 6.0, N_HEADS_ATTN, dtype=f32), (L, N_HEADS_ATTN)) + nrm(ks[3], (L, N_HEADS_ATTN), 0.1)
    q_norm_g = 1.0 + nrm(ks[4], (L, HEAD_DIM), 0.02)
    k_norm_g = 1.0 + nrm(ks[5], (L, HEAD_DIM), 0.02)
    ssm_A_re = -0.5 + nrm(ks[6], (L, N_SSM_GROUPS, SSM_STATE), 0.01)
    ssm_A_im = jnp.pi * jnp.arange(SSM_STATE, dtype=f32)[None, None, :] + nrm(ks[7], (L, N_SSM_GROUPS, SSM_STATE), 0.01)
    ssm_log_dt = jax.random.uniform(ks[8], (L, N_SSM_GROUPS), f32, math.log(DT_MIN), math.log(DT_MAX))
    ssm_B_re = nrm(ks[9], (L, N_SSM_GROUPS, SSM_STATE, SSM_GROUP), (2 * SSM_GROUP) ** -0.5)
    ssm_B_im = nrm(ks[10], (L, N_SSM_GROUPS, SSM_STATE, SSM_GROUP), (2 * SSM_GROUP) ** -0.5)
    ssm_C_re = nrm(ks[11], (L, N_SSM_GROUPS, SSM_GROUP, SSM_STATE), (2 * SSM_STATE) ** -0.5)
    ssm_C_im = nrm(ks[12], (L, N_SSM_GROUPS, SSM_GROUP, SSM_STATE), (2 * SSM_STATE) ** -0.5)
    ssm_D = nrm(ks[13], (L, D_SSM), 1.0)
    w_glu = nrm(ks[14], (L, D_SSM, D_SSM), D_SSM ** -0.5)
    w_proj_attn = nrm(ks[15], (L, D_ATTN, D_MODEL), D_ATTN ** -0.5)
    w_proj_ssm = nrm(ks[16], (L, D_SSM, D_MODEL), D_SSM ** -0.5)
    w_out = nrm(ks[17], (L, D_MODEL, D_MODEL), D_MODEL ** -0.5)
    norm_ffn_g = 1.0 + nrm(ks[18], (L, D_MODEL), 0.02)
    w_router_group = nrm(ks[19], (L, D_MODEL, N_EXPERT_GROUPS), D_MODEL ** -0.5)
    b_router_group = nrm(ks[20], (L, N_EXPERT_GROUPS), 0.01)
    w_router_expert = nrm(ks[21], (L, D_MODEL, N_EXPERTS), D_MODEL ** -0.5)
    b_router_expert = nrm(ks[22], (L, N_EXPERTS), 0.01)
    w_expert_gate = nrm(ks[23], (L, N_EXPERTS, D_MODEL, D_EXPERT), D_MODEL ** -0.5)
    w_expert_up = nrm(ks[24], (L, N_EXPERTS, D_MODEL, D_EXPERT), D_MODEL ** -0.5)
    w_expert_down = nrm(ks[25], (L, N_EXPERTS, D_EXPERT, D_MODEL), D_EXPERT ** -0.5)
    return {"x": x, "norm_mix_g": norm_mix_g, "w_in": w_in, "b_forget": b_forget,
            "q_norm_g": q_norm_g, "k_norm_g": k_norm_g,
            "ssm_A_re": ssm_A_re, "ssm_A_im": ssm_A_im, "ssm_log_dt": ssm_log_dt,
            "ssm_B_re": ssm_B_re, "ssm_B_im": ssm_B_im, "ssm_C_re": ssm_C_re, "ssm_C_im": ssm_C_im,
            "ssm_D": ssm_D, "w_glu": w_glu, "w_proj_attn": w_proj_attn, "w_proj_ssm": w_proj_ssm,
            "w_out": w_out, "norm_ffn_g": norm_ffn_g,
            "w_router_group": w_router_group, "b_router_group": b_router_group,
            "w_router_expert": w_router_expert, "b_router_expert": b_router_expert,
            "w_expert_gate": w_expert_gate, "w_expert_up": w_expert_up, "w_expert_down": w_expert_down}

def first_block(x, norm_mix_g, w_in, b_forget, q_norm_g, k_norm_g,
              ssm_A_re, ssm_A_im, ssm_log_dt, ssm_B_re, ssm_B_im, ssm_C_re, ssm_C_im,
              ssm_D, w_glu, w_proj_attn, w_proj_ssm, w_out, norm_ffn_g,
              w_router_group, b_router_group, w_router_expert, b_router_expert,
              w_expert_gate, w_expert_up, w_expert_down):
    b, s, _ = x.shape
    splits = np.cumsum([D_ATTN, D_ATTN, D_ATTN, N_HEADS_ATTN, D_SSM, D_MODEL]).tolist()
    for l in range(DEPTH):
        h = _rmsnorm(x, norm_mix_g[l])
        z = h @ w_in[l]
        q, k, v, f, u_ssm, g_attn, g_ssm = jnp.split(z, splits, axis=-1)
        q = _rmsnorm(q.reshape(b, s, N_HEADS_ATTN, HEAD_DIM), q_norm_g[l])
        k = _rmsnorm(k.reshape(b, s, N_HEADS_ATTN, HEAD_DIM), k_norm_g[l])
        v = v.reshape(b, s, N_HEADS_ATTN, HEAD_DIM)
        y_attn = _forgetting_attention(q, k, v, f + b_forget[l]).reshape(b, s, D_ATTN)
        y_ssm = _s5(u_ssm, ssm_A_re[l], ssm_A_im[l], ssm_log_dt[l], ssm_B_re[l], ssm_B_im[l],
                    ssm_C_re[l], ssm_C_im[l], ssm_D[l], w_glu[l])
        mixed = (jax.nn.sigmoid(g_attn) * (y_attn @ w_proj_attn[l])
                 + jax.nn.sigmoid(g_ssm) * (y_ssm @ w_proj_ssm[l]))
        x = x + mixed @ w_out[l]
        x = x + _hier_moe(_rmsnorm(x, norm_ffn_g[l]), w_router_group[l], b_router_group[l],
                          w_router_expert[l], b_router_expert[l],
                          w_expert_gate[l], w_expert_up[l], w_expert_down[l])
    return x


DEPTH_2 = 2

N_MIXERS = 2
MEM_LEN = 256
MEM_HEADS = 4
MEM_WIDTH = MEM_HEADS * HEAD_DIM
MIX_WIDTH = D_MODEL - MEM_WIDTH
CONV_WIDTH = 31
MOBA_HEADS = MIX_WIDTH // HEAD_DIM
MOBA_BLOCK = 256
MOBA_TOPK = 3
Q_CHUNK = 64
N_GROUPS = 4
EXPERT_TOPK = 2
D_EXPERT_2 = 512
LN_EPS = 1e-5
DEEPNORM_ALPHA = (2 * DEPTH_2) ** 0.25
DEEPNORM_BETA = (8 * DEPTH_2) ** -0.25
N_CONV_LAYERS = (DEPTH_2 + 1) // 2
N_MOBA_LAYERS = DEPTH_2 // 2


def layer_norm(x, g, b):
    xf = x.astype(jnp.float32)
    mu = jnp.mean(xf, axis=-1, keepdims=True)
    var = jnp.mean(jnp.square(xf - mu), axis=-1, keepdims=True)
    return ((xf - mu) * lax.rsqrt(var + LN_EPS) * g + b).astype(x.dtype)

def conformer_conv(u, dw_w, dw_b, ln_g, ln_b):
    a, gate = jnp.split(u, 2, axis=-1)
    h = a * jax.nn.sigmoid(gate)
    h = lax.conv_general_dilated(
        h, dw_w[:, None, :], window_strides=(1,),
        padding=[(CONV_WIDTH - 1, 0)],
        dimension_numbers=('NWC', 'WIO', 'NWC'),
        feature_group_count=MIX_WIDTH) + dw_b
    h = layer_norm(h, ln_g, ln_b)
    return jax.nn.silu(h)

def memory_attention(q, mem_k, mem_v):
    s = jnp.einsum('bshd,bmhd->bhsm', q, mem_k).astype(jnp.float32) * (HEAD_DIM ** -0.5)
    p = jax.nn.softmax(s, axis=-1).astype(q.dtype)
    return jnp.einsum('bhsm,bmhd->bshd', p, mem_v)

def moba_attention(q, k, v):
    b_, h_, s_, hd = q.shape
    n_blocks = -(-s_ // MOBA_BLOCK)
    s_pad = n_blocks * MOBA_BLOCK
    pad = ((0, 0), (0, 0), (0, s_pad - s_), (0, 0))
    q, k, v = jnp.pad(q, pad), jnp.pad(k, pad), jnp.pad(v, pad)
    k_blk = k.reshape(b_, h_, n_blocks, MOBA_BLOCK, hd)
    v_blk = v.reshape(b_, h_, n_blocks, MOBA_BLOCK, hd)
    k_mean = jnp.mean(k_blk.astype(jnp.float32), axis=3)
    n_sel = min(MOBA_TOPK, n_blocks - 1)
    scale = hd ** -0.5
    b_idx = jnp.arange(b_)[:, None, None, None]
    h_idx = jnp.arange(h_)[None, :, None, None]

    def chunk(ci):
        start = ci * Q_CHUNK
        q_c = lax.dynamic_slice_in_dim(q, start, Q_CHUNK, axis=2)
        own = start // MOBA_BLOCK
        q_pos = start + jnp.arange(Q_CHUNK)
        k_own = lax.dynamic_index_in_dim(k_blk, own, axis=2, keepdims=False)
        v_own = lax.dynamic_index_in_dim(v_blk, own, axis=2, keepdims=False)
        k_pos = own * MOBA_BLOCK + jnp.arange(MOBA_BLOCK)
        s_own = jnp.einsum('bhqd,bhkd->bhqk', q_c, k_own).astype(jnp.float32) * scale
        s_own = jnp.where(k_pos[None, :] <= q_pos[:, None], s_own, -jnp.inf)
        if n_sel == 0:
            p = jax.nn.softmax(s_own, axis=-1).astype(v.dtype)
            return jnp.einsum('bhqk,bhkd->bhqd', p, v_own)
        gate = jnp.einsum('bhqd,bhnd->bhqn', q_c.astype(jnp.float32), k_mean)
        gate = jnp.where(jnp.arange(n_blocks) < own, gate, -jnp.inf)
        _, idx = lax.top_k(gate, n_sel)
        valid = idx < own
        k_sel = k_blk[b_idx, h_idx, idx]
        v_sel = v_blk[b_idx, h_idx, idx]
        s_sel = jnp.einsum('bhqd,bhqnkd->bhqnk', q_c, k_sel).astype(jnp.float32) * scale
        s_sel = jnp.where(valid[..., None], s_sel, -jnp.inf)
        s_sel = s_sel.reshape(b_, h_, Q_CHUNK, n_sel * MOBA_BLOCK)
        p = jax.nn.softmax(jnp.concatenate([s_own, s_sel], axis=-1), axis=-1).astype(v.dtype)
        p_own = p[..., :MOBA_BLOCK]
        p_sel = p[..., MOBA_BLOCK:].reshape(b_, h_, Q_CHUNK, n_sel, MOBA_BLOCK)
        return (jnp.einsum('bhqk,bhkd->bhqd', p_own, v_own)
                + jnp.einsum('bhqnk,bhqnkd->bhqd', p_sel, v_sel))

    outs = lax.map(chunk, jnp.arange(s_pad // Q_CHUNK))
    out = jnp.moveaxis(outs, 0, 2).reshape(b_, h_, s_pad, hd)
    return out[:, :, :s_]

def hierarchical_moe(x, w_rg, b_rg, w_re, b_re, w_gate, w_up, w_down):
    b_, s_, d_ = x.shape
    t = x.reshape(-1, d_)
    n_tok = t.shape[0]
    rows = jnp.arange(n_tok)
    g_logits = jnp.dot(t, w_rg).astype(jnp.float32) + b_rg
    g_prob = jax.nn.softmax(g_logits, axis=-1)
    g_idx = jnp.argmax(g_logits, axis=-1)
    g_w = g_prob[rows, g_idx]
    e_logits = (jnp.dot(t, w_re).astype(jnp.float32) + b_re).reshape(n_tok, N_GROUPS, EXPERTS_PER_GROUP)
    e_sel = e_logits[rows, g_idx]
    top_v, top_i = lax.top_k(e_sel, EXPERT_TOPK)
    top_w = jax.nn.softmax(top_v, axis=-1) * g_w[:, None]
    within = jnp.sum(jax.nn.one_hot(top_i, EXPERTS_PER_GROUP, dtype=jnp.float32) * top_w[..., None], axis=1)
    combine = (jax.nn.one_hot(g_idx, N_GROUPS, dtype=jnp.float32)[:, :, None]
               * within[:, None, :]).astype(t.dtype)
    out = jnp.zeros_like(t)
    for g in range(N_GROUPS):
        h = (jax.nn.silu(jnp.einsum('td,edf->tef', t, w_gate[g]))
             * jnp.einsum('td,edf->tef', t, w_up[g]))
        out = out + jnp.einsum('tef,efd->td', h * combine[:, g, :, None], w_down[g])
    return out.reshape(b_, s_, d_)

def second_inputs(seed: int = 0) -> dict:
    key = jax.random.key(seed)
    ks = jax.random.split(key, 24)
    f32 = jnp.float32
    nrm = lambda k, shape, scale: jax.random.normal(k, shape, f32) * scale
    na, nb, L = N_CONV_LAYERS, N_MOBA_LAYERS, DEPTH_2
    G, E, F, D = N_GROUPS, EXPERTS_PER_GROUP, D_EXPERT_2, D_MODEL
    return {
        "x": nrm(ks[0], (BATCH, SEQ, D), 1.0),
        "mem": nrm(ks[1], (BATCH, MEM_LEN, D), 1.0),
        "w_mem_kv": nrm(ks[2], (D, 2 * MEM_WIDTH), D ** -0.5),
        "conv_w_in": nrm(ks[3], (na, D, 2 * MIX_WIDTH + MEM_WIDTH), D ** -0.5),
        "conv_dw_w": nrm(ks[4], (na, CONV_WIDTH, MIX_WIDTH), CONV_WIDTH ** -0.5),
        "conv_dw_b": nrm(ks[5], (na, MIX_WIDTH), 0.02),
        "conv_ln_g": 1.0 + nrm(ks[6], (na, MIX_WIDTH), 0.02),
        "conv_ln_b": nrm(ks[7], (na, MIX_WIDTH), 0.02),
        "moba_w_in": nrm(ks[8], (nb, D, 3 * MIX_WIDTH + MEM_WIDTH), D ** -0.5),
        "w_o": nrm(ks[9], (L, D, D), D ** -0.5 * DEEPNORM_BETA),
        "ln1_g": 1.0 + nrm(ks[10], (L, D), 0.02),
        "ln1_b": nrm(ks[11], (L, D), 0.02),
        "w_rg": nrm(ks[12], (L, D, G), D ** -0.5),
        "b_rg": nrm(ks[13], (L, G), 0.01),
        "w_re": nrm(ks[14], (L, D, G * E), D ** -0.5),
        "b_re": nrm(ks[15], (L, G * E), 0.01),
        "w_gate": nrm(ks[16], (L, G, E, D, F), D ** -0.5),
        "w_up": nrm(ks[17], (L, G, E, D, F), D ** -0.5),
        "w_down": nrm(ks[18], (L, G, E, F, D), F ** -0.5 * DEEPNORM_BETA),
        "ln2_g": 1.0 + nrm(ks[19], (L, D), 0.02),
        "ln2_b": nrm(ks[20], (L, D), 0.02),
    }

def second_block(x, mem, w_mem_kv, conv_w_in, conv_dw_w, conv_dw_b, conv_ln_g, conv_ln_b,
              moba_w_in, w_o, ln1_g, ln1_b, w_rg, b_rg, w_re, b_re, w_gate, w_up, w_down,
              ln2_g, ln2_b):
    b_, s_, _ = x.shape
    mem_kv = jnp.dot(mem, w_mem_kv).reshape(b_, MEM_LEN, 2, MEM_HEADS, HEAD_DIM)
    mem_k, mem_v = mem_kv[:, :, 0], mem_kv[:, :, 1]
    for i in range(DEPTH_2):
        j = i // N_MIXERS
        if i % N_MIXERS == 0:
            u = jnp.dot(x, conv_w_in[j])
            y_mix = conformer_conv(u[..., :2 * MIX_WIDTH], conv_dw_w[j], conv_dw_b[j],
                                   conv_ln_g[j], conv_ln_b[j])
            q_mem = u[..., 2 * MIX_WIDTH:]
        else:
            u = jnp.dot(x, moba_w_in[j])
            qkv = u[..., :3 * MIX_WIDTH].reshape(b_, s_, 3, MOBA_HEADS, HEAD_DIM)
            qkv = jnp.transpose(qkv, (2, 0, 3, 1, 4))
            y_mix = moba_attention(qkv[0], qkv[1], qkv[2])
            y_mix = jnp.transpose(y_mix, (0, 2, 1, 3)).reshape(b_, s_, MIX_WIDTH)
            q_mem = u[..., 3 * MIX_WIDTH:]
        y_mem = memory_attention(q_mem.reshape(b_, s_, MEM_HEADS, HEAD_DIM), mem_k, mem_v)
        y_mem = y_mem.reshape(b_, s_, MEM_WIDTH)
        y = jnp.dot(jnp.concatenate([y_mix, y_mem], axis=-1), w_o[i])
        x = layer_norm(DEEPNORM_ALPHA * x + y, ln1_g[i], ln1_b[i])
        f = hierarchical_moe(x, w_rg[i], b_rg[i], w_re[i], b_re[i], w_gate[i], w_up[i], w_down[i])
        x = layer_norm(DEEPNORM_ALPHA * x + f, ln2_g[i], ln2_b[i])
    return x


def setup_inputs(seed=0):
    out = dict(first_inputs(seed))
    for name, value in second_inputs(seed + 1).items():
        if name != "x":
            out[name + "_2"] = value
    return out


def reference(
    x, norm_mix_g, w_in, b_forget, q_norm_g, k_norm_g, ssm_A_re, ssm_A_im, ssm_log_dt, ssm_B_re,
    ssm_B_im, ssm_C_re, ssm_C_im, ssm_D, w_glu, w_proj_attn, w_proj_ssm, w_out, norm_ffn_g,
    w_router_group, b_router_group, w_router_expert, b_router_expert, w_expert_gate,
    w_expert_up, w_expert_down, mem_2, w_mem_kv_2, conv_w_in_2, conv_dw_w_2, conv_dw_b_2,
    conv_ln_g_2, conv_ln_b_2, moba_w_in_2, w_o_2, ln1_g_2, ln1_b_2, w_rg_2, b_rg_2, w_re_2,
    b_re_2, w_gate_2, w_up_2, w_down_2, ln2_g_2, ln2_b_2,
):
    x = first_block(
        x, norm_mix_g, w_in, b_forget, q_norm_g, k_norm_g, ssm_A_re, ssm_A_im, ssm_log_dt,
        ssm_B_re, ssm_B_im, ssm_C_re, ssm_C_im, ssm_D, w_glu, w_proj_attn, w_proj_ssm, w_out,
        norm_ffn_g, w_router_group, b_router_group, w_router_expert, b_router_expert,
        w_expert_gate, w_expert_up, w_expert_down,
    )
    return second_block(
        x, mem_2, w_mem_kv_2, conv_w_in_2, conv_dw_w_2, conv_dw_b_2, conv_ln_g_2, conv_ln_b_2,
        moba_w_in_2, w_o_2, ln1_g_2, ln1_b_2, w_rg_2, b_rg_2, w_re_2, b_re_2, w_gate_2, w_up_2,
        w_down_2, ln2_g_2, ln2_b_2,
    )


_drawn_inputs = setup_inputs


def setup_inputs(seed=0):
    import zlib

    import numpy as np

    out = dict(_drawn_inputs(seed))
    spreads = {}
    factors = {'norm_mix_g': 3.116,
     'q_norm_g': 8.0,
     'k_norm_g': 5.363,
     'ssm_A_re': 64.0,
     'ssm_B_re': 3.074,
     'ssm_C_re': 2.871,
     'b_router_group': 12.714,
     'b_router_expert': 14.719,
     'conv_dw_b_2': 5.36,
     'conv_ln_g_2': 74.06,
     'conv_ln_b_2': 71.112,
     'b_rg_2': 7.703,
     'b_re_2': 21.683,
     'norm_ffn_g': 3.304}
    for name, (base, spread) in spreads.items():
        noise = np.random.default_rng([zlib.crc32(name.encode()), seed]).standard_normal(out[name].shape)
        drawn = base * np.exp(spread * noise) if base else spread * noise
        out[name] = __import__('jax').numpy.asarray(drawn.astype(out[name].dtype))
    for name, factor in factors.items():
        out[name] = (out[name] * factor).astype(out[name].dtype)
    return out
```

```python
from contextlib import ExitStack

import numpy as np
import concourse.bass as bass
from concourse import mybir

ALU = mybir.AluOpType
ACT = mybir.ActivationFunctionType
AX = mybir.AxisListType
F32 = mybir.dt.float32
I32 = mybir.dt.int32

P = 128
D = 1024
KD = D // P
T = 256
TH = T // P
HD = 64
NE, NG, EPG = 32, 4, 8
NR = NG + NE
CAP = 64
PAIRS = NE // 2
NJ = 16
NQ = 4
HALF_T = 128
LEVELS = 7
TAPS = 31
MIX = 768
MT = MIX // P
PAD = TAPS - 1
SLOT = 4096
NSLOT = 6
ALPHA = (2 * 2) ** 0.25
MASKED = -1e30
TWO_PI_HI = 6.28125
TWO_PI_LO = 2 * np.pi - 6.28125
ROUND = 1.5 * 2 ** 23
SIN_MAX = 3.1415925

VEC = {}
_n = 0
for _name, _w in (("mix_g", KD), ("qg", 1), ("kg", 1), ("a_re", NJ), ("a_im", NJ), ("log_dt", NJ),
                  ("d_skip", NQ), ("dw_b", MT), ("ln_g", MT), ("ln_b", MT), ("dw_w", MT * TAPS),
                  ("c_re", NJ * 16), ("c_im", NJ * 16)):
    VEC[_name] = (_n, _n + _w)
    _n += _w
NVEC = _n

STREAM = (["u", "q", "k", "v", "g0", "g1", "g2", "g3", "glu", "pa", "ps", "wo0", "wo1", "memkv"],
          ["c0", "c1", "c2", "c3", "w2o0", "w2o1"],
          ["m0", "m1", "m2", "m3", "m4", "w3o0", "w3o1"])
CHUNKS = [n for part in STREAM for n in part]


def build(nc, ins, out):
    ctx = ExitStack()
    with ctx:
        _build(ctx, nc, ins, out)


def _build(ctx, nc, ins, out):
    def sb(name, shape, dt=F32):
        return ctx.enter_context(nc.sbuf_tensor(name, shape, dt))

    sems = {}

    def flag(name):
        if name not in sems:
            sems[name] = ctx.enter_context(nc.semaphore(name))
        return sems[name]

    ring = sb("ring", [P, NSLOT, SLOT])
    x_sb = sb("x_sb", [P, TH, D])
    xT = sb("xT", [P, KD, T])
    ident = sb("ident", [P, P])
    ones = sb("ones", [P, P])
    before = sb("before", [P, P])
    upto = sb("upto", [P, TH, T])
    mask = sb("mask", [P, TH, T])
    col_id = sb("col_id", [P, CAP])
    vec = sb("vec", [P, NVEC])
    rows = sb("rows", [P, 2, D])
    head_sel = rows[:, 0, :].rearrange("p (h t) -> p h t", h=8)
    nF = sb("nF", [P, T])
    mem_k = sb("mem_k", [P, 2, T])
    mem_v = sb("mem_v", [P, TH, 256])
    wr = sb("wr", [P, KD, NR])
    brow = sb("brow", [P, 8 + 3 * NR])
    small = sb("small", [P, 256])
    npass = sb("npass", [P, 1], I32)
    arena = sb("arena", [P, 15360])

    def at(off, *dims):
        n = int(np.prod(dims))
        a = arena[:, off:off + n]
        if len(dims) == 1:
            return a
        names = "abcd"[:len(dims)]
        return a.rearrange(f"p ({' '.join(names)}) -> p {' '.join(names)}",
                           **{c: d for c, d in zip(names[:-1], dims[:-1])})

    V = lambda name: vec[:, VEC[name][0]:VEC[name][1]]

    gates = at(0, 16, T)
    h_tok = at(0, TH, D)
    qk_tok = at(4096, TH, 1024)
    zs = at(4096, 2, 4, HALF_T)
    tmp = at(5120, 2, 4, HALF_T)
    mixedT = at(4096, KD, T)
    ws = at(6144, 2, 2, 4, HALF_T)
    y_ssm = at(6144, NQ, T)
    v_tok = at(8192, TH, 512)
    qz1 = at(9216, 8, T)
    kT1 = at(11264, 4, T)
    uT = at(12288, NQ, T)
    yg = at(13312, NQ, T)
    ya = at(14336, 4, T)
    powers = ring[:, 3, :].rearrange("p (c j t) -> p c j t", c=2, j=NJ)
    b_blk = ring[:, 4:6, 0:2048].rearrange("p c (j s) -> p c j s", j=NJ)
    c_blk = ring[:, 4:6, 2048:4096].rearrange("p c (j s) -> p c j s", j=NJ)
    L_buf = rows[:, 1, 0:512].rearrange("p (b t) -> p b t", b=2)
    PT_buf = rows[:, 1, 512:1024].rearrange("p (b t) -> p b t", b=2)
    P_buf = sb("P_buf", [P, 2, T])
    gatez = at(0, 2, T)
    hpad = at(2048, MT, PAD + T)
    conv = at(3840, MT, T)
    sq = at(5376, MT, T)
    stat = at(6912, 4, T)
    qz2 = at(8192, 4, T)
    yT = at(9216, KD, T)
    qz3 = at(0, 12, T)
    kT3 = at(3072, MT, T)
    v3 = at(4608, TH, MIX)
    qz3m = at(6144, 4, T)
    xh = at(0, TH, D)
    S = at(2048, 2, TH, 2 * CAP)
    Sw = at(2560, 2, TH, 2 * CAP)
    SwT = at(3072, T)
    xg = at(3328, 2, KD, 2 * CAP)
    sg = at(5376, 2, 4 * CAP)
    hh = at(5888, 2, 4 * CAP)
    og = at(6400, D)
    rt = at(7424, 4096)
    rank = at(11520, TH, NE + 2)
    wcomb = at(11588, TH, NE + 2)
    sel = at(11656, TH, NE)
    junk = at(12288, D)

    gain = rows[:, 0, :]
    mem_tok = at(2048, TH, D)
    memT = at(13312, KD, T)
    wf = sb("wf", [P, KD, 8])
    lf = sb("lf", [P, 2, TH, 8])
    e_tab = sb("e_tab", [P, LEVELS, 2, NJ])
    ssm_s = sb("ssm_s", [P, 16, NJ])

    def e_pow(k, c):
        return e_tab[:, k, c, :]

    rms_ms = small[:, 0:2]
    rms_r = small[:, 2:4]
    ln_r = small[:, 4:6]
    nmax = lambda n: small[:, 8 + n % 2:9 + n % 2]
    psums = lambda n: small[:, 10 + n % 2:11 + n % 2]
    precip = lambda n: small[:, 12 + n % 2:13 + n % 2]
    Ft = small[:, 16:32].rearrange("p (a h) -> p a h", a=2)
    qk_r = small[:, 32:64]
    f_raw, f_abs, f_e, f_l = (small[:, 64 + 16 * n:80 + 16 * n] for n in range(4))
    bn6 = small[:, 128:152].rearrange("p (a b c) -> p a b c", a=2, b=2)
    bn2 = small[:, 152:156].rearrange("p (a b) -> p a b", a=2)
    s_dt, s_adt, s_mag, s_th = (ssm_s[:, n, :] for n in range(4))
    s_ang = ssm_s[:, 4:6, :].rearrange("p c j -> p (c j)")
    mix_tmp = at(7168, 2, T)
    square_junk = at(2048, D)

    def rt_at(off, *dims):
        return at(7424 + off, *dims)

    r_L, r_gd, r_ge = rt_at(0, TH, NR), rt_at(72, TH, NG), rt_at(80, TH, NG)
    r_geq, r_gc, r_goh, r_pen = (rt_at(88 + 8 * n, TH, NG) for n in range(4))
    r_gmax, r_gfirst, r_gs, r_gw, r_m1, r_m2, r_f1, r_f2, r_d21, r_p2, r_rd, r_w1, r_w2 = (
        rt_at(120 + 2 * n, TH) for n in range(13))
    r_EL, r_eq, r_cand, r_oh1, r_oh2, r_t = (rt_at(160 + 64 * n, TH, NE) for n in range(6))
    r_cmax, r_np = rt_at(600, 1), rt_at(601, 1)

    psum = ctx.enter_context(nc.psum_tensor("psum", [P, 8, 512], F32))

    bank_full = [flag(f"bank_full{b}") for b in range(8)]
    bank_free = [flag(f"bank_free{b}") for b in range(8)]
    plan, uses = {}, [0] * 8

    def use(name, bank):
        plan[name] = (bank, uses[bank])
        uses[bank] += 1

    turn = [0]

    def use2(*name):
        use(name, turn[0] % 2)
        turn[0] += 1

    def plan_attention(name, heads):
        for n in range(2 * heads):
            use((name, "score", n), 2 + n % 2)
            use((name, "pt", n), 4 + n % 2)
        for p in range(heads // 2):
            use((name, "pv", p), 6 + p % 2)

    def plan_turn(name):
        for n in range(4):
            use2(name, n)

    plan_turn("hT")
    for n in range(2):
        use2("u", n)
    for w in "qkv":
        for th in range(TH):
            use2(w, th)
    use2("f")
    for w in ("qT", "kT"):
        for th in range(TH):
            use2(w, th)
    use2("F")
    for q in range(NQ):
        for b in range(2, 6):
            use(("bu", q, b), b)
        use(("y", q), 6 + q % 2)
        use2("gate", 2 * q)
        use2("gate", 2 * q + 1)
    plan_attention("at1", 8)
    use2("glu", 0)
    use2("glu", 1)
    for n in range(4):
        use2("pa", n)
        use2("ps", n)
    for n in range(4):
        use2("res1", n)
    plan_turn("memT")
    use2("memk")
    for th in range(TH):
        use2("memv", th)

    def plan_moe(name):
        plan_turn(name + "xT")
        use2(name + "logits")
        use2(name + "rank")

    plan_moe("e1")
    before_moe = {"e1": list(uses)}
    plan_turn("x2T")
    for n in range(MT):
        use2("conv", n)
    use2("qm2")
    use2("mean")
    use2("var")
    plan_attention("at2", 4)
    for n in range(4):
        use2("res2", n)
    plan_moe("e2")
    before_moe["e2"] = list(uses)
    plan_turn("x3T")
    for n in range(3):
        use2("mq", n)
    for n in range(3):
        use2("mk", n)
    for th in range(TH):
        use2("mv0", th)
    for th in range(TH):
        use2("mv1", th)
    use2("qm3")
    plan_attention("at3", 12)
    plan_attention("at3m", 4)
    for n in range(4):
        use2("res3", n)
    plan_moe("e3")
    before_moe["e3"] = list(uses)

    def open_bank(pe, *name):
        b, m = plan[name]
        if m:
            pe.wait_ge(bank_free[b], m)
        return b

    def close_bank(ins, *name):
        ins.then_inc(bank_full[plan[name][0]], 1)

    def full(eng, *name):
        b, m = plan[name]
        eng.wait_ge(bank_full[b], m + 1)
        return psum[:, b, :]

    def read_out(ins, *name):
        ins.then_inc(bank_free[plan[name][0]], 1)

    def evacuated(eng, *name):
        b, m = plan[name]
        eng.wait_ge(bank_free[b], m + 1)

    last_use = {"u": ("u", 1), "q": ("q", 1), "k": ("k", 1), "v": ("v", 1), "glu": ("glu", 1), "pa": ("pa", 3),
                "ps": ("ps", 3), "wo0": ("res1", 3), "wo1": ("res1", 3), "memkv": ("memv", 1), "c3": ("qm2",),
                "w2o0": ("res2", 3), "w2o1": ("res2", 3), "m0": ("mq", 1), "m1": ("mk", 0), "m2": ("mk", 2),
                "m3": ("mv0", 1), "m4": ("qm3",), "w3o0": ("res3", 3), "w3o1": ("res3", 3)}
    for n in range(4):
        last_use[f"g{n}"] = ("gate", 2 * n + 1)
    for n in range(3):
        last_use[f"c{n}"] = ("conv", 2 * n + 1)
    loaded = [flag(f"loaded{s}") for s in range(2 * NSLOT)]
    used = [flag(f"used{s}") for s in range(2 * NSLOT)]
    loads, moe_uses = [0] * (2 * NSLOT), [0] * (2 * NSLOT)
    holder = [None] * NSLOT
    where, moe_loads, moe_used, moe_after = {}, {}, {}, {}
    for part, (names, width) in enumerate(zip(STREAM, (3, NSLOT, NSLOT))):
        for n, c in enumerate(names):
            s = n % width
            where[c] = (s, loads[2 * s], holder[s] or (moe_uses[2 * s], moe_uses[2 * s + 1]))
            loads[2 * s] += 1
            holder[s] = c
        e = f"e{part + 1}"
        moe_loads[e], moe_used[e], moe_after[e] = list(loads), list(moe_uses), list(holder)
        holder = [None] * NSLOT
        for s in range(2 * NSLOT):
            n = 8 if part == 0 else 16 * (s % 2 == 0)
            loads[s] += n
            moe_uses[s] += n

    def load_chunk(sp, c):
        s, _, prior = where[c]
        if isinstance(prior, str):
            full(sp, *last_use[prior])
        else:
            for half in range(2):
                if prior[half]:
                    sp.wait_ge(used[2 * s + half], prior[half])
        sp.dma_start(ring[:, s, :], ins["stream"][CHUNKS.index(c)]).then_inc(loaded[2 * s], 16)

    def chunk(pe, c, inner):
        s, before_, _ = where[c]
        pe.wait_ge(loaded[2 * s], 16 * (before_ + 1))
        return ring[:, s, :].rearrange("p (k n) -> p k n", n=inner)

    def moe_slots(e, u):
        if e == "e1":
            return [(6 * u + w, 1, 0) for w in range(6)]
        return [(2 * w, 2, u) for w in range(6)]

    def moe_view(e, hs):
        return ring[:, hs // 2, (hs % 2) * 2048:(hs % 2) * 2048 + (2 if e == "e1" else 4) * 1024]

    def moe_steps(e):
        return [e + n for n in ("_zero", "_gd", "_sel", "_d21", "_npass")]

    milestones = {
        "vec": ["ssm_adt", "ssm_angle", "ssm_powers2", "x_ms", "h_tok", "qk_ms", "f_abs", "qk_tok", "logf"]
        + [f"ssm_state{n}" for n in range(2 * NQ)] + ["y_ssm", "x1", "x1_ms", "e1_tok"] + moe_steps("e1")
        + ["x2"] + [f"glu_in{n}" for n in range(MT)] + ["conv_done", "conv_sq", "conv_var", "ln21_var", "e2_tok"]
        + moe_steps("e2") + ["ln22_var", "x3", "ln31_var", "e3_tok"] + moe_steps("e3") + ["ln32_var", "x_final"],
        "act": ["ssm_dt", "ssm_mag", "ssm_sin", "x_sq", "x_rms", "qk_rms", "f_ln", "x1_sq", "x1_rms", "e1_ge", "e1_p2"]
        + [f"conv_gate{n}" for n in range(MT)] + ["conv_std", "ln21_std", "e2_ge", "e2_p2", "ln22_std", "ln31_std",
                                                  "e3_ge", "e3_p2", "ln32_std"],
        "pool": ["ident", "masks", "powers"]}
    finished = {who: flag(who + "_finished") for who in milestones}
    said = {who: 0 for who in milestones}

    def finish(eng, who, name):
        assert milestones[who][said[who]] == name, (name, milestones[who][said[who]])
        said[who] += 1
        eng.sem_inc(finished[who], 1)

    def after(eng, who, name):
        eng.wait_ge(finished[who], milestones[who].index(name) + 1)

    per_layer = {"S": 2 * (PAIRS + 1), "gathA": PAIRS + 1, "gathB": PAIRS + 1, "xgA": PAIRS + 1, "xgB": PAIRS + 1,
                 "silu": NE, "h": NE, "T": PAIRS, "SwT": PAIRS, "down": PAIRS, "outA": PAIRS, "outB": PAIRS,
                 "scattered": PAIRS}

    def moe_wait(eng, e, name, value):
        eng.wait_ge(flag("moe_" + name), value + (int(e[1]) - 1) * per_layer[name])

    heads_before = {"at1": 0, "at2": 8, "at3": 12, "at3m": 24}

    def attn_wait(eng, name, what, value):
        eng.wait_ge(flag("attn_" + what), value + 2 * heads_before[name])

    block = ctx.enter_context(nc.Block())
    small_sem = flag("constants_loaded")
    NSMALL = 3

    @block.sync
    def _(sp):
        sp.dma_start(x_sb[:, :, :], ins["x"].rearrange("(h p) d -> p h d", p=P)).then_inc(flag("x_loaded"), 16)
        for c in STREAM[0]:
            load_chunk(sp, c)
        for part, e in enumerate(("e1", "e2", "e3")):
            if part == 0:
                full(sp, "y", NQ - 1)
            for c in moe_after[e]:
                if c:
                    full(sp, *last_use[c])
            if part == 1:
                for s in range(NSLOT):
                    sp.wait_ge(used[2 * s + 1], moe_used[e][2 * s + 1])
            base = moe_used[e]
            with sp.Fori(0, 8) as i:
                for u in range(2):
                    for w, (hs, per, at_u) in enumerate(moe_slots(e, u)):
                        sp.wait_ge(used[hs], i * per + (base[hs] + at_u))
                        expert = i * 4 + (2 * u + (w // 2 if w < 4 else w - 4))
                        src = ins[e + ("_gate", "_up", "_gate", "_up", "_down", "_down")[w]]
                        sp.dma_start(moe_view(e, hs), src[expert, :, :]).then_inc(loaded[hs], 16)
            after(sp, "vec", e + "_npass")
            n = sp.value_load(npass[0:1, 0:1], min_val=1, max_val=T // CAP)
            with sp.If(n > 1):
                moe_wait(sp, e, "scattered", PAIRS)
                with sp.Fori(1, n) as p:
                    with sp.Fori(0, NE) as x:
                        for w, src in enumerate(("_gate", "_up", "_down")):
                            sp.wait_ge(flag(e + "_ovf_pe"), (p - 1) * (4 * NE) + x * 4)
                            sp.dma_start(moe_view(e, 2 * w), ins[e + src][x, :, :]).then_inc(flag(e + "_ovf_loaded"), 16)
                sp.wait_ge(flag("moe_sum_ready"), int(e[1]))
            if part < 2:
                for c in STREAM[part + 1]:
                    load_chunk(sp, c)
        after(sp, "vec", "x_final")
        sp.dma_start(out.rearrange("(h p) d -> p h d", p=P), x_sb[:, :, :]).then_inc(flag("stored"), 16)
        sp.wait_ge(flag("stored"), 16)

    @block.gpsimd
    def _(po):
        made = flag("pool_made")
        n = [0]

        def step(ins_):
            n[0] += 1
            ins_.then_inc(made, 1)
            po.wait_ge(made, n[0])

        step(po.memset(ident[:, :], 0.0))
        step(po.affine_select(out=ident[:, :], in_=ident[:, :], compare_op=ALU.not_equal, fill=1.0, base=0,
                              pattern=[[-1, P]], channel_multiplier=1))
        finish(po, "pool", "ident")
        step(po.memset(ones[:, :], 1.0))
        step(po.memset(before[:, :], 1.0))
        step(po.affine_select(out=before[:, :], in_=before[:, :], compare_op=ALU.is_gt, fill=0.0, base=0,
                              pattern=[[1, P]], channel_multiplier=-1))
        step(po.memset(upto[:, :, :], 1.0))
        step(po.memset(mask[:, :, :], 0.0))
        for h in range(TH):
            step(po.affine_select(out=upto[:, h, :], in_=upto[:, h, :], compare_op=ALU.is_ge, fill=0.0,
                                  base=-P * h, pattern=[[1, T]], channel_multiplier=-1))
            step(po.affine_select(out=mask[:, h, :], in_=mask[:, h, :], compare_op=ALU.is_ge, fill=MASKED,
                                  base=P * h, pattern=[[-1, T]], channel_multiplier=1))
        step(po.iota(col_id[:, :], pattern=[[1, CAP]], base=0, channel_multiplier=0,
                     allow_small_or_imprecise_dtypes=True))
        step(po.memset(rows[:, 0, :], 1.0))
        step(po.affine_select(out=head_sel, in_=head_sel, compare_op=ALU.is_equal, fill=0.0, base=0,
                              pattern=[[-1, 8], [0, P]], channel_multiplier=1))
        step(po.memset(nF[:, :], 0.0))
        finish(po, "pool", "masks")
        after(po, "vec", "ssm_powers2")
        pw = powers
        step(po.memset(pw[:, 0, :, 0:1], 1.0))
        step(po.memset(pw[:, 1, :, 0:1], 0.0))
        pt1 = ring[:, 4:6, 2048:4096]
        for k in range(LEVELS):
            Lk = 1 << k
            er = e_pow(k, 0).unsqueeze(2).broadcast_to([P, NJ, Lk])
            ei = e_pow(k, 1).unsqueeze(2).broadcast_to([P, NJ, Lk])
            t1 = pt1[:, 0, 0:NJ * Lk].rearrange("p (j t) -> p j t", j=NJ)
            t2 = pt1[:, 1, 0:NJ * Lk].rearrange("p (j t) -> p j t", j=NJ)
            pr, pi = pw[:, 0, :, 0:Lk], pw[:, 1, :, 0:Lk]
            step(po.tensor_tensor(t1, pr, er, ALU.mult))
            step(po.tensor_tensor(t2, pi, ei, ALU.mult))
            step(po.tensor_tensor(pw[:, 0, :, Lk:2 * Lk], t1, t2, ALU.subtract))
            step(po.tensor_tensor(t1, pr, ei, ALU.mult))
            step(po.tensor_tensor(t2, pi, er, ALU.mult))
            step(po.tensor_tensor(pw[:, 1, :, Lk:2 * Lk], t1, t2, ALU.add))
        finish(po, "pool", "powers")

    @block.tensor
    def _(pe):
        mm = pe.matmul

        def turn_to_T(name, src):
            for n in range(4):
                th, kk = n // 2, n % 2
                b = open_bank(pe, name, n)
                for k in range(4):
                    last = pe.transpose(psum[:, b, k * P:(k + 1) * P], src[:, th, (4 * kk + k) * P:(4 * kk + k + 1) * P], ident[:, :])
                close_bank(last, name, n)

        def wait_T(name):
            for n in range(4):
                evacuated(pe, name, n)

        def to_T(w, cols, name, rhs, done=None, first=0, K=KD):
            b = open_bank(pe, *name)
            for n, c in enumerate(cols):
                for k in range(K):
                    last = mm(psum[:, b, n * T:(n + 1) * T], w[:, k, c * P:(c + 1) * P], rhs[:, k, :],
                              start=(k == 0), stop=(k == K - 1))
            close_bank(last, *name)

        def to_tok(w, c0, c1, name, th, lhs, k0=0, K=KD, start=True, stop=True, close=True):
            b = open_bank(pe, *name) if start else plan[name][0]
            for k in range(K):
                last = mm(psum[:, b, 0:c1 - c0], lhs[:, k0 + k, th * P:(th + 1) * P], w[:, k, c0:c1],
                          start=(start and k == 0), stop=(stop and k == K - 1))
            if close:
                close_bank(last, *name)
            return last

        def attention(name, heads, qz, kT, v, causal, forget=False):
            N = 2 * heads

            def unit(n):
                p, th, j = n // 4, n // 2 % 2, n % 2
                return 2 * p + j, th, (P if causal and th == 0 else T)

            for n in range(N + 2):
                if n < N:
                    h, th, W = unit(n)
                    b = open_bank(pe, name, "score", n)
                    last = mm(psum[:, b, 0:W], qz[:, h, th * P:(th + 1) * P], kT(h)[:, 0:W], start=True, stop=not forget)
                    if forget:
                        last = mm(psum[:, b, 0:W], head_sel[:, h, :], nF[:, 0:W], start=False, stop=True)
                    close_bank(last, name, "score", n)
                if 1 <= n <= N:
                    m = n - 1
                    h, th, W = unit(m)
                    b = open_bank(pe, name, "pt", m)
                    attn_wait(pe, name, "probs", m + 1)
                    for s in range(W // P):
                        last = pe.transpose(psum[:, b, s * P:(s + 1) * P], P_buf[:, m % 2, s * P:(s + 1) * P], ident[:, :])
                    close_bank(last, name, "pt", m)
                if n >= 2:
                    m = n - 2
                    h, th, W = unit(m)
                    p = m // 4
                    evacuated(pe, name, "pt", m)
                    b = open_bank(pe, name, "pv", p) if m % 4 == 0 else plan[(name, "pv", p)][0]
                    for s in range(W // P):
                        last = mm(psum[(h % 2) * HD:(h % 2 + 1) * HD, b, th * P:(th + 1) * P], v(s, h),
                                  PT_buf[:, m % 2, s * P:(s + 1) * P], start=(s == 0), stop=(s == W // P - 1))
                    if m % 4 == 3:
                        close_bank(last, name, "pv", p)

        def residual(name, chunks, lhs):
            w = [chunk(pe, c, D) for c in chunks]
            for n in range(4):
                th, hf = n // 2, n % 2
                to_tok(w[0], hf * 512, hf * 512 + 512, (name, n), th, lhs, 0, 4, True, False, False)
                to_tok(w[1], hf * 512, hf * 512 + 512, (name, n), th, lhs, 4, 4, False, True, True)

        def moe(e, tok):
            F = 2 if e == "e1" else 4
            lbase = moe_loads[e]
            turn_to_T(e + "xT", tok)
            wait_T(e + "xT")
            pe.wait_ge(flag("router_w"), 16 * int(e[1]))
            b = open_bank(pe, e + "logits")
            for th in range(TH):
                for k in range(KD):
                    last = mm(psum[:, b, th * NR:(th + 1) * NR], xT[:, k, th * P:(th + 1) * P], wr[:, k, :],
                              start=(k == 0), stop=(k == KD - 1))
            close_bank(last, e + "logits")
            b = open_bank(pe, e + "rank")
            after(pe, "vec", e + "_sel")
            mm(psum[:, b, 0:NE], before[:, :], sel[:, 0, :], start=True, stop=True)
            mm(psum[:, b, NE:2 * NE], ones[:, :], sel[:, 0, :], start=True, stop=False)
            mm(psum[:, b, NE:2 * NE], before[:, :], sel[:, 1, :], start=False, stop=True)
            mm(psum[:, b, 2 * NE:3 * NE], ones[:, :], sel[:, 0, :], start=True, stop=False)
            last = mm(psum[:, b, 2 * NE:3 * NE], ones[:, :], sel[:, 1, :], start=False, stop=True)
            close_bank(last, e + "rank")
            for b in range(8):
                pe.wait_ge(bank_free[b], before_moe[e][b])
            after(pe, "vec", e + "_zero")
            for b in range(4):
                mm(psum[:, b, :], ones[:, :], og[:, 0:512], start=True, stop=False, skip_group_check=True)

            def gather(par):
                for half, (b, sem) in enumerate(((4, "gathA"), (7, "gathB"))):
                    for k in range(4):
                        for th in range(TH):
                            last = mm(psum[:, b, k * 2 * CAP:(k + 1) * 2 * CAP], tok[:, th, (4 * half + k) * P:(4 * half + k + 1) * P],
                                      S[:, par, th, :], start=(th == 0), stop=(th == TH - 1))
                    last.then_inc(flag("moe_" + sem), 1)
                    if half == 0:
                        yield

            moe_wait(pe, e, "S", 2)
            for _ in gather(0):
                pass

            with pe.Fori(0, 8) as i:
                for u in range(2):
                    def c(k, per=1):
                        return i * (2 * per) + (u * per + k)

                    slots = moe_slots(e, u)
                    views = [moe_view(e, s[0]) for s in slots]

                    def arrived(w):
                        hs, per, at_u = slots[w]
                        pe.wait_ge(loaded[hs], i * (16 * per) + 16 * (lbase[hs] + at_u + 1))

                    moe_wait(pe, e, "xgA", c(1))
                    moe_wait(pe, e, "xgB", c(1))
                    for x in range(2):
                        b = 5 + x
                        if x == 0:
                            moe_wait(pe, e, "SwT", c(0))
                        else:
                            moe_wait(pe, e, "outA", c(0))
                        for g in range(2):
                            w = 2 * x + g
                            arrived(w)
                            wv = views[w].rearrange("p (k n) -> p k n", k=KD)
                            for f in range(F):
                                for k in range(KD):
                                    last = mm(psum[:, b, (g * F + f) * CAP:(g * F + f + 1) * CAP], wv[:, k, f * P:(f + 1) * P],
                                              xg[:, u, k, x * CAP:(x + 1) * CAP], start=(k == 0), stop=(k == KD - 1))
                            last.then_inc(used[slots[w][0]], 1)
                    moe_wait(pe, e, "h", c(1, 2))
                    for th in range(TH):
                        last = pe.transpose(psum[:, 5, th * P:(th + 1) * P], Sw[:, u, th, :], ident[:, :])
                    last.then_inc(flag("moe_T"), 1)
                    moe_wait(pe, e, "S", c(4, 2))
                    g = gather(1 - u)
                    next(g)
                    moe_wait(pe, e, "outB", c(0))
                    for _ in g:
                        pass
                    moe_wait(pe, e, "h", c(2, 2))
                    arrived(4)
                    arrived(5)
                    for half in range(2):
                        b = 6 + half
                        if half:
                            moe_wait(pe, e, "xgB", c(2))
                        for x in range(2):
                            wv = views[4 + x].rearrange("p (k n) -> p k n", n=D)
                            for f in range(F):
                                last = mm(psum[x * CAP:(x + 1) * CAP, b, :], hh[:, x, f * CAP:(f + 1) * CAP],
                                          wv[:, f, half * 512:(half + 1) * 512], start=(f == 0), stop=(f == F - 1))
                            if half:
                                last.then_inc(used[slots[4 + x][0]], 1)
                        if half == 0:
                            last.then_inc(flag("moe_down"), 1)
                    moe_wait(pe, e, "SwT", c(1))
                    moe_wait(pe, e, "outA", c(1))
                    for half in range(2):
                        if half:
                            moe_wait(pe, e, "outB", c(1))
                        for th in range(TH):
                            last = mm(psum[:, 2 * th + half, :], SwT[:, th * P:(th + 1) * P], og[:, half * 512:(half + 1) * 512],
                                      start=False, stop=False, skip_group_check=True)
                    last.then_inc(flag("moe_scattered"), 1)
            moe_wait(pe, e, "xgA", PAIRS + 1)
            moe_wait(pe, e, "xgB", PAIRS + 1)

            n = pe.value_load(npass[0:1, 0:1], min_val=1, max_val=T // CAP)
            with pe.If(n > 1):
                with pe.Fori(1, n) as p:
                    with pe.Fori(0, NE) as x:
                        j = (p - 1) * NE + x
                        pe.wait_ge(flag(e + "_ovf_vec"), j * 8 + p + 2)
                        for half, b in enumerate((4, 7)):
                            for k in range(4):
                                for th in range(TH):
                                    last = mm(psum[:, b, k * CAP:(k + 1) * CAP], tok[:, th, (4 * half + k) * P:(4 * half + k + 1) * P],
                                              S[:, 0, th, 0:CAP], start=(th == 0), stop=(th == TH - 1))
                        for th in range(TH):
                            last = pe.transpose(psum[0:CAP, 6, th * P:(th + 1) * P], Sw[:, 0, th, 0:CAP], ident[:, :])
                        last.then_inc(flag(e + "_ovf_pe"), 1)
                        pe.wait_ge(flag(e + "_ovf_vec"), j * 8 + p + 5)
                        pe.wait_ge(flag(e + "_ovf_loaded"), j * 48 + 48)
                        for g in range(2):
                            wv = moe_view(e, 2 * g).rearrange("p (k n) -> p k n", k=KD)
                            for f in range(F):
                                for k in range(KD):
                                    last = mm(psum[:, 5, (g * F + f) * CAP:(g * F + f + 1) * CAP], wv[:, k, f * P:(f + 1) * P],
                                              xg[:, 0, k, 0:CAP], start=(k == 0), stop=(k == KD - 1))
                        last.then_inc(flag(e + "_ovf_pe"), 1)
                        pe.wait_ge(flag(e + "_ovf_vec"), j * 8 + p + 6)
                        wv = moe_view(e, 4).rearrange("p (k n) -> p k n", n=D)
                        for half in range(2):
                            for f in range(F):
                                last = mm(psum[0:CAP, 6 + half, :], hh[:, 0, f * CAP:(f + 1) * CAP],
                                          wv[:, f, half * 512:(half + 1) * 512], start=(f == 0), stop=(f == F - 1))
                        last.then_inc(flag(e + "_ovf_pe"), 1)
                        pe.wait_ge(flag(e + "_ovf_vec"), j * 8 + p + 8)
                        for half in range(2):
                            for th in range(TH):
                                last = mm(psum[:, 2 * th + half, :], SwT[0:CAP, th * P:(th + 1) * P], og[0:CAP, half * 512:(half + 1) * 512],
                                          start=False, stop=False, skip_group_check=True)
                        last.then_inc(flag(e + "_ovf_pe"), 1)
                        pe.wait_ge(flag(e + "_ovf_pe"), j * 4 + 4)
            moe_wait(pe, e, "scattered", PAIRS)
            pe.sem_inc(flag("moe_sum_ready"), 1)

        after(pe, "pool", "ident")
        after(pe, "vec", "h_tok")
        turn_to_T("hT", h_tok)
        wait_T("hT")
        w = chunk(pe, "u", 512)
        to_T(w, (0, 1), ("u", 0), xT)
        to_T(w, (2, 3), ("u", 1), xT)
        for name in "qkv":
            w = chunk(pe, name, 512)
            for th in range(TH):
                to_tok(w, 0, 512, (name, th), th, xT)
        pe.wait_ge(small_sem, 16 * NSMALL)
        b = open_bank(pe, "f")
        for th in range(TH):
            for k in range(KD):
                last = mm(psum[:, b, th * 8:(th + 1) * 8], xT[:, k, th * P:(th + 1) * P], wf[:, k, :],
                          start=(k == 0), stop=(k == KD - 1))
        close_bank(last, "f")
        for w_, c0 in (("qT", 0), ("kT", 512)):
            after(pe, "vec", "qk_tok")
            for th in range(TH):
                b = open_bank(pe, w_, th)
                for k in range(4):
                    last = pe.transpose(psum[:, b, k * P:(k + 1) * P], qk_tok[:, th, c0 + k * P:c0 + (k + 1) * P], ident[:, :])
                close_bank(last, w_, th)
        after(pe, "pool", "masks")
        after(pe, "vec", "logf")
        b = open_bank(pe, "F")
        mm(psum[:, b, 0:8], upto[:, 0, 0:P], lf[:, 0, 0, :], start=True, stop=True)
        mm(psum[:, b, 8:16], upto[:, 0, P:T], lf[:, 0, 0, :], start=True, stop=False)
        mm(psum[:, b, 8:16], upto[:, 1, P:T], lf[:, 0, 1, :], start=False, stop=True)
        mm(psum[0:8, b, 128:128 + T], lf[:, 1, 0, :], upto[:, 0, :], start=True, stop=False)
        last = mm(psum[0:8, b, 128:128 + T], lf[:, 1, 1, :], upto[:, 1, :], start=False, stop=True)
        close_bank(last, "F")
        pe.wait_ge(flag("b_loaded"), 32)
        for q in range(NQ):
            for c_ in range(2):
                for hb in range(2):
                    bank = 2 + 2 * c_ + hb
                    open_bank(pe, "bu", q, bank)
                    for jj in (2 * hb, 2 * hb + 1):
                        last = mm(psum[:, bank, (jj % 2) * T:(jj % 2 + 1) * T], b_blk[:, c_, 4 * q + jj, :], uT[:, q, :],
                                  start=True, stop=True)
                    close_bank(last, "bu", q, bank)
            w = chunk(pe, f"g{q}", 512)
            to_T(w, (0, 1), ("gate", 2 * q), xT)
            to_T(w, (2, 3), ("gate", 2 * q + 1), xT)
            b = open_bank(pe, "y", q)
            for half in range(2):
                after(pe, "vec", f"ssm_state{2 * q + half}")
                for jj in range(4):
                    for c_ in range(2):
                        last = mm(psum[:, b, half * HALF_T:(half + 1) * HALF_T], c_blk[:, c_, 4 * q + jj, :], ws[:, half, c_, jj, :],
                                  start=(jj == 0 and c_ == 0), stop=(jj == 3 and c_ == 1))
                last.then_inc(flag("ssm_y"), 1)
            pe.wait_ge(flag("ssm_y"), 2 * q + 2)
            pe.sem_inc(bank_full[b], 1)
        for name in ("qT", "kT"):
            for th in range(TH):
                evacuated(pe, name, th)
        evacuated(pe, "F")
        evacuated(pe, "v", 0)
        evacuated(pe, "v", 1)
        attention("at1", 8, qz1, lambda h: kT1[:, h // 2, :], lambda s, h: v_tok[:, s, h * HD:(h + 1) * HD], True, True)
        w = chunk(pe, "glu", 512)
        pe.wait_ge(flag("gelu"), NQ)
        to_T(w, (0, 1), ("glu", 0), yg, K=4)
        to_T(w, (2, 3), ("glu", 1), yg, K=4)
        for p in range(4):
            evacuated(pe, "at1", "pv", p)
        wa, ws_ = chunk(pe, "pa", D), chunk(pe, "ps", D)
        for n in range(4):
            to_T(wa, (2 * n, 2 * n + 1), ("pa", n), ya, K=4)
            if n == 0:
                after(pe, "vec", "y_ssm")
            to_T(ws_, (2 * n, 2 * n + 1), ("ps", n), y_ssm, K=4)
        pe.wait_ge(flag("mixed"), 4)
        residual("res1", ("wo0", "wo1"), mixedT)
        pe.wait_ge(flag("mem_loaded"), 16)
        turn_to_T("memT", mem_tok)
        wait_T("memT")
        w = chunk(pe, "memkv", 512)
        to_T(w, (0, 1), ("memk",), memT)
        for th in range(TH):
            to_tok(w, 256, 512, ("memv", th), th, memT)
        after(pe, "vec", "e1_tok")
        moe("e1", xh)

        after(pe, "vec", "x2")
        turn_to_T("x2T", x_sb)
        wait_T("x2T")
        for n in range(MT):
            if n % 2 == 0:
                w = chunk(pe, f"c{n // 2}", 512)
            to_T(w, (2 * (n % 2), 2 * (n % 2) + 1), ("conv", n), xT)
        w = chunk(pe, "c3", 512)
        to_T(w, (0, 1), ("qm2",), xT)
        evacuated(pe, "qm2")
        evacuated(pe, "memk")
        evacuated(pe, "memv", 0)
        evacuated(pe, "memv", 1)

        def channel_sums(name, src):
            b = open_bank(pe, name)
            for k in range(MT):
                last = mm(psum[:, b, 0:T], ones[:, :], src[:, k, :], start=(k == 0), stop=(k == MT - 1))
            close_bank(last, name)

        after(pe, "vec", "conv_done")
        channel_sums("mean", conv)
        after(pe, "vec", "conv_sq")
        channel_sums("var", sq)
        attention("at2", 4, qz2, lambda h: mem_k[:, h // 2, :], lambda s, h: mem_v[:, s, h * HD:(h + 1) * HD], False)
        for p in range(2):
            evacuated(pe, "at2", "pv", p)
        pe.wait_ge(flag("conv_out"), MT)
        residual("res2", ("w2o0", "w2o1"), yT)
        after(pe, "vec", "e2_tok")
        moe("e2", x_sb)

        after(pe, "vec", "x3")
        turn_to_T("x3T", x_sb)
        wait_T("x3T")
        w = chunk(pe, "m0", 512)
        to_T(w, (0, 1), ("mq", 0), xT)
        to_T(w, (2, 3), ("mq", 1), xT)
        w = chunk(pe, "m1", 512)
        to_T(w, (0, 1), ("mq", 2), xT)
        to_T(w, (2, 3), ("mk", 0), xT)
        w = chunk(pe, "m2", 512)
        to_T(w, (0, 1), ("mk", 1), xT)
        to_T(w, (2, 3), ("mk", 2), xT)
        w = chunk(pe, "m3", 512)
        for th in range(TH):
            to_tok(w, 0, 512, ("mv0", th), th, xT)
        w = chunk(pe, "m4", 512)
        for th in range(TH):
            to_tok(w, 0, 256, ("mv1", th), th, xT)
        to_T(w, (2, 3), ("qm3",), xT)
        for n in range(3):
            evacuated(pe, "mq", n)
            evacuated(pe, "mk", n)
        for th in range(TH):
            evacuated(pe, "mv0", th)
            evacuated(pe, "mv1", th)
        evacuated(pe, "qm3")
        attention("at3", 12, qz3, lambda h: kT3[:, h // 2, :], lambda s, h: v3[:, s, h * HD:(h + 1) * HD], True)
        attention("at3m", 4, qz3m, lambda h: mem_k[:, h // 2, :], lambda s, h: mem_v[:, s, h * HD:(h + 1) * HD], False)
        for p in range(6):
            evacuated(pe, "at3", "pv", p)
        for p in range(2):
            evacuated(pe, "at3m", "pv", p)
        residual("res3", ("w3o0", "w3o1"), yT)
        after(pe, "vec", "e3_tok")
        moe("e3", x_sb)

    @block.scalar
    def _(ac):
        act = ac.activation
        chain = flag("act_chain")
        n_chain = [0]

        def step(ins_):
            n_chain[0] += 1
            ins_.then_inc(chain, 1)
            ac.wait_ge(chain, n_chain[0])

        def copy_out(name, dst, src):
            read_out(act(dst, src, ACT.Copy), *name)

        def attention(name, heads, out_T):
            N = 2 * heads

            def width(n):
                return P if name in ("at1", "at3") and n // 2 % 2 == 0 else T

            for n in range(N + 2):
                if n < N:
                    W = width(n)
                    attn_wait(ac, name, "logits", n + 1)
                    if n >= 2:
                        full(ac, name, "pt", n - 2)
                    act(P_buf[:, n % 2, 0:W], L_buf[:, n % 2, 0:W], ACT.Exp, bias=nmax(n), accum_out=psums(n)).then_inc(flag("attn_exp"), 1)
                if 1 <= n <= N:
                    m = n - 1
                    W = width(m)
                    src = full(ac, name, "pt", m)
                    copy_out((name, "pt", m), PT_buf[:, m % 2, 0:W], src[:, 0:W])
                m = n - 2
                if n >= 2 and m % 4 == 3:
                    p = m // 4
                    src = full(ac, name, "pv", p)
                    copy_out((name, "pv", p), out_T[:, p, :], src[:, 0:T])

        def moe(e):
            F = 2 if e == "e1" else 4
            W = F * CAP

            def gathered(par):
                act(xg[:, par, 0:4, :], psum[:, 4, :].rearrange("p (k c) -> p k c", k=4), ACT.Copy).then_inc(flag("moe_xgA"), 1)

            after(ac, "vec", e + "_gd")
            step(act(r_ge, r_gd, ACT.Exp))
            finish(ac, "act", e + "_ge")
            after(ac, "vec", e + "_d21")
            step(act(r_p2, r_d21, ACT.Exp))
            finish(ac, "act", e + "_p2")
            if e != "e3":
                ac.dma_start(wr[:, :, :], ins["wr"][int(e[1])]).then_inc(flag("router_w"), 16)

            moe_wait(ac, e, "gathA", 1)
            gathered(0)
            with ac.Fori(0, 8) as i:
                for u in range(2):
                    def c(k, per=1):
                        return i * (2 * per) + (u * per + k)

                    for x in range(2):
                        hs, per, at_u = moe_slots(e, u)[2 * x + 1]
                        ac.wait_ge(used[hs], i * per + (moe_used[e][hs] + at_u + 1))
                        act(sg[:, x, 0:W], psum[:, 5 + x, 0:W], ACT.Silu).then_inc(flag("moe_silu"), 1)
                    moe_wait(ac, e, "T", c(1))
                    act(SwT[:, :], psum[:, 5, 0:T], ACT.Copy).then_inc(flag("moe_SwT"), 1)
                    moe_wait(ac, e, "gathA", c(2))
                    gathered(1 - u)
                    moe_wait(ac, e, "down", c(1))
                    act(og[:, 0:512], psum[:, 6, :], ACT.Copy).then_inc(flag("moe_outA"), 1)
            after(ac, "vec", e + "_npass")
            n = ac.value_load(npass[0:1, 0:1], min_val=1, max_val=T // CAP)
            with ac.If(n > 1):
                with ac.Fori(1, n) as p:
                    with ac.Fori(0, NE) as x:
                        j = (p - 1) * NE + x
                        ac.wait_ge(flag(e + "_ovf_pe"), j * 4 + 2)
                        act(sg[:, 0, 0:W], psum[:, 5, 0:W], ACT.Silu).then_inc(flag(e + "_ovf_silu"), 1)

        ac.dma_start(vec[:, :], ins["vec"]).then_inc(small_sem, 16)
        ac.dma_start(wf[:, :, :], ins["wf"]).then_inc(small_sem, 16)
        ac.dma_start(brow[:, :], ins["brow"].partition_broadcast(P)).then_inc(small_sem, 16)
        ac.dma_start(wr[:, :, :], ins["wr"][0]).then_inc(flag("router_w"), 16)
        for c_ in range(2):
            ac.dma_start(b_blk[:, c_, :, :], ins["b_blk"][c_]).then_inc(flag("b_loaded"), 16)
        ac.wait_ge(small_sem, 16 * NSMALL)
        step(act(s_dt, V("log_dt"), ACT.Exp))
        finish(ac, "act", "ssm_dt")
        after(ac, "vec", "ssm_adt")
        step(act(s_mag, s_adt, ACT.Exp))
        finish(ac, "act", "ssm_mag")
        after(ac, "vec", "ssm_angle")
        step(act(e_tab[:, 0, :, :].rearrange("p c j -> p (c j)"), s_ang, ACT.Sin))
        finish(ac, "act", "ssm_sin")

        def rms_norm(squares, got, ready):
            for th in range(TH):
                step(act(squares, x_sb[:, th, :], ACT.Square, accum_out=rms_ms[:, th:th + 1]))
            finish(ac, "act", got + "_sq")
            after(ac, "vec", got + "_ms")
            step(act(rms_r, rms_r, ACT.Sqrt))
            finish(ac, "act", got + "_rms")

        ac.wait_ge(flag("x_loaded"), 16)
        rms_norm(square_junk, "x", None)
        for n in range(2):
            src = full(ac, "u", n)
            copy_out(("u", n), uT[:, 2 * n:2 * n + 2, :], src.rearrange("p (a t) -> p a t", a=2))
        for th in range(TH):
            src = full(ac, "v", th)
            copy_out(("v", th), v_tok[:, th, :], src)
        after(ac, "vec", "qk_ms")
        step(act(qk_r, qk_r, ACT.Sqrt))
        finish(ac, "act", "qk_rms")
        after(ac, "vec", "f_abs")
        step(act(f_e, f_abs, ACT.Exp, scale=-1.0))
        step(act(f_l, f_e, ACT.Ln, bias=1.0))
        finish(ac, "act", "f_ln")
        for n in range(2 * NQ):
            src = full(ac, "gate", n)
            read_out(act(gates[:, 2 * n:2 * n + 2, :], src.rearrange("p (a t) -> p a t", a=2), ACT.Sigmoid), "gate", n)
        for q in range(NQ):
            evacuated(ac, "y", q)
            act(yg[:, q, :], yg[:, q, :], ACT.Gelu_apprx_tanh).then_inc(flag("gelu"), 1)
        attention("at1", 8, ya)
        ac.dma_start(gain, ins["rows"][0:1, :].partition_broadcast(P)).then_inc(flag("gain_loaded"), 16)
        for n in range(2):
            src = full(ac, "glu", n)
            read_out(act(y_ssm[:, 2 * n:2 * n + 2, :], src.rearrange("p (a t) -> p a t", a=2), ACT.Sigmoid), "glu", n)
        ac.wait_ge(flag("mixed"), 4)
        ac.dma_start(mem_tok, ins["mem"].rearrange("(h p) d -> p h d", p=P)).then_inc(flag("mem_loaded"), 16)
        after(ac, "vec", "x1")
        rms_norm(junk, "x1", None)
        src = full(ac, "memk")
        copy_out(("memk",), mem_k[:, :, :], src.rearrange("p (a t) -> p a t", a=2))
        for th in range(TH):
            src = full(ac, "memv", th)
            copy_out(("memv", th), mem_v[:, th, :], src[:, 0:256])
        moe("e1")

        for n in range(MT):
            full(ac, "conv", n)
            if n >= 2:
                after(ac, "vec", f"glu_in{n - 2}")
            step(act(gatez[:, n % 2, :], psum[:, plan[("conv", n)][0], T:2 * T], ACT.Sigmoid))
            finish(ac, "act", f"conv_gate{n}")
        after(ac, "vec", "conv_var")
        step(act(stat[:, 1, :], stat[:, 1, :], ACT.Sqrt))
        finish(ac, "act", "conv_std")
        for n in range(MT):
            ac.wait_ge(flag("conv_norm"), n + 1)
            act(yT[:, n, :], conv[:, n, :], ACT.Silu, bias=V("ln_b")[:, n:n + 1], scale=V("ln_g")[:, n:n + 1]).then_inc(flag("conv_out"), 1)
        attention("at2", 4, yT[:, MT:KD, :])

        def layer_norm(name):
            after(ac, "vec", name + "_var")
            step(act(ln_r, ln_r, ACT.Sqrt))
            finish(ac, "act", name + "_std")

        def load_rows(a):
            for r in range(2):
                ac.dma_start(rows[:, r, :], ins["rows"][a + r:a + r + 1, :].partition_broadcast(P)).then_inc(flag(f"rows{a}"), 16)

        load_rows(1)
        layer_norm("ln21")
        after(ac, "vec", "e2_tok")
        load_rows(3)
        moe("e2")
        layer_norm("ln22")

        for n in range(3):
            src = full(ac, "mk", n)
            copy_out(("mk", n), kT3[:, 2 * n:2 * n + 2, :], src.rearrange("p (a t) -> p a t", a=2))
        for th in range(TH):
            src = full(ac, "mv0", th)
            copy_out(("mv0", th), v3[:, th, 0:512], src)
        for th in range(TH):
            src = full(ac, "mv1", th)
            copy_out(("mv1", th), v3[:, th, 512:768], src[:, 0:256])
        attention("at3", 12, yT[:, 0:MT, :])
        attention("at3m", 4, yT[:, MT:KD, :])
        load_rows(5)
        layer_norm("ln31")
        after(ac, "vec", "e3_tok")
        load_rows(7)
        moe("e3")
        layer_norm("ln32")

    @block.vector
    def _(ve):
        chain = flag("vec_chain")
        n_chain = [0]
        tt, ts, stt = ve.tensor_tensor, ve.tensor_scalar, ve.scalar_tensor_tensor

        def step(ins_):
            n_chain[0] += 1
            ins_.then_inc(chain, 1)
            ve.wait_ge(chain, n_chain[0])

        def tell(name):
            finish(ve, "vec", name)

        def over(a, *shape):
            while len(a.shape) < len(shape):
                a = a.unsqueeze(len(a.shape))
            return a.broadcast_to(list(shape))

        def rows_over(a, n):
            return a.unsqueeze(1).broadcast_to([P, n, a.shape[1]])

        def take_T(name, scale=None):
            for n in range(4):
                th, kk = n // 2, n % 2
                src = full(ve, name, n).rearrange("p (k t) -> p k t", k=4)
                dst = (memT if name == "memT" else xT)[:, 4 * kk:4 * kk + 4, th * P:(th + 1) * P]
                if scale is None:
                    read_out(ve.tensor_copy(dst, src), name, n)
                else:
                    read_out(tt(dst, src, over(scale[:, 4 * kk:4 * kk + 4], P, 4, P), ALU.mult), name, n)

        def split_heads(name, dst, src, j0, s1, s2=None):
            nt = src.shape[1]
            d = dst.rearrange("p (j o) t -> p j o t", o=2)
            for o in range(2):
                r = slice(o * HD, (o + 1) * HD)
                sc = s1[r] if s1 is not None else 1.0
                last = ts(d[r, j0:j0 + nt, o, :], src[r], sc, s2 if s2 is not None else 1.0, ALU.mult, ALU.mult)
                if o == 0:
                    step(last)
            read_out(last, *name)

        def attention(name, heads, op, scalar, causal):
            N = 2 * heads

            def unit(n):
                p, th, j = n // 4, n // 2 % 2, n % 2
                return 2 * p + j, th, (P if causal and th == 0 else T)

            for n in range(N + 1):
                if n < N:
                    h, th, W = unit(n)
                    src = full(ve, name, "score", n)[:, 0:W]
                    if n >= 2:
                        attn_wait(ve, name, "exp", n - 1)
                    dst = L_buf[:, n % 2, 0:W]
                    if causal:
                        ins_ = stt(out=dst, in0=src, scalar=scalar(h, th), in1=mask[:, th, 0:W], op0=op, op1=ALU.add)
                    else:
                        ins_ = ts(dst, src, scalar(h, th), None, op)
                    read_out(ins_, name, "score", n)
                    evacuated(ve, name, "score", n)
                    ve.tensor_reduce(nmax(n), dst, AX.X, ALU.max, negate=True).then_inc(flag("attn_logits"), 1)
                if n >= 1:
                    m = n - 1
                    h, th, W = unit(m)
                    attn_wait(ve, name, "exp", m + 1)
                    step(ve.reciprocal(precip(m), psums(m)))
                    ts(P_buf[:, m % 2, 0:W], P_buf[:, m % 2, 0:W], precip(m), None, ALU.mult).then_inc(flag("attn_probs"), 1)

        def residual(name, alpha):
            for n in range(4):
                th, hf = n // 2, n % 2
                src = full(ve, name, n)
                dst = x_sb[:, th, hf * 512:(hf + 1) * 512]
                read_out(stt(out=dst, in0=dst, scalar=alpha, in1=src, op0=ALU.mult, op1=ALU.add), name, n)
            for n in range(4):
                evacuated(ve, name, n)

        def moe_sum(e, alpha):
            ve.wait_ge(flag("moe_sum_ready"), int(e[1]))
            for n in range(4):
                th, hf = n // 2, n % 2
                dst = x_sb[:, th, hf * 512:(hf + 1) * 512]
                step(stt(out=dst, in0=dst, scalar=alpha, in1=psum[:, n, :], op0=ALU.mult, op1=ALU.add))

        def layer_norm(name, a):
            for th in range(TH):
                for hf in range(2):
                    step(ve.bn_stats(bn6[:, th, hf, :], x_sb[:, th, hf * 512:(hf + 1) * 512]))
                step(ve.bn_aggr(bn2[:, th, :], bn6[:, th, :, :]))
            step(ts(ln_r, bn2[:, :, 1], 1e-5, None, ALU.add))
            tell(name + "_var")
            after(ve, "act", name + "_std")
            step(ve.reciprocal(ln_r, ln_r))
            for th in range(TH):
                step(ts(x_sb[:, th, :], x_sb[:, th, :], bn2[:, th, 0:1], ln_r[:, th:th + 1], ALU.subtract, ALU.mult))
            ve.wait_ge(flag(f"rows{a}"), 32)
            step(tt(x_sb[:, :, :], x_sb[:, :, :], rows_over(rows[:, 0, :], TH), ALU.mult))
            step(tt(x_sb[:, :, :], x_sb[:, :, :], rows_over(rows[:, 1, :], TH), ALU.add))

        def rms_norm(name, dst):
            after(ve, "act", name + "_sq")
            step(ts(rms_r, rms_ms, 1.0 / D, 1e-6, ALU.mult, ALU.add))
            tell(name + "_ms")
            after(ve, "act", name + "_rms")
            step(ve.reciprocal(rms_r, rms_r))
            for th in range(TH):
                step(ts(dst[:, th, :], x_sb[:, th, :], rms_r[:, th:th + 1], None, ALU.mult))

        def moe(e):
            F = 2 if e == "e1" else 4
            W = F * CAP
            n_e = int(e[1]) - 1
            take_T(e + "xT")
            step(ve.memset(og[:, 0:512], 0.0))
            tell(e + "_zero")
            src = full(ve, e + "logits")[:, 0:TH * NR].rearrange("p (h n) -> p h n", h=TH)
            read_out(tt(r_L, src, rows_over(brow[:, 8 + n_e * NR:8 + (n_e + 1) * NR], TH), ALU.add), e + "logits")
            evacuated(ve, e + "logits")
            step(ve.tensor_reduce(r_gmax, r_L[:, :, 0:NG], AX.X, ALU.max))
            step(tt(r_gd, r_L[:, :, 0:NG], over(r_gmax, P, TH, NG), ALU.subtract))
            tell(e + "_gd")

            def first_max(x, top, eq, cand, first, onehot, n):
                step(tt(eq, x, over(top, P, TH, n), ALU.is_equal))
                step(stt(out=cand, in0=eq, scalar=-100.0, in1=rows_over(col_id[:, 0:n], TH), op0=ALU.mult, op1=ALU.add))
                step(ve.tensor_reduce(first, cand, AX.X, ALU.min))
                step(tt(onehot, cand, over(first, P, TH, n), ALU.is_equal))

            first_max(r_L[:, :, 0:NG], r_gmax, r_geq, r_gc, r_gfirst, r_goh, NG)
            step(ts(r_pen, r_goh, -1.0, 1e30, ALU.add, ALU.mult))
            step(tt(r_EL.rearrange("p h (g x) -> p h g x", g=NG), r_L[:, :, NG:NR].rearrange("p h (g x) -> p h g x", g=NG),
                    over(r_pen, P, TH, NG, EPG), ALU.add))
            step(ve.tensor_reduce(r_m1, r_EL, AX.X, ALU.max))
            first_max(r_EL, r_m1, r_eq, r_cand, r_f1, r_oh1, NE)
            step(stt(out=r_EL, in0=r_oh1, scalar=-3e38, in1=r_EL, op0=ALU.mult, op1=ALU.add))
            step(ve.tensor_reduce(r_m2, r_EL, AX.X, ALU.max))
            first_max(r_EL, r_m2, r_eq, r_cand, r_f2, r_oh2, NE)
            step(tt(sel, r_oh1, r_oh2, ALU.add))
            tell(e + "_sel")
            step(tt(r_d21, r_m2, r_m1, ALU.subtract))
            tell(e + "_d21")
            after(ve, "act", e + "_ge")
            step(ve.tensor_reduce(r_gs, r_ge, AX.X, ALU.add))
            step(ve.reciprocal(r_gw, r_gs))
            after(ve, "act", e + "_p2")
            step(ts(r_rd, r_p2, 1.0, None, ALU.add))
            step(ve.reciprocal(r_rd, r_rd))
            step(tt(r_w1, r_gw, r_rd, ALU.mult))
            step(tt(r_w2, r_w1, r_p2, ALU.mult))
            step(ve.memset(wcomb, 0.0))
            step(ve.memset(rank, -1.0))
            step(tt(r_t, r_oh1, over(r_w1, P, TH, NE), ALU.mult))
            step(tt(r_cand, r_oh2, over(r_w2, P, TH, NE), ALU.mult))
            step(tt(wcomb[:, :, 0:NE], r_t, r_cand, ALU.add))
            src = full(ve, e + "rank")
            step(stt(out=r_t, in0=src[:, 0:2 * NE].rearrange("p (h n) -> p h n", h=TH), scalar=1.0, in1=sel, op0=ALU.add, op1=ALU.mult))
            step(ts(rank[:, :, 0:NE], r_t, -1.0, None, ALU.add))
            read_out(ve.tensor_reduce(r_cmax, src[:, 2 * NE:3 * NE], AX.X, ALU.max), e + "rank")
            evacuated(ve, e + "rank")
            step(ts(r_np, r_cmax, float(CAP), 1.0, ALU.is_gt, ALU.add))
            for k in range(2, T // CAP):
                step(stt(out=r_np, in0=r_cmax, scalar=float(k * CAP), in1=r_np, op0=ALU.is_gt, op1=ALU.add))
            step(ve.tensor_copy(npass[:, :], r_np))
            tell(e + "_npass")

            def one_hot(par, j):
                s4 = S[:, par, :, :].rearrange("p h (x c) -> p h x c", x=2)
                sw4 = Sw[:, par, :, :].rearrange("p h (x c) -> p h x c", x=2)
                ids = col_id[:, :].unsqueeze(1).unsqueeze(1).broadcast_to([P, TH, 2, CAP])
                tt(s4, ids, over(rank[:, :, bass.ds(j * 2, 2)], P, TH, 2, CAP), ALU.is_equal).then_inc(flag("moe_S"), 1)
                moe_wait(ve, e, "S", j * 2 + 1)
                tt(sw4, s4, over(wcomb[:, :, bass.ds(j * 2, 2)], P, TH, 2, CAP), ALU.mult).then_inc(flag("moe_S"), 1)

            def gathered(par):
                ve.tensor_copy(xg[:, par, 4:8, :], psum[:, 7, :].rearrange("p (k c) -> p k c", k=4)).then_inc(flag("moe_xgB"), 1)

            one_hot(0, 0)
            moe_wait(ve, e, "gathB", 1)
            gathered(0)
            with ve.Fori(0, 8) as i:
                for u in range(2):
                    def c(k, per=1):
                        return i * (2 * per) + (u * per + k)

                    one_hot(1 - u, c(1))
                    for x in range(2):
                        moe_wait(ve, e, "silu", c(x + 1, 2))
                        tt(hh[:, x, 0:W], sg[:, x, 0:W], psum[:, 5 + x, W:2 * W], ALU.mult).then_inc(flag("moe_h"), 1)
                    moe_wait(ve, e, "gathB", c(2))
                    gathered(1 - u)
                    hs, per, at_u = moe_slots(e, u)[5]
                    ve.wait_ge(used[hs], i * per + (moe_used[e][hs] + at_u + 1))
                    ve.tensor_copy(og[:, 512:1024], psum[:, 7, :]).then_inc(flag("moe_outB"), 1)
            n = ve.value_load(npass[0:1, 0:1], min_val=1, max_val=T // CAP)
            with ve.If(n > 1):
                moe_wait(ve, e, "scattered", PAIRS)
                with ve.Fori(1, n) as p:
                    ve.wait_ge(flag(e + "_ovf_pe"), (p - 1) * (4 * NE))
                    ts(rank, rank, -float(CAP), None, ALU.add).then_inc(flag(e + "_ovf_vec"), 1)
                    with ve.Fori(0, NE) as x:
                        j = (p - 1) * NE + x
                        ve.wait_ge(flag(e + "_ovf_pe"), j * 4)
                        ve.wait_ge(flag(e + "_ovf_vec"), (p - 1) * (8 * NE + 1) + 1)
                        s3, sw3 = S[:, 0, :, 0:CAP], Sw[:, 0, :, 0:CAP]
                        tt(s3, rows_over(col_id[:, :], TH), rank[:, :, bass.ds(x, 1)].broadcast_to([P, TH, CAP]), ALU.is_equal).then_inc(flag(e + "_ovf_vec"), 1)
                        ve.wait_ge(flag(e + "_ovf_vec"), j * 8 + p + 1)
                        tt(sw3, s3, wcomb[:, :, bass.ds(x, 1)].broadcast_to([P, TH, CAP]), ALU.mult).then_inc(flag(e + "_ovf_vec"), 1)
                        ve.wait_ge(flag(e + "_ovf_pe"), j * 4 + 1)
                        for half, b in enumerate((4, 7)):
                            ve.tensor_copy(xg[:, 0, 4 * half:4 * half + 4, 0:CAP], psum[:, b, 0:4 * CAP].rearrange("p (k c) -> p k c", k=4)).then_inc(flag(e + "_ovf_vec"), 1)
                        ve.tensor_copy(SwT[0:CAP, :], psum[0:CAP, 6, 0:T]).then_inc(flag(e + "_ovf_vec"), 1)
                        ve.wait_ge(flag(e + "_ovf_silu"), j + 1)
                        tt(hh[:, 0, 0:W], sg[:, 0, 0:W], psum[:, 5, W:2 * W], ALU.mult).then_inc(flag(e + "_ovf_vec"), 1)
                        ve.wait_ge(flag(e + "_ovf_pe"), j * 4 + 3)
                        for half in range(2):
                            ve.tensor_copy(og[0:CAP, half * 512:(half + 1) * 512], psum[0:CAP, 6 + half, :]).then_inc(flag(e + "_ovf_vec"), 1)

        after(ve, "act", "ssm_dt")
        sc = lambda n: ssm_s[:, n, :]
        step(tt(s_adt, V("a_re"), s_dt, ALU.mult))
        tell("ssm_adt")
        step(tt(s_th, V("a_im"), s_dt, ALU.mult))
        step(ts(sc(6), s_th, 1.0 / (2 * np.pi), ROUND, ALU.mult, ALU.add))
        step(ts(sc(6), sc(6), -ROUND, None, ALU.add))
        step(stt(out=sc(7), in0=sc(6), scalar=-TWO_PI_HI, in1=s_th, op0=ALU.mult, op1=ALU.add))
        step(stt(out=sc(7), in0=sc(6), scalar=-TWO_PI_LO, in1=sc(7), op0=ALU.mult, op1=ALU.add))
        step(ts(sc(5), sc(7), SIN_MAX, -SIN_MAX, ALU.min, ALU.max))
        step(stt(out=sc(6), in0=sc(5), scalar=-1.0, in1=sc(5), op0=ALU.mult, op1=ALU.min))
        step(ts(sc(4), sc(6), np.pi / 2, None, ALU.add))
        tell("ssm_angle")
        after(ve, "act", "ssm_sin")
        for k in range(LEVELS - 1):
            step(tt(sc(6), e_pow(k, 0), e_pow(k, 0), ALU.mult))
            step(tt(sc(7), e_pow(k, 1), e_pow(k, 1), ALU.mult))
            step(tt(e_pow(k + 1, 0), sc(6), sc(7), ALU.subtract))
            step(stt(out=e_pow(k + 1, 1), in0=e_pow(k, 0), scalar=2.0, in1=e_pow(k, 1), op0=ALU.mult, op1=ALU.mult))
        tell("ssm_powers2")
        rms_norm("x", h_tok)
        tell("h_tok")
        are, aim = V("a_re"), V("a_im")
        step(tt(sc(6), s_mag, e_pow(0, 0), ALU.mult))
        step(ts(sc(6), sc(6), -1.0, None, ALU.add))
        step(tt(sc(7), s_mag, e_pow(0, 1), ALU.mult))
        step(tt(sc(8), are, are, ALU.mult))
        step(tt(sc(9), aim, aim, ALU.mult))
        step(tt(sc(8), sc(8), sc(9), ALU.add))
        step(ve.reciprocal(sc(8), sc(8)))
        step(tt(sc(9), sc(6), are, ALU.mult))
        step(tt(sc(10), sc(7), aim, ALU.mult))
        step(tt(sc(9), sc(9), sc(10), ALU.add))
        step(tt(sc(9), sc(9), sc(8), ALU.mult))
        step(tt(sc(10), sc(7), are, ALU.mult))
        step(tt(sc(11), sc(6), aim, ALU.mult))
        step(tt(sc(10), sc(10), sc(11), ALU.subtract))
        step(tt(sc(10), sc(10), sc(8), ALU.mult))
        take_T("hT", V("mix_g"))
        for w, c0 in (("q", 0), ("k", 512)):
            for th in range(TH):
                src = full(ve, w, th)
                read_out(ve.tensor_copy(qk_tok[:, th, c0:c0 + 512], src), w, th)
        for w in "qk":
            for th in range(TH):
                evacuated(ve, w, th)
        for th in range(TH):
            step(tt(square_junk, qk_tok[:, th, :], qk_tok[:, th, :], ALU.mult))
            step(ve.tensor_reduce(qk_r[:, th * 16:(th + 1) * 16], square_junk.rearrange("p (h d) -> p h d", h=16), AX.X, ALU.add))
        step(ts(qk_r, qk_r, 1.0 / HD, 1e-6, ALU.mult, ALU.add))
        tell("qk_ms")
        src = full(ve, "f")[:, 0:16].rearrange("p (a h) -> p a h", a=2)
        fr = f_raw.rearrange("p (a h) -> p a h", a=2)
        read_out(tt(fr, src, rows_over(brow[:, 0:8], TH), ALU.add), "f")
        evacuated(ve, "f")
        step(stt(out=f_abs, in0=f_raw, scalar=-1.0, in1=f_raw, op0=ALU.mult, op1=ALU.max))
        tell("f_abs")
        after(ve, "act", "qk_rms")
        step(ve.reciprocal(qk_r, qk_r))
        for th in range(TH):
            v3_ = qk_tok[:, th, :].rearrange("p (h d) -> p h d", h=16)
            step(tt(v3_, v3_, over(qk_r[:, th * 16:(th + 1) * 16], P, 16, HD), ALU.mult))
        tell("qk_tok")
        after(ve, "act", "f_ln")
        lf_pos = lf[:, 0, :, :].rearrange("p a h -> p (a h)")
        lf_neg = lf[:, 1, :, :].rearrange("p a h -> p (a h)")
        step(stt(out=lf_pos, in0=f_raw, scalar=0.0, in1=f_l, op0=ALU.min, op1=ALU.subtract))
        step(ts(lf_neg, lf_pos, -1.0, None, ALU.mult))
        tell("logf")
        step(ve.memset(qz1, 0.0))
        for th in range(TH):
            src = full(ve, "qT", th).rearrange("p (j t) -> p j t", j=4)
            split_heads(("qT", th), qz1[:, :, th * P:(th + 1) * P], src, 0, V("qg"), HD ** -0.5)
        for th in range(TH):
            src = full(ve, "kT", th).rearrange("p (j t) -> p j t", j=4)
            read_out(ts(kT1[:, :, th * P:(th + 1) * P], src, V("kg"), None, ALU.mult), "kT", th)
        after(ve, "pool", "masks")
        src = full(ve, "F")
        step(ve.tensor_copy(Ft, src[:, 0:16].rearrange("p (a h) -> p a h", a=2)))
        read_out(ve.tensor_copy(nF[0:8, :], src[0:8, 128:128 + T]), "F")
        after(ve, "pool", "powers")
        step(ve.memset(c_blk, 0.0))
        cr, ci = (V(n).rearrange("p (j c) -> p j c", j=NJ) for n in ("c_re", "c_im"))
        fr_, fi_ = over(sc(9), P, NJ, 16), over(sc(10), P, NJ, 16)
        t1, t2 = (at(4096 + 256 * n, NJ, 16) for n in range(2))
        for c_ in range(2):
            step(tt(t1, cr, (fr_, fi_)[c_], ALU.mult))
            step(tt(t2, ci, (fi_, fr_)[c_], ALU.mult))
            step(tt(t1, t1, t2, (ALU.subtract, ALU.add)[c_]))
            if c_:
                step(ts(t1, t1, -1.0, None, ALU.mult))
            t1q = t1.rearrange("p (q j) c -> p q j c", q=NQ)
            blk = c_blk[:, c_, :, :].rearrange("p (q j) s -> p q j s", q=NQ)
            for jj in range(4):
                for o in range(2):
                    r = slice(o * HD, (o + 1) * HD)
                    col = (2 * jj + o) * 16
                    step(ve.tensor_copy(blk[r, :, jj, col:col + 16], t1q[r, :, jj, :]))
        ta, tb = tmp[:, 0, :, :], tmp[:, 1, :, :]
        zr, zi = zs[:, 0, :, :], zs[:, 1, :, :]
        carry = ssm_s[:, 12:16, 0:4]
        for q in range(NQ):
            js = slice(4 * q, 4 * q + 4)
            c_t, s_t = powers[:, 0, js, :], powers[:, 1, js, :]
            for b in range(2, 6):
                full(ve, "bu", q, b)
            bu = psum[:, 2:6, :].rearrange("p (c b) (a t) -> p c (b a) t", c=2, a=2)
            for half in range(2):
                br, bi = (bu[:, c_, :, half * HALF_T:(half + 1) * HALF_T] for c_ in range(2))
                wr_, wi = ws[:, half, 0, :, :], ws[:, half, 1, :, :]
                if q:
                    ve.wait_ge(flag("ssm_y"), 2 * (q - 1) + half + 1)
                step(tt(ta, c_t, br, ALU.mult))
                step(tt(tb, s_t, bi, ALU.mult))
                step(tt(wr_, ta, tb, ALU.add))
                step(tt(ta, c_t, bi, ALU.mult))
                step(tt(tb, s_t, br, ALU.mult))
                step(tt(wi, ta, tb, ALU.subtract))
                if half:
                    for b in range(2, 6):
                        ve.sem_inc(bank_free[b], 1)
                for jj in range(4):
                    mag = s_mag[:, 4 * q + jj:4 * q + jj + 1].broadcast_to([P, HALF_T])
                    for c_, (w_, z_) in enumerate(((wr_, zr), (wi, zi))):
                        init = carry[:, c_, jj:jj + 1] if half else 0.0
                        step(ve.tensor_tensor_scan(z_[:, jj, :], mag, w_[:, jj, :], init, ALU.mult, ALU.add))
                step(tt(ta, c_t, zr, ALU.mult))
                step(tt(tb, s_t, zi, ALU.mult))
                step(tt(wr_, ta, tb, ALU.subtract))
                step(tt(ta, c_t, zi, ALU.mult))
                step(tt(tb, s_t, zr, ALU.mult))
                step(tt(wi, ta, tb, ALU.add))
                tell(f"ssm_state{2 * q + half}")
                if half == 0:
                    c1, s1 = e_pow(0, 0)[:, js], e_pow(0, 1)[:, js]
                    xr, xi = wr_[:, :, HALF_T - 1], wi[:, :, HALF_T - 1]
                    step(tt(carry[:, 2, :], c1, xr, ALU.mult))
                    step(tt(carry[:, 3, :], s1, xi, ALU.mult))
                    step(tt(carry[:, 0, :], carry[:, 2, :], carry[:, 3, :], ALU.subtract))
                    step(tt(carry[:, 2, :], c1, xi, ALU.mult))
                    step(tt(carry[:, 3, :], s1, xr, ALU.mult))
                    step(tt(carry[:, 1, :], carry[:, 2, :], carry[:, 3, :], ALU.add))
            src = full(ve, "y", q)
            read_out(stt(out=yg[:, q, :], in0=uT[:, q, :], scalar=V("d_skip")[:, q:q + 1], in1=src[:, 0:T],
                         op0=ALU.mult, op1=ALU.add), "y", q)
        attention("at1", 8, ALU.add, lambda h, th: Ft[:, th, h:h + 1], True)
        for n in range(2):
            evacuated(ve, "glu", n)
        step(tt(y_ssm, y_ssm, yg, ALU.mult))
        tell("y_ssm")
        for n in range(4):
            src = full(ve, "pa", n).rearrange("p (a t) -> p a t", a=2)
            read_out(tt(mixedT[:, 2 * n:2 * n + 2, :], src, gates[:, 2 * n:2 * n + 2, :], ALU.mult), "pa", n)
            src = full(ve, "ps", n).rearrange("p (a t) -> p a t", a=2)
            read_out(tt(mix_tmp, src, gates[:, 8 + 2 * n:10 + 2 * n, :], ALU.mult), "ps", n)
            evacuated(ve, "pa", n)
            evacuated(ve, "ps", n)
            tt(mixedT[:, 2 * n:2 * n + 2, :], mixedT[:, 2 * n:2 * n + 2, :], mix_tmp, ALU.add).then_inc(flag("mixed"), 1)
            ve.wait_ge(flag("mixed"), n + 1)
        residual("res1", 1.0)
        tell("x1")
        rms_norm("x1", xh)
        ve.wait_ge(flag("gain_loaded"), 16)
        step(tt(xh, xh, rows_over(gain, TH), ALU.mult))
        tell("e1_tok")
        take_T("memT")
        moe("e1")
        moe_sum("e1", 1.0)
        tell("x2")

        take_T("x2T")
        step(ve.memset(hpad, 0.0))
        step(ve.memset(qz2, 0.0))
        for n in range(MT):
            after(ve, "act", f"conv_gate{n}")
            src = full(ve, "conv", n)
            read_out(tt(hpad[:, n, PAD:PAD + T], src[:, 0:T], gatez[:, n % 2, :], ALU.mult), "conv", n)
            evacuated(ve, "conv", n)
            tell(f"glu_in{n}")
        src = full(ve, "qm2").rearrange("p (a t) -> p a t", a=2)
        split_heads(("qm2",), qz2, src, 0, None)
        tap = flag("conv_tap")
        dw = V("dw_w")
        for n in range(MT):
            ts(conv[:, n, :], hpad[:, n, 0:T], dw[:, n * TAPS:n * TAPS + 1], V("dw_b")[:, n:n + 1], ALU.mult, ALU.add).then_inc(tap, 1)
        with ve.Fori(1, TAPS) as k:
            for n in range(MT):
                ve.wait_ge(tap, k * MT + (n - MT + 1))
                stt(out=conv[:, n, :], in0=hpad[:, n, bass.ds(k, T)], scalar=dw[:, bass.ds(k + n * TAPS, 1)],
                    in1=conv[:, n, :], op0=ALU.mult, op1=ALU.add).then_inc(tap, 1)
        ve.wait_ge(tap, MT * TAPS)
        tell("conv_done")
        src = full(ve, "mean")
        read_out(ts(stat[:, 0, :], src[:, 0:T], 1.0 / MIX, None, ALU.mult), "mean")
        evacuated(ve, "mean")
        step(tt(conv, conv, rows_over(stat[:, 0, :], MT), ALU.subtract))
        step(tt(sq, conv, conv, ALU.mult))
        tell("conv_sq")
        src = full(ve, "var")
        read_out(ts(stat[:, 1, :], src[:, 0:T], 1.0 / MIX, 1e-5, ALU.mult, ALU.add), "var")
        evacuated(ve, "var")
        tell("conv_var")
        after(ve, "act", "conv_std")
        step(ve.reciprocal(stat[:, 1, :], stat[:, 1, :]))
        for n in range(MT):
            tt(conv[:, n, :], conv[:, n, :], stat[:, 1, :], ALU.mult).then_inc(flag("conv_norm"), 1)
        attention("at2", 4, ALU.mult, lambda h, th: HD ** -0.5, False)
        residual("res2", ALPHA)
        layer_norm("ln21", 1)
        tell("e2_tok")
        moe("e2")
        moe_sum("e2", ALPHA)
        layer_norm("ln22", 3)
        tell("x3")

        take_T("x3T")
        step(ve.memset(qz3, 0.0))
        step(ve.memset(qz3m, 0.0))
        for n in range(3):
            src = full(ve, "mq", n).rearrange("p (a t) -> p a t", a=2)
            split_heads(("mq", n), qz3, src, 2 * n, None)
        src = full(ve, "qm3").rearrange("p (a t) -> p a t", a=2)
        split_heads(("qm3",), qz3m, src, 0, None)
        attention("at3", 12, ALU.mult, lambda h, th: HD ** -0.5, True)
        attention("at3m", 4, ALU.mult, lambda h, th: HD ** -0.5, False)
        residual("res3", ALPHA)
        layer_norm("ln31", 5)
        tell("e3_tok")
        moe("e3")
        moe_sum("e3", ALPHA)
        layer_norm("ln32", 7)
        tell("x_final")


def _tiles(w, c0, c1, slot=True):
    w = w[:, c0:c1]
    k = w.shape[0] // P
    w = w.reshape(k, P, c1 - c0).transpose(1, 0, 2)
    if k * (c1 - c0) < SLOT:
        out = np.zeros((P, SLOT), np.float32)
        if k == KD:
            out.reshape(P, KD, 512)[:, :, :c1 - c0] = w
        else:
            out[:, :k * (c1 - c0)] = w.reshape(P, -1)
        return out
    return w.reshape(P, -1)


def _experts(w):
    e, r, c = w.shape
    return np.ascontiguousarray(w.reshape(e, r // P, P, c).transpose(0, 2, 1, 3).reshape(e, P, (r // P) * c))


def _layout(a):
    w_in = a["w_in"][0]
    chunks = {"u": _tiles(w_in, 1544, 2056), "q": _tiles(w_in, 0, 512), "k": _tiles(w_in, 512, 1024),
              "v": _tiles(w_in, 1024, 1536), "glu": _tiles(a["w_glu"][0], 0, 512),
              "pa": _tiles(a["w_proj_attn"][0], 0, D), "ps": _tiles(a["w_proj_ssm"][0], 0, D),
              "memkv": _tiles(a["w_mem_kv_2"], 0, 512)}
    for n in range(4):
        chunks[f"g{n}"] = _tiles(w_in, 2056 + 512 * n, 2568 + 512 * n)
    for name, w in (("wo", a["w_out"][0]), ("w2o", a["w_o_2"][0]), ("w3o", a["w_o_2"][1])):
        for n in range(2):
            chunks[f"{name}{n}"] = _tiles(w[512 * n:512 * (n + 1)], 0, D)
    cw = a["conv_w_in_2"][0]
    for n in range(3):
        cols = [cw[:, c + P * (2 * n + m):c + P * (2 * n + m + 1)] for m in range(2) for c in (0, MIX)]
        chunks[f"c{n}"] = _tiles(np.concatenate(cols, 1), 0, 512)
    chunks["c3"] = _tiles(cw, 2 * MIX, 2 * MIX + 256)
    mw = a["moba_w_in_2"][0]
    for n in range(5):
        chunks[f"m{n}"] = _tiles(mw, 512 * n, 512 * (n + 1))
    out = {"stream": np.stack([chunks[c] for c in CHUNKS])}

    by_part = lambda v: v.reshape(-1, P).T
    state = lambda v: v.reshape(NJ, 2 * HD).T
    cmat = lambda c: c.transpose(0, 2, 1).reshape(NJ, P, 16).transpose(1, 0, 2).reshape(P, NJ * 16)
    ldt = np.repeat(a["ssm_log_dt"][0][:, None], HD, axis=1)
    parts = {"mix_g": by_part(a["norm_mix_g"][0]), "qg": np.tile(a["q_norm_g"][0], 2)[:, None],
             "kg": np.tile(a["k_norm_g"][0], 2)[:, None], "a_re": state(a["ssm_A_re"][0]), "a_im": state(a["ssm_A_im"][0]),
             "log_dt": state(ldt), "d_skip": by_part(a["ssm_D"][0]), "dw_b": by_part(a["conv_dw_b_2"][0]),
             "ln_g": by_part(a["conv_ln_g_2"][0]), "ln_b": by_part(a["conv_ln_b_2"][0]),
             "dw_w": a["conv_dw_w_2"][0].T.reshape(MT, P, TAPS).transpose(1, 0, 2).reshape(P, MT * TAPS),
             "c_re": cmat(a["ssm_C_re"][0]), "c_im": cmat(a["ssm_C_im"][0])}
    out["vec"] = np.concatenate([parts[n] for n in VEC], 1)
    blk = np.zeros((2, P, NJ, P), np.float32)
    for c, name in enumerate(("ssm_B_re", "ssm_B_im")):
        b = a[name][0]
        for g in range(32):
            j, o = g // 2, g % 2
            r = (g % 8) * 16
            blk[c, r:r + 16, j, o * HD:(o + 1) * HD] = b[g].T
    out["b_blk"] = blk
    out["wf"] = w_in[:, 1536:1544].reshape(KD, P, 8).transpose(1, 0, 2)
    rg = [a["w_router_group"][0], a["w_rg_2"][0], a["w_rg_2"][1]]
    re = [a["w_router_expert"][0], a["w_re_2"][0], a["w_re_2"][1]]
    out["wr"] = np.stack([np.concatenate([g, e], 1).reshape(KD, P, NR).transpose(1, 0, 2) for g, e in zip(rg, re)])
    out["brow"] = np.concatenate([a["b_forget"][0], a["b_router_group"][0], a["b_router_expert"][0],
                                  a["b_rg_2"][0], a["b_re_2"][0], a["b_rg_2"][1], a["b_re_2"][1]])[None, :]
    rows = [a["norm_ffn_g"][0]]
    for n in range(2):
        rows += [a["ln1_g_2"][n], a["ln1_b_2"][n], a["ln2_g_2"][n], a["ln2_b_2"][n]]
    out["rows"] = np.stack(rows)
    out["x"] = a["x"][0]
    out["mem"] = a["mem_2"][0]
    for e, (g, u, d) in (("e1", (a["w_expert_gate"][0], a["w_expert_up"][0], a["w_expert_down"][0])),
                         ("e2", tuple(a[n][0].reshape(NE, *a[n].shape[3:]) for n in ("w_gate_2", "w_up_2", "w_down_2"))),
                         ("e3", tuple(a[n][1].reshape(NE, *a[n].shape[3:]) for n in ("w_gate_2", "w_up_2", "w_down_2")))):
        out[e + "_gate"], out[e + "_up"], out[e + "_down"] = _experts(g), _experts(u), _experts(d)
    return {n: np.ascontiguousarray(v) for n, v in out.items()}


def kernel(**inputs):
    import concourse.bacc as _bacc
    from concourse.bass_utils import run_bass_kernel_spmd as _run

    arrays = _layout({n: np.asarray(v) for n, v in inputs.items()})
    nc = _bacc.Bacc("TRN2", target_bir_lowering=False, num_devices=1)
    named = {n: nc.dram_tensor(f"in_{n}", v.shape, F32, kind="ExternalInput").ap() for n, v in arrays.items()}
    out = nc.dram_tensor("out_x", (T, D), F32, kind="ExternalOutput").ap()
    build(nc, named, out)
    r = _run(nc, [{f"in_{n}": v for n, v in arrays.items()}], core_ids=[0])
    return r.results[0]["out_x"].reshape(1, T, D)
```

```python
from contextlib import ExitStack

import numpy as np
import concourse.bass as bass
from concourse import mybir

ALU = mybir.AluOpType
ACT = mybir.ActivationFunctionType
AX = mybir.AxisListType
F32 = mybir.dt.float32
I32 = mybir.dt.int32

P = 128
D = 1024
KD = D // P
T = 256
TH = T // P
HD = 64
NE, NG, EPG = 32, 4, 8
NR = NG + NE
TOP_K = 2
CAP = 64
PAIRS = NE // 2
EXTRA = T // CAP - 1
NOVF = TOP_K * T // CAP - 1
NJ = 16
NQ = 4
HALF_T = 128
LEVELS = 7
TAPS = 31
MIX = 768
MT = MIX // P
PAD = TAPS - 1
SLOT = 4096
NSLOT = 6
NBUF = 4
ALPHA = (2 * 2) ** 0.25
MASKED = -1e30
TWO_PI_HI = 6.28125
TWO_PI_LO = 2 * np.pi - 6.28125
ROUND = 1.5 * 2 ** 23
SIN_MAX = 3.1415925

VEC = {}
_n = 0
for _name, _w in (("mix_g", KD), ("qg", 1), ("kg", 1), ("a_re", NJ), ("a_im", NJ), ("log_dt", NJ),
                  ("d_skip", NQ), ("dw_b", MT), ("ln_g", MT), ("ln_b", MT), ("dw_w", MT * TAPS),
                  ("c_re", NJ * 16), ("c_im", NJ * 16)):
    VEC[_name] = (_n, _n + _w)
    _n += _w
NVEC = _n

STREAM = (["u", "q", "k", "v", "g0", "g1", "g2", "g3", "glu", "pa", "ps", "wo0", "wo1", "memkv"],
          ["c0", "c1", "c2", "c3", "w2o0", "w2o1"],
          ["m0", "m1", "m2", "m3", "m4", "w3o0", "w3o1"])
CHUNKS = [n for part in STREAM for n in part]


def build(nc, ins, out):
    ctx = ExitStack()
    with ctx:
        _build(ctx, nc, ins, out)


def _build(ctx, nc, ins, out):
    def sb(name, shape, dt=F32):
        return ctx.enter_context(nc.sbuf_tensor(name, shape, dt))

    sems = {}

    def flag(name):
        if name not in sems:
            sems[name] = ctx.enter_context(nc.semaphore(name))
        return sems[name]

    ring = sb("ring", [P, NSLOT, SLOT])
    x_sb = sb("x_sb", [P, TH, D])
    xT = sb("xT", [P, KD, T])
    ident = sb("ident", [P, P])
    ones = sb("ones", [P, P])
    before = sb("before", [P, P])
    upto = sb("upto", [P, TH, T])
    mask = sb("mask", [P, TH, T])
    col_id = sb("col_id", [P, EXTRA * NE])
    vec = sb("vec", [P, NVEC])
    rows = sb("rows", [P, 2, D])
    head_sel = rows[:, 0, :].rearrange("p (h t) -> p h t", h=8)
    nF = sb("nF", [P, T])
    mem_k = sb("mem_k", [P, 2, T])
    mem_v = sb("mem_v", [P, TH, 256])
    wr = sb("wr", [P, KD, NR])
    brow = sb("brow", [P, 8 + 3 * NR])
    small = sb("small", [P, 256])
    ovf = sb("ovf", [P, 2 * NOVF + 2], I32)
    arena = sb("arena", [P, 15360])

    def at(off, *dims):
        n = int(np.prod(dims))
        a = arena[:, off:off + n]
        if len(dims) == 1:
            return a
        names = "abcd"[:len(dims)]
        return a.rearrange(f"p ({' '.join(names)}) -> p {' '.join(names)}",
                           **{c: d for c, d in zip(names[:-1], dims[:-1])})

    V = lambda name: vec[:, VEC[name][0]:VEC[name][1]]

    gates = at(0, 16, T)
    h_tok = at(0, TH, D)
    qk_tok = at(2048, TH, 1024)
    zs = at(4096, 2, 4, HALF_T)
    tmp = at(5120, 2, 4, HALF_T)
    mixedT = at(4096, KD, T)
    ws = at(6144, 2, 2, 4, HALF_T)
    y_ssm = at(6144, NQ, T)
    v_tok = at(8192, TH, 512)
    qz1 = at(9216, 8, T)
    kT1 = at(11264, 4, T)
    uT = at(12288, NQ, T)
    yg = at(13312, NQ, T)
    ya = at(14336, 4, T)
    powers = ring[:, 3, :].rearrange("p (c j t) -> p c j t", c=2, j=NJ)
    b_blk = ring[:, 4:6, 0:2048].rearrange("p c (j s) -> p c j s", j=NJ)
    c_blk = ring[:, 4:6, 2048:4096].rearrange("p c (j s) -> p c j s", j=NJ)
    P_buf = rows[:, 1, :].rearrange("p (b t) -> p b t", b=NBUF)
    PT_buf = sb("PT_buf", [P, 2, T])
    gatez = at(0, 2, T)
    hpad = at(2048, MT, PAD + T)
    conv = at(3840, MT, T)
    sq = at(5376, MT, T)
    stat = at(6912, 4, T)
    qz2 = at(8192, 4, T)
    yT = at(9216, KD, T)
    qz3 = at(0, 12, T)
    kT3 = at(3072, MT, T)
    v3 = at(4608, TH, MIX)
    qz3m = at(6144, 4, T)
    xh = at(0, TH, D)
    S = at(2048, 2, TH, 2 * CAP)
    Sw = at(2560, 2, TH, 2 * CAP)
    SwT = at(3072, T)
    xg = at(3328, 2, KD, 2 * CAP)
    sg = at(5376, 512)
    hT = at(5888, 4, 2 * CAP)
    og = at(6400, D)
    rt = at(7424, 4096)
    rank = at(11520, TH, NE + 2)
    wcomb = at(11588, TH, NE + 2)
    sel = at(11656, TH, NE)
    hh = at(11720, 512)
    rank3 = at(12232, TH, EXTRA, NE)
    wcomb3 = at(12424, TH, EXTRA, NE)
    item_eq = at(12616, NOVF, EXTRA * NE)
    item_t = at(13288, NOVF, EXTRA * NE)
    junk = at(12288, D)

    gain = rows[:, 0, :]
    mem_tok = at(9216, TH, D)
    memT = at(13312, KD, T)
    wf = sb("wf", [P, KD, 8])
    lf = sb("lf", [P, 2, TH, 8])
    e_tab = sb("e_tab", [P, LEVELS + 1, 2, NJ])
    ssm_s = sb("ssm_s", [P, 16, NJ])

    def e_pow(k, c):
        return e_tab[:, k, c, :]

    rms_ms = small[:, 0:2]
    rms_r = small[:, 2:4]
    ln_r = small[:, 4:6]
    nmax = lambda n: small[:, 156 + n % NBUF:157 + n % NBUF]
    psums = lambda n: small[:, 160 + n % NBUF:161 + n % NBUF]
    precip = lambda n: small[:, 164 + n % NBUF:165 + n % NBUF]
    Ft = small[:, 16:32].rearrange("p (a h) -> p a h", a=2)
    qk_r = small[:, 32:64]
    f_raw, f_abs, f_e, f_l = (small[:, 64 + 16 * n:80 + 16 * n] for n in range(4))
    bn6 = small[:, 128:152].rearrange("p (a b c) -> p a b c", a=2, b=2)
    bn2 = small[:, 152:156].rearrange("p (a b) -> p a b", a=2)
    s_dt, s_adt, s_mag, s_th = (ssm_s[:, n, :] for n in range(4))
    s_ang = ssm_s[:, 4:6, :].rearrange("p c j -> p (c j)")
    mix_tmp = at(7168, 2, T)
    square_junk = at(14336, D)

    def rt_at(off, *dims):
        return at(7424 + off, *dims)

    r_L, r_gd, r_ge = rt_at(0, TH, NR), rt_at(72, TH, NG), rt_at(80, TH, NG)
    r_geq, r_gc, r_goh, r_pen = (rt_at(88 + 8 * n, TH, NG) for n in range(4))
    r_gmax, r_gfirst, r_gs, r_gw, r_m1, r_m2, r_f1, r_f2, r_d21, r_p2, r_rd, r_w1, r_w2 = (
        rt_at(120 + 2 * n, TH) for n in range(13))
    r_EL, r_eq, r_cand, r_oh1, r_oh2, r_t = (rt_at(160 + 64 * n, TH, NE) for n in range(6))
    r_cnt, r_over, r_pos = rt_at(600, NE), rt_at(632, EXTRA, NE), rt_at(728, EXTRA * NE)
    r_list = rt_at(824, 2 * NOVF + 2)
    r_expert = rt_at(848, EXTRA, NE)

    psum = ctx.enter_context(nc.psum_tensor("psum", [P, 8, 512], F32))

    bank_full = [flag(f"bank_full{b}") for b in range(8)]
    bank_free = [flag(f"bank_free{b}") for b in range(8)]
    plan, uses = {}, [0] * 8

    def use(name, bank):
        plan[name] = (bank, uses[bank])
        uses[bank] += 1

    turn = [0]

    def use2(*name):
        use(name, turn[0] % 2)
        turn[0] += 1

    def plan_attention(name, heads):
        for n in range(2 * heads):
            use((name, "score", n), 2 + n % 2)
            use((name, "pt", n), 4 + n % 2)
        for p in range(heads // 2):
            use((name, "pv", p), 6 + p % 2)

    def plan_turn(name):
        for n in range(4):
            use2(name, n)

    plan_turn("hT")
    for n in range(2):
        use2("u", n)
    for q in range(NQ):
        for b in range(2, 6):
            use(("bu", q, b), b)
        use(("y", q), 6 + q % 2)
    for w in "qk":
        for th in range(TH):
            use2(w, th)
    use2("f")
    for th in range(TH):
        use2("v", th)
    use2("gate", 0)
    for w in ("qT", "kT"):
        for th in range(TH):
            use2(w, th)
    use2("F")
    for n in range(1, 2 * NQ):
        use2("gate", n)
    plan_attention("at1", 8)
    use2("glu", 0)
    use2("glu", 1)
    for n in range(4):
        use2("pa", n)
        use2("ps", n)
    plan_turn("memT")
    for n in range(4):
        use2("res1", n)
    use2("memk")
    for th in range(TH):
        use2("memv", th)

    def plan_moe(name):
        plan_turn(name + "xT")
        use2(name + "logits")
        use2(name + "rank")

    plan_moe("e1")
    before_moe = {"e1": list(uses)}
    plan_turn("x2T")
    for n in range(MT):
        use2("conv", n)
    use2("qm2")
    use2("mean")
    use2("var")
    plan_attention("at2", 4)
    for n in range(4):
        use2("res2", n)
    plan_moe("e2")
    before_moe["e2"] = list(uses)
    plan_turn("x3T")
    for n in range(3):
        use2("mq", n)
    for n in range(3):
        use2("mk", n)
    for th in range(TH):
        use2("mv0", th)
    for th in range(TH):
        use2("mv1", th)
    use2("qm3")
    plan_attention("at3", 12)
    plan_attention("at3m", 4)
    for n in range(4):
        use2("res3", n)
    plan_moe("e3")
    before_moe["e3"] = list(uses)

    def open_bank(pe, *name):
        b, m = plan[name]
        if m:
            pe.wait_ge(bank_free[b], m)
        return b

    def close_bank(ins, *name):
        ins.then_inc(bank_full[plan[name][0]], 1)

    def full(eng, *name):
        b, m = plan[name]
        eng.wait_ge(bank_full[b], m + 1)
        return psum[:, b, :]

    def read_out(ins, *name):
        ins.then_inc(bank_free[plan[name][0]], 1)

    def evacuated(eng, *name):
        b, m = plan[name]
        eng.wait_ge(bank_free[b], m + 1)

    last_use = {"u": ("u", 1), "q": ("q", 1), "k": ("k", 1), "v": ("v", 1), "glu": ("glu", 1), "pa": ("pa", 3),
                "ps": ("ps", 3), "wo0": ("res1", 3), "wo1": ("res1", 3), "memkv": ("memv", 1), "c3": ("qm2",),
                "w2o0": ("res2", 3), "w2o1": ("res2", 3), "m0": ("mq", 1), "m1": ("mk", 0), "m2": ("mk", 2),
                "m3": ("mv0", 1), "m4": ("qm3",), "w3o0": ("res3", 3), "w3o1": ("res3", 3)}
    for n in range(4):
        last_use[f"g{n}"] = ("gate", 2 * n + 1)
    for n in range(3):
        last_use[f"c{n}"] = ("conv", 2 * n + 1)
    loaded = [flag(f"loaded{s}") for s in range(2 * NSLOT)]
    used = [flag(f"used{s}") for s in range(2 * NSLOT)]
    loads, moe_uses = [0] * (2 * NSLOT), [0] * (2 * NSLOT)
    holder = [None] * NSLOT
    where, moe_loads, moe_used, moe_after = {}, {}, {}, {}
    for part, (names, width) in enumerate(zip(STREAM, (3, NSLOT, NSLOT))):
        for n, c in enumerate(names):
            s = n % width
            where[c] = (s, loads[2 * s], holder[s] or (moe_uses[2 * s], moe_uses[2 * s + 1]))
            loads[2 * s] += 1
            holder[s] = c
        e = f"e{part + 1}"
        moe_loads[e], moe_used[e], moe_after[e] = list(loads), list(moe_uses), list(holder)
        holder = [None] * NSLOT
        for s in range(2 * NSLOT):
            n = 8 if part == 0 else 16 * (s % 2 == 0)
            loads[s] += n
            moe_uses[s] += n

    def load_chunk(sp, c):
        s, _, prior = where[c]
        if isinstance(prior, str):
            full(sp, *last_use[prior])
        else:
            for half in range(2):
                if prior[half]:
                    sp.wait_ge(used[2 * s + half], prior[half] + SEED)
        sp.dma_start(ring[:, s, :], ins["stream"][CHUNKS.index(c)]).then_inc(loaded[2 * s], 16)

    def chunk(pe, c, inner):
        s, before_, _ = where[c]
        pe.wait_ge(loaded[2 * s], 16 * (before_ + 1))
        return ring[:, s, :].rearrange("p (k n) -> p k n", n=inner)

    def moe_slots(e, u):
        if e == "e1":
            return [(6 * u + w, 1, 0) for w in range(6)]
        return [(2 * w, 2, u) for w in range(6)]

    def moe_view(e, hs):
        return ring[:, hs // 2, (hs % 2) * 2048:(hs % 2) * 2048 + (2 if e == "e1" else 4) * 1024]

    def moe_steps(e):
        return [e + n for n in ("_zero", "_gd", "_sel", "_d21", "_items")]

    milestones = {
        "vec": ["x_ms", "h_tok", "ssm_adt", "ssm_angle", "ssm_powers2", "ssm_state0", "ssm_state1", "qk_ms", "f_abs",
                "qk_tok", "logf"] + [f"ssm_state{n}" for n in range(2, 2 * NQ)] + ["y_ssm", "x1", "x1_ms", "e1_tok"] + moe_steps("e1")
        + ["x2"] + [f"glu_in{n}" for n in range(MT)] + ["conv_done", "conv_sq", "conv_var", "ln21_var", "e2_tok"]
        + moe_steps("e2") + ["ln22_var", "x3", "ln31_var", "e3_tok"] + moe_steps("e3") + ["ln32_var", "x_final"],
        "act": ["x_sq", "x_rms", "ssm_dt", "ssm_mag", "ssm_sin", "qk_rms", "f_ln", "x1_sq", "x1_rms", "e1_ge", "e1_p2"]
        + [f"conv_gate{n}" for n in range(MT)] + ["conv_std", "ln21_std", "e2_ge", "e2_p2", "ln22_std", "ln31_std",
                                                  "e3_ge", "e3_p2", "ln32_std"],
        "pool": ["ident", "masks", "zeros", "powers"]}
    finished = {who: flag(who + "_finished") for who in milestones}
    said = {who: 0 for who in milestones}

    def finish(eng, who, name):
        assert milestones[who][said[who]] == name, (name, milestones[who][said[who]])
        said[who] += 1
        eng.sem_inc(finished[who], 1)

    def after(eng, who, name):
        eng.wait_ge(finished[who], milestones[who].index(name) + 1)

    per_layer = {"S": 2 * (PAIRS + 1), "gathA": PAIRS + 1, "gathB": PAIRS + 1, "xgA": PAIRS + 1, "xgB": PAIRS + 1,
                 "gate": PAIRS, "silu": PAIRS, "up": PAIRS, "h": PAIRS, "T": PAIRS, "hT": PAIRS, "Sw": PAIRS, "SwT": PAIRS,
                 "down": PAIRS, "outA": PAIRS, "outB": PAIRS,
                 "scattered": PAIRS}

    SEED = 1

    def moe_wait(eng, e, name, value):
        eng.wait_ge(flag("moe_" + name), value + ((int(e[1]) - 1) * per_layer[name] + SEED))

    heads_before = {"at1": 0, "at2": 8, "at3": 12, "at3m": 24}

    def attn_wait(eng, name, what, value):
        eng.wait_ge(flag("attn_" + what), value + 2 * heads_before[name])

    OVF_PE, OVF_VEC = 5, 9

    block = ctx.enter_context(nc.Block())
    small_sem = flag("constants_loaded")
    NSMALL = 3

    @block.sync
    def _(sp):
        sp.dma_start(x_sb[:, :, :], ins["x"].rearrange("(h p) d -> p h d", p=P)).then_inc(flag("x_loaded"), 16)
        sp.dma_start(vec[:, :], ins["vec"]).then_inc(small_sem, 16)
        sp.dma_start(wf[:, :, :], ins["wf"]).then_inc(small_sem, 16)
        sp.dma_start(brow[:, :], ins["brow"].partition_broadcast(P)).then_inc(small_sem, 16)
        load_chunk(sp, STREAM[0][0])
        for c_ in range(2):
            sp.dma_start(b_blk[:, c_, :, :], ins["b_blk"][c_]).then_inc(flag("b_loaded"), 16)
        sp.dma_start(wr[:, :, :], ins["wr"][0]).then_inc(flag("router_w"), 16)
        for c in STREAM[0][1:]:
            load_chunk(sp, c)
        for part, e in enumerate(("e1", "e2", "e3")):
            if part == 0:
                full(sp, "y", NQ - 1)
            for c in moe_after[e]:
                if c:
                    full(sp, *last_use[c])
            if part == 1:
                for s in range(NSLOT):
                    sp.wait_ge(used[2 * s + 1], moe_used[e][2 * s + 1] + SEED)
            base = moe_used[e]
            with sp.Fori(0, 8) as i:
                for u in range(2):
                    for w, (hs, per, at_u) in enumerate(moe_slots(e, u)):
                        sp.wait_ge(used[hs], i * per + (base[hs] + at_u + SEED))
                        expert = i * 4 + (2 * u + w % 2)
                        src = ins[e + ("_gate", "_up", "_down")[w // 2]]
                        sp.dma_start(moe_view(e, hs), src[expert, :, :]).then_inc(loaded[hs], 16)
            after(sp, "vec", e + "_items")
            n = sp.value_load(ovf[0:1, 2 * NOVF:2 * NOVF + 1], min_val=0, max_val=NOVF)
            with sp.If(n > 0):
                with sp.Fori(0, n) as k:
                    expert = sp.value_load(ovf[0:1, bass.ds(k + NOVF, 1)], min_val=0, max_val=NE - 1)
                    for w, name in enumerate(("_gate", "_up", "_down")):
                        hs, per, _ = moe_slots(e, 0)[2 * w]
                        sp.wait_ge(used[hs], moe_used[e][hs] + 8 * per + SEED)
                        sp.wait_ge(flag(e + "_ovf_pe"), k * OVF_PE + (0, 2, 2, 4)[w + 1])
                        sp.dma_start(moe_view(e, hs), ins[e + name][expert, :, :]).then_inc(flag(e + f"_ovf_loaded{w}"), 16)
                sp.wait_ge(flag("moe_sum_ready"), int(e[1]))
            if part < 2:
                for c in STREAM[part + 1]:
                    load_chunk(sp, c)
        after(sp, "vec", "x_final")
        sp.dma_start(out.rearrange("(h p) d -> p h d", p=P), x_sb[:, :, :]).then_inc(flag("stored"), 16)
        sp.wait_ge(flag("stored"), 16)

    @block.gpsimd
    def _(po):
        made = flag("pool_made")
        n = [0]

        def step(ins_):
            n[0] += 1
            ins_.then_inc(made, 1)
            po.wait_ge(made, n[0])

        step(po.memset(ident[:, :], 0.0))
        step(po.affine_select(out=ident[:, :], in_=ident[:, :], compare_op=ALU.not_equal, fill=1.0, base=0,
                              pattern=[[-1, P]], channel_multiplier=1))
        finish(po, "pool", "ident")
        step(po.memset(ones[:, :], 1.0))
        step(po.memset(before[:, :], 1.0))
        step(po.affine_select(out=before[:, :], in_=before[:, :], compare_op=ALU.is_gt, fill=0.0, base=0,
                              pattern=[[1, P]], channel_multiplier=-1))
        step(po.memset(upto[:, :, :], 1.0))
        step(po.memset(mask[:, :, :], 0.0))
        for h in range(TH):
            step(po.affine_select(out=upto[:, h, :], in_=upto[:, h, :], compare_op=ALU.is_ge, fill=0.0,
                                  base=-P * h, pattern=[[1, T]], channel_multiplier=-1))
            step(po.affine_select(out=mask[:, h, :], in_=mask[:, h, :], compare_op=ALU.is_ge, fill=MASKED,
                                  base=P * h, pattern=[[-1, T]], channel_multiplier=1))
        step(po.iota(col_id[:, :], pattern=[[1, EXTRA * NE]], base=0, channel_multiplier=0,
                     allow_small_or_imprecise_dtypes=True))
        step(po.memset(rows[:, 0, :], 1.0))
        step(po.affine_select(out=head_sel, in_=head_sel, compare_op=ALU.is_equal, fill=0.0, base=0,
                              pattern=[[-1, 8], [0, P]], channel_multiplier=1))
        step(po.memset(nF[:, :], 0.0))
        finish(po, "pool", "masks")
        step(po.memset(c_blk, 0.0))
        step(po.memset(qz1, 0.0))
        finish(po, "pool", "zeros")
        after(po, "vec", "ssm_powers2")
        pw = powers
        step(po.memset(pw[:, 0, :, 0:1], 1.0))
        step(po.memset(pw[:, 1, :, 0:1], 0.0))
        scratch = at(6144, 2, NJ * HALF_T // 2)
        for k in range(LEVELS):
            Lk = 1 << k
            er = e_pow(k, 0).unsqueeze(2).broadcast_to([P, NJ, Lk])
            ei = e_pow(k, 1).unsqueeze(2).broadcast_to([P, NJ, Lk])
            t1 = scratch[:, 0, 0:NJ * Lk].rearrange("p (j t) -> p j t", j=NJ)
            t2 = scratch[:, 1, 0:NJ * Lk].rearrange("p (j t) -> p j t", j=NJ)
            pr, pi = pw[:, 0, :, 0:Lk], pw[:, 1, :, 0:Lk]
            step(po.tensor_tensor(t1, pr, er, ALU.mult))
            step(po.tensor_tensor(t2, pi, ei, ALU.mult))
            step(po.tensor_tensor(pw[:, 0, :, Lk:2 * Lk], t1, t2, ALU.subtract))
            step(po.tensor_tensor(t1, pr, ei, ALU.mult))
            step(po.tensor_tensor(t2, pi, er, ALU.mult))
            step(po.tensor_tensor(pw[:, 1, :, Lk:2 * Lk], t1, t2, ALU.add))
        finish(po, "pool", "powers")

    @block.tensor
    def _(pe):
        mm = pe.matmul
        for name in per_layer:
            pe.sem_inc(flag("moe_" + name), SEED)
        for s in used:
            pe.sem_inc(s, SEED)
        for e in ("e1", "e2", "e3"):
            pe.sem_inc(flag(e + "_ovf_pe"), OVF_PE)

        def turn_to_T(name, src):
            for n in range(4):
                th, kk = n // 2, n % 2
                b = open_bank(pe, name, n)
                for k in range(4):
                    last = pe.transpose(psum[:, b, k * P:(k + 1) * P], src[:, th, (4 * kk + k) * P:(4 * kk + k + 1) * P], ident[:, :])
                close_bank(last, name, n)

        def wait_T(name):
            for n in range(4):
                evacuated(pe, name, n)

        def to_T(w, cols, name, rhs, done=None, first=0, K=KD):
            b = open_bank(pe, *name)
            for n, c in enumerate(cols):
                for k in range(K):
                    last = mm(psum[:, b, n * T:(n + 1) * T], w[:, k, c * P:(c + 1) * P], rhs[:, k, :],
                              start=(k == 0), stop=(k == K - 1))
            close_bank(last, *name)

        def to_tok(w, c0, c1, name, th, lhs, k0=0, K=KD, start=True, stop=True, close=True):
            b = open_bank(pe, *name) if start else plan[name][0]
            for k in range(K):
                last = mm(psum[:, b, 0:c1 - c0], lhs[:, k0 + k, th * P:(th + 1) * P], w[:, k, c0:c1],
                          start=(start and k == 0), stop=(stop and k == K - 1))
            if close:
                close_bank(last, *name)
            return last

        def attention(name, heads, qz, kT, v, causal, forget=False):
            N = 2 * heads

            def unit(n):
                p, th, j = n // 4, n // 2 % 2, n % 2
                return 2 * p + j, th, (P if causal and th == 0 else T)

            LAG = NBUF - 1
            for n in range(N + LAG + 1):
                if n < N:
                    h, th, W = unit(n)
                    b = open_bank(pe, name, "score", n)
                    last = mm(psum[:, b, 0:W], qz[:, h, th * P:(th + 1) * P], kT(h)[:, 0:W], start=True, stop=not forget)
                    if forget:
                        last = mm(psum[:, b, 0:W], head_sel[:, h, :], nF[:, 0:W], start=False, stop=True)
                    close_bank(last, name, "score", n)
                m = n - LAG
                if 0 <= m < N:
                    h, th, W = unit(m)
                    b = open_bank(pe, name, "pt", m)
                    attn_wait(pe, name, "probs", m + 1)
                    for s in range(W // P):
                        last = pe.transpose(psum[:, b, s * P:(s + 1) * P], P_buf[:, m % NBUF, s * P:(s + 1) * P], ident[:, :])
                    close_bank(last, name, "pt", m)
                m = n - LAG - 1
                if m >= 0:
                    h, th, W = unit(m)
                    p = m // 4
                    evacuated(pe, name, "pt", m)
                    b = open_bank(pe, name, "pv", p) if m % 4 == 0 else plan[(name, "pv", p)][0]
                    for s in range(W // P):
                        last = mm(psum[(h % 2) * HD:(h % 2 + 1) * HD, b, th * P:(th + 1) * P], v(s, h),
                                  PT_buf[:, m % 2, s * P:(s + 1) * P], start=(s == 0), stop=(s == W // P - 1))
                    if m % 4 == 3:
                        close_bank(last, name, "pv", p)

        def residual(name, chunks, lhs):
            w = [chunk(pe, c, D) for c in chunks]
            for n in range(4):
                th, hf = n // 2, n % 2
                to_tok(w[0], hf * 512, hf * 512 + 512, (name, n), th, lhs, 0, 4, True, False, False)
                to_tok(w[1], hf * 512, hf * 512 + 512, (name, n), th, lhs, 4, 4, False, True, True)

        def moe(e, tok):
            F = 2 if e == "e1" else 4
            FW = F * P
            lbase = moe_loads[e]
            turn_to_T(e + "xT", tok)
            wait_T(e + "xT")
            pe.wait_ge(flag("router_w"), 16 * int(e[1]))
            b = open_bank(pe, e + "logits")
            for th in range(TH):
                for k in range(KD):
                    last = mm(psum[:, b, th * NR:(th + 1) * NR], xT[:, k, th * P:(th + 1) * P], wr[:, k, :],
                              start=(k == 0), stop=(k == KD - 1))
            close_bank(last, e + "logits")
            b = open_bank(pe, e + "rank")
            after(pe, "vec", e + "_sel")
            mm(psum[:, b, 0:NE], before[:, :], sel[:, 0, :], start=True, stop=True)
            mm(psum[:, b, NE:2 * NE], ones[:, :], sel[:, 0, :], start=True, stop=False)
            mm(psum[:, b, NE:2 * NE], before[:, :], sel[:, 1, :], start=False, stop=True)
            mm(psum[:, b, 2 * NE:3 * NE], ones[:, :], sel[:, 0, :], start=True, stop=False)
            last = mm(psum[:, b, 2 * NE:3 * NE], ones[:, :], sel[:, 1, :], start=False, stop=True)
            close_bank(last, e + "rank")
            for b in range(8):
                pe.wait_ge(bank_free[b], before_moe[e][b])
            after(pe, "vec", e + "_zero")
            for b in range(4):
                mm(psum[:, b, :], ones[:, :], og[:, 0:512], start=True, stop=False, skip_group_check=True)

            def gather(par, half):
                for k in range(4):
                    for th in range(TH):
                        last = mm(psum[:, (4, 7)[half], k * 2 * CAP:(k + 1) * 2 * CAP], tok[:, th, (4 * half + k) * P:(4 * half + k + 1) * P],
                                  S[:, par, th, :], start=(th == 0), stop=(th == TH - 1))
                last.then_inc(flag(("moe_gathA", "moe_gathB")[half]), 1)

            moe_wait(pe, e, "S", 2)
            gather(0, 0)
            gather(0, 1)

            after(pe, "vec", e + "_items")
            with pe.Fori(0, 8) as i:
                for u in range(2):
                    def c(k, per=1):
                        return i * (2 * per) + (u * per + k)

                    slots = moe_slots(e, u)
                    views = [moe_view(e, s[0]) for s in slots]

                    def arrived(w):
                        hs, per, at_u = slots[w]
                        pe.wait_ge(loaded[hs], i * (16 * per) + 16 * (lbase[hs] + at_u + 1))

                    moe_wait(pe, e, "xgA", c(1))
                    moe_wait(pe, e, "xgB", c(1))
                    for g in range(2):
                        if g == 0:
                            moe_wait(pe, e, "hT", c(0))
                        else:
                            moe_wait(pe, e, "SwT", c(0))
                        arrived(2 * g)
                        arrived(2 * g + 1)
                        wv = [views[2 * g + x].rearrange("p (k n) -> p k n", k=KD) for x in range(2)]
                        for k in range(KD):
                            for x in range(2):
                                last = mm(psum[x * CAP:(x + 1) * CAP, 5 + g, 0:FW], xg[:, u, k, x * CAP:(x + 1) * CAP], wv[x][:, k, :],
                                          start=(k == 0), stop=(k == KD - 1))
                                if k == KD - 1:
                                    last.then_inc(used[slots[2 * g + x][0]], 1)
                    moe_wait(pe, e, "S", c(4, 2))
                    moe_wait(pe, e, "outA", c(0))
                    gather(1 - u, 0)
                    moe_wait(pe, e, "h", c(1))
                    for f in range(F):
                        last = pe.transpose(psum[:, 5, f * P:(f + 1) * P], hh[:, f * P:(f + 1) * P], ident[:, :])
                    last.then_inc(flag("moe_T"), 1)
                    moe_wait(pe, e, "outB", c(0))
                    gather(1 - u, 1)
                    for th in range(TH):
                        last = pe.transpose(psum[:, 6, th * P:(th + 1) * P], Sw[:, u, th, :], ident[:, :])
                    last.then_inc(flag("moe_Sw"), 1)
                    moe_wait(pe, e, "hT", c(1))
                    arrived(4)
                    arrived(5)
                    wv = [views[4 + x].rearrange("p (k n) -> p k n", n=D) for x in range(2)]
                    for half in range(2):
                        moe_wait(pe, e, ("xgA", "xgB")[half], c(2))
                        for f in range(F):
                            for x in range(2):
                                last = mm(psum[x * CAP:(x + 1) * CAP, (4, 7)[half], :], hT[:, f, x * CAP:(x + 1) * CAP],
                                          wv[x][:, f, half * 512:(half + 1) * 512], start=(f == 0), stop=(f == F - 1))
                                if half and f == F - 1:
                                    last.then_inc(used[slots[4 + x][0]], 1)
                        if half == 0:
                            last.then_inc(flag("moe_down"), 1)
                    moe_wait(pe, e, "SwT", c(1))
                    moe_wait(pe, e, "outA", c(1))
                    for half in range(2):
                        if half:
                            moe_wait(pe, e, "outB", c(1))
                        for th in range(TH):
                            last = mm(psum[:, 2 * th + half, :], SwT[:, th * P:(th + 1) * P], og[:, half * 512:(half + 1) * 512],
                                      start=False, stop=False, skip_group_check=True)
                    last.then_inc(flag("moe_scattered"), 1)
            moe_wait(pe, e, "xgA", PAIRS + 1)
            moe_wait(pe, e, "xgB", PAIRS + 1)

            ovp, ovv = flag(e + "_ovf_pe"), flag(e + "_ovf_vec")
            n = pe.value_load(ovf[0:1, 2 * NOVF:2 * NOVF + 1], min_val=0, max_val=NOVF)
            with pe.If(n > 0):
                with pe.Fori(0, n) as k_:
                    pe.wait_ge(ovv, k_ * OVF_VEC + 2)
                    for half, b in enumerate((4, 7)):
                        for k in range(4):
                            for th in range(TH):
                                mm(psum[:, b, k * CAP:(k + 1) * CAP], tok[:, th, (4 * half + k) * P:(4 * half + k + 1) * P],
                                   S[:, 0, th, 0:CAP], start=(th == 0), stop=(th == TH - 1))
                    for th in range(TH):
                        last = pe.transpose(psum[0:CAP, 6, th * P:(th + 1) * P], Sw[:, 0, th, 0:CAP], ident[:, :])
                    last.then_inc(ovp, 1)
                    pe.wait_ge(ovv, k_ * OVF_VEC + 5)
                    for g in range(2):
                        pe.wait_ge(flag(e + f"_ovf_loaded{g}"), k_ * 16 + 16)
                        wv = moe_view(e, moe_slots(e, 0)[2 * g][0]).rearrange("p (k n) -> p k n", k=KD)
                        for k in range(KD):
                            last = mm(psum[0:CAP, 5 + g, 0:FW], xg[:, 0, k, 0:CAP], wv[:, k, :], start=(k == 0), stop=(k == KD - 1))
                    last.then_inc(ovp, 1)
                    pe.wait_ge(ovv, k_ * OVF_VEC + 6)
                    for f in range(F):
                        last = pe.transpose(psum[:, 5, f * P:(f + 1) * P], hh[:, f * P:(f + 1) * P], ident[:, :])
                    last.then_inc(ovp, 1)
                    pe.wait_ge(ovv, k_ * OVF_VEC + 7)
                    pe.wait_ge(flag(e + "_ovf_loaded2"), k_ * 16 + 16)
                    wv = moe_view(e, moe_slots(e, 0)[4][0]).rearrange("p (k n) -> p k n", n=D)
                    for half, b in enumerate((4, 7)):
                        for f in range(F):
                            last = mm(psum[0:CAP, b, :], hT[:, f, 0:CAP], wv[:, f, half * 512:(half + 1) * 512],
                                      start=(f == 0), stop=(f == F - 1))
                    last.then_inc(ovp, 1)
                    pe.wait_ge(ovv, k_ * OVF_VEC + 9)
                    for half in range(2):
                        for th in range(TH):
                            last = mm(psum[:, 2 * th + half, :], SwT[0:CAP, th * P:(th + 1) * P], og[0:CAP, half * 512:(half + 1) * 512],
                                      start=False, stop=False, skip_group_check=True)
                    last.then_inc(ovp, 1)
                    pe.wait_ge(ovp, k_ * OVF_PE + 2 * OVF_PE)
            moe_wait(pe, e, "scattered", PAIRS)
            pe.sem_inc(flag("moe_sum_ready"), 1)

        after(pe, "pool", "ident")
        after(pe, "vec", "h_tok")
        turn_to_T("hT", h_tok)
        wait_T("hT")
        w = chunk(pe, "u", 512)
        to_T(w, (0, 1), ("u", 0), xT)
        to_T(w, (2, 3), ("u", 1), xT)

        def ssm_in(q):
            for c_ in range(2):
                for hb in range(2):
                    bank = 2 + 2 * c_ + hb
                    open_bank(pe, "bu", q, bank)
                    for jj in (2 * hb, 2 * hb + 1):
                        last = mm(psum[:, bank, (jj % 2) * T:(jj % 2 + 1) * T], b_blk[:, c_, 4 * q + jj, :], uT[:, q, :],
                                  start=True, stop=True)
                    close_bank(last, "bu", q, bank)

        def ssm_out(q):
            b = open_bank(pe, "y", q)
            for half in range(2):
                after(pe, "vec", f"ssm_state{2 * q + half}")
                for jj in range(4):
                    for c_ in range(2):
                        last = mm(psum[:, b, half * HALF_T:(half + 1) * HALF_T], c_blk[:, c_, 4 * q + jj, :], ws[:, half, c_, jj, :],
                                  start=(jj == 0 and c_ == 0), stop=(jj == 3 and c_ == 1))
                last.then_inc(flag("ssm_y"), 1)
            pe.wait_ge(flag("ssm_y"), 2 * q + 2)
            pe.sem_inc(bank_full[b], 1)

        def gate(n):
            w = chunk(pe, f"g{n // 2}", 512)
            to_T(w, (2 * (n % 2), 2 * (n % 2) + 1), ("gate", n), xT)

        def project(name):
            w = chunk(pe, name, 512)
            for th in range(TH):
                to_tok(w, 0, 512, (name, th), th, xT)

        pe.wait_ge(flag("b_loaded"), 32)
        evacuated(pe, "u", 0)
        ssm_in(0)
        evacuated(pe, "u", 1)
        project("q")
        project("k")
        ssm_in(1)
        pe.wait_ge(small_sem, 16 * NSMALL)
        b = open_bank(pe, "f")
        for th in range(TH):
            for k in range(KD):
                last = mm(psum[:, b, th * 8:(th + 1) * 8], xT[:, k, th * P:(th + 1) * P], wf[:, k, :],
                          start=(k == 0), stop=(k == KD - 1))
        close_bank(last, "f")
        project("v")
        ssm_out(0)
        gate(0)
        ssm_in(2)
        for w_, c0 in (("qT", 0), ("kT", 512)):
            after(pe, "vec", "qk_tok")
            for th in range(TH):
                b = open_bank(pe, w_, th)
                for k in range(4):
                    last = pe.transpose(psum[:, b, k * P:(k + 1) * P], qk_tok[:, th, c0 + k * P:c0 + (k + 1) * P], ident[:, :])
                close_bank(last, w_, th)
        after(pe, "pool", "masks")
        after(pe, "vec", "logf")
        b = open_bank(pe, "F")
        mm(psum[:, b, 0:8], upto[:, 0, 0:P], lf[:, 0, 0, :], start=True, stop=True)
        mm(psum[:, b, 8:16], upto[:, 0, P:T], lf[:, 0, 0, :], start=True, stop=False)
        mm(psum[:, b, 8:16], upto[:, 1, P:T], lf[:, 0, 1, :], start=False, stop=True)
        mm(psum[0:8, b, 128:128 + T], lf[:, 1, 0, :], upto[:, 0, :], start=True, stop=False)
        last = mm(psum[0:8, b, 128:128 + T], lf[:, 1, 1, :], upto[:, 1, :], start=False, stop=True)
        close_bank(last, "F")
        gate(1)
        gate(2)
        ssm_out(1)
        ssm_in(3)
        gate(3)
        gate(4)
        ssm_out(2)
        gate(5)
        gate(6)
        gate(7)
        ssm_out(3)
        for name in ("qT", "kT"):
            for th in range(TH):
                evacuated(pe, name, th)
        evacuated(pe, "F")
        evacuated(pe, "v", 0)
        evacuated(pe, "v", 1)
        attention("at1", 8, qz1, lambda h: kT1[:, h // 2, :], lambda s, h: v_tok[:, s, h * HD:(h + 1) * HD], True, True)
        w = chunk(pe, "glu", 512)
        pe.wait_ge(flag("gelu"), NQ)
        to_T(w, (0, 1), ("glu", 0), yg, K=4)
        to_T(w, (2, 3), ("glu", 1), yg, K=4)
        for p in range(4):
            evacuated(pe, "at1", "pv", p)
        wa, ws_ = chunk(pe, "pa", D), chunk(pe, "ps", D)
        for n in range(4):
            to_T(wa, (2 * n, 2 * n + 1), ("pa", n), ya, K=4)
            if n == 0:
                after(pe, "vec", "y_ssm")
            to_T(ws_, (2 * n, 2 * n + 1), ("ps", n), y_ssm, K=4)
        pe.wait_ge(flag("mem_loaded"), 16)
        turn_to_T("memT", mem_tok)
        pe.wait_ge(flag("mixed"), 4)
        residual("res1", ("wo0", "wo1"), mixedT)
        wait_T("memT")
        w = chunk(pe, "memkv", 512)
        to_T(w, (0, 1), ("memk",), memT)
        for th in range(TH):
            to_tok(w, 256, 512, ("memv", th), th, memT)
        after(pe, "vec", "e1_tok")
        moe("e1", xh)

        after(pe, "vec", "x2")
        turn_to_T("x2T", x_sb)
        wait_T("x2T")
        for n in range(MT):
            if n % 2 == 0:
                w = chunk(pe, f"c{n // 2}", 512)
            to_T(w, (2 * (n % 2), 2 * (n % 2) + 1), ("conv", n), xT)
        w = chunk(pe, "c3", 512)
        to_T(w, (0, 1), ("qm2",), xT)
        evacuated(pe, "qm2")
        evacuated(pe, "memk")
        evacuated(pe, "memv", 0)
        evacuated(pe, "memv", 1)

        def channel_sums(name, src):
            b = open_bank(pe, name)
            for k in range(MT):
                last = mm(psum[:, b, 0:T], ones[:, :], src[:, k, :], start=(k == 0), stop=(k == MT - 1))
            close_bank(last, name)

        after(pe, "vec", "conv_done")
        channel_sums("mean", conv)
        after(pe, "vec", "conv_sq")
        channel_sums("var", sq)
        attention("at2", 4, qz2, lambda h: mem_k[:, h // 2, :], lambda s, h: mem_v[:, s, h * HD:(h + 1) * HD], False)
        for p in range(2):
            evacuated(pe, "at2", "pv", p)
        pe.wait_ge(flag("conv_out"), MT)
        residual("res2", ("w2o0", "w2o1"), yT)
        after(pe, "vec", "e2_tok")
        moe("e2", x_sb)

        after(pe, "vec", "x3")
        turn_to_T("x3T", x_sb)
        wait_T("x3T")
        w = chunk(pe, "m0", 512)
        to_T(w, (0, 1), ("mq", 0), xT)
        to_T(w, (2, 3), ("mq", 1), xT)
        w = chunk(pe, "m1", 512)
        to_T(w, (0, 1), ("mq", 2), xT)
        to_T(w, (2, 3), ("mk", 0), xT)
        w = chunk(pe, "m2", 512)
        to_T(w, (0, 1), ("mk", 1), xT)
        to_T(w, (2, 3), ("mk", 2), xT)
        w = chunk(pe, "m3", 512)
        for th in range(TH):
            to_tok(w, 0, 512, ("mv0", th), th, xT)
        w = chunk(pe, "m4", 512)
        for th in range(TH):
            to_tok(w, 0, 256, ("mv1", th), th, xT)
        to_T(w, (2, 3), ("qm3",), xT)
        for n in range(3):
            evacuated(pe, "mq", n)
            evacuated(pe, "mk", n)
        for th in range(TH):
            evacuated(pe, "mv0", th)
            evacuated(pe, "mv1", th)
        evacuated(pe, "qm3")
        attention("at3", 12, qz3, lambda h: kT3[:, h // 2, :], lambda s, h: v3[:, s, h * HD:(h + 1) * HD], True)
        attention("at3m", 4, qz3m, lambda h: mem_k[:, h // 2, :], lambda s, h: mem_v[:, s, h * HD:(h + 1) * HD], False)
        for p in range(6):
            evacuated(pe, "at3", "pv", p)
        for p in range(2):
            evacuated(pe, "at3m", "pv", p)
        residual("res3", ("w3o0", "w3o1"), yT)
        after(pe, "vec", "e3_tok")
        moe("e3", x_sb)

    @block.scalar
    def _(ac):
        act = ac.activation
        chain = flag("act_chain")
        n_chain = [0]

        def step(ins_):
            n_chain[0] += 1
            ins_.then_inc(chain, 1)
            ac.wait_ge(chain, n_chain[0])

        def copy_out(name, dst, src):
            read_out(act(dst, src, ACT.Copy), *name)

        def attention(name, heads, out_T):
            N = 2 * heads

            def width(n):
                return P if name in ("at1", "at3") and n // 2 % 2 == 0 else T

            LAG = NBUF - 1
            for n in range(N + LAG + 1):
                if n < N:
                    W = width(n)
                    attn_wait(ac, name, "logits", n + 1)
                    act(P_buf[:, n % NBUF, 0:W], P_buf[:, n % NBUF, 0:W], ACT.Exp, bias=nmax(n), accum_out=psums(n)).then_inc(flag("attn_exp"), 1)
                m = n - LAG
                if 0 <= m < N:
                    W = width(m)
                    src = full(ac, name, "pt", m)
                    copy_out((name, "pt", m), PT_buf[:, m % 2, 0:W], src[:, 0:W])
                m = n - LAG - 1
                if m >= 0 and m % 4 == 3:
                    p = m // 4
                    src = full(ac, name, "pv", p)
                    copy_out((name, "pv", p), out_T[:, p, :], src[:, 0:T])

        def moe(e):
            F = 2 if e == "e1" else 4
            FW = F * P

            def gathered(par):
                act(xg[:, par, 0:4, :], psum[:, 4, :].rearrange("p (k c) -> p k c", k=4), ACT.Copy).then_inc(flag("moe_xgA"), 1)

            after(ac, "vec", e + "_gd")
            step(act(r_ge, r_gd, ACT.Exp))
            finish(ac, "act", e + "_ge")
            after(ac, "vec", e + "_d21")
            step(act(r_p2, r_d21, ACT.Exp))
            finish(ac, "act", e + "_p2")
            if e != "e3":
                ac.dma_start(wr[:, :, :], ins["wr"][int(e[1])]).then_inc(flag("router_w"), 16)

            moe_wait(ac, e, "gathA", 1)
            gathered(0)
            after(ac, "vec", e + "_items")
            with ac.Fori(0, 8) as i:
                for u in range(2):
                    def c(k, per=1):
                        return i * (2 * per) + (u * per + k)

                    hs, per, at_u = moe_slots(e, u)[1]
                    ac.wait_ge(used[hs], i * per + (moe_used[e][hs] + at_u + 1 + SEED))
                    act(sg[:, 0:FW], psum[:, 5, 0:FW], ACT.Silu).then_inc(flag("moe_silu"), 1)
                    moe_wait(ac, e, "gathA", c(2))
                    gathered(1 - u)
                    moe_wait(ac, e, "T", c(1))
                    act(hT[:, 0:F, :], psum[:, 5, 0:FW].rearrange("p (f c) -> p f c", f=F), ACT.Copy).then_inc(flag("moe_hT"), 1)
                    moe_wait(ac, e, "down", c(1))
                    act(og[:, 0:512], psum[:, 4, :], ACT.Copy).then_inc(flag("moe_outA"), 1)
            n = ac.value_load(ovf[0:1, 2 * NOVF:2 * NOVF + 1], min_val=0, max_val=NOVF)
            with ac.If(n > 0):
                with ac.Fori(0, n) as k_:
                    ac.wait_ge(flag(e + "_ovf_pe"), k_ * OVF_PE + (OVF_PE + 2))
                    act(sg[0:CAP, 0:FW], psum[0:CAP, 5, 0:FW], ACT.Silu).then_inc(flag(e + "_ovf_silu"), 1)

        def rms_norm(squares, got, ready):
            for th in range(TH):
                step(act(squares, x_sb[:, th, :], ACT.Square, accum_out=rms_ms[:, th:th + 1]))
            finish(ac, "act", got + "_sq")
            after(ac, "vec", got + "_ms")
            step(act(rms_r, rms_r, ACT.Sqrt))
            finish(ac, "act", got + "_rms")

        ac.wait_ge(flag("x_loaded"), 16)
        rms_norm(square_junk, "x", None)
        ac.wait_ge(small_sem, 16 * NSMALL)
        step(act(s_dt, V("log_dt"), ACT.Exp))
        finish(ac, "act", "ssm_dt")
        after(ac, "vec", "ssm_adt")
        step(act(s_mag, s_adt, ACT.Exp))
        finish(ac, "act", "ssm_mag")
        after(ac, "vec", "ssm_angle")
        step(act(e_tab[:, 0, :, :].rearrange("p c j -> p (c j)"), s_ang, ACT.Sin))
        finish(ac, "act", "ssm_sin")

        for n in range(2):
            src = full(ac, "u", n)
            copy_out(("u", n), uT[:, 2 * n:2 * n + 2, :], src.rearrange("p (a t) -> p a t", a=2))
        after(ac, "vec", "qk_ms")
        step(act(qk_r, qk_r, ACT.Sqrt))
        finish(ac, "act", "qk_rms")
        after(ac, "vec", "f_abs")
        step(act(f_e, f_abs, ACT.Exp, scale=-1.0))
        step(act(f_l, f_e, ACT.Ln, bias=1.0))
        finish(ac, "act", "f_ln")
        for th in range(TH):
            src = full(ac, "v", th)
            copy_out(("v", th), v_tok[:, th, :], src)
        for n in range(2 * NQ):
            src = full(ac, "gate", n)
            read_out(act(gates[:, 2 * n:2 * n + 2, :], src.rearrange("p (a t) -> p a t", a=2), ACT.Sigmoid), "gate", n)
        for q in range(NQ):
            evacuated(ac, "y", q)
            act(yg[:, q, :], yg[:, q, :], ACT.Gelu_apprx_tanh).then_inc(flag("gelu"), 1)
        attention("at1", 8, ya)
        ac.dma_start(gain, ins["rows"][0:1, :].partition_broadcast(P)).then_inc(flag("gain_loaded"), 16)
        for n in range(2):
            src = full(ac, "glu", n)
            read_out(act(y_ssm[:, 2 * n:2 * n + 2, :], src.rearrange("p (a t) -> p a t", a=2), ACT.Sigmoid), "glu", n)
        ac.dma_start(mem_tok, ins["mem"].rearrange("(h p) d -> p h d", p=P)).then_inc(flag("mem_loaded"), 16)
        after(ac, "vec", "x1")
        rms_norm(junk, "x1", None)
        src = full(ac, "memk")
        copy_out(("memk",), mem_k[:, :, :], src.rearrange("p (a t) -> p a t", a=2))
        for th in range(TH):
            src = full(ac, "memv", th)
            copy_out(("memv", th), mem_v[:, th, :], src[:, 0:256])
        moe("e1")

        for n in range(MT):
            full(ac, "conv", n)
            if n >= 2:
                after(ac, "vec", f"glu_in{n - 2}")
            step(act(gatez[:, n % 2, :], psum[:, plan[("conv", n)][0], T:2 * T], ACT.Sigmoid))
            finish(ac, "act", f"conv_gate{n}")
        after(ac, "vec", "conv_var")
        step(act(stat[:, 1, :], stat[:, 1, :], ACT.Sqrt))
        finish(ac, "act", "conv_std")
        for n in range(MT):
            ac.wait_ge(flag("conv_norm"), n + 1)
            act(yT[:, n, :], conv[:, n, :], ACT.Silu, bias=V("ln_b")[:, n:n + 1], scale=V("ln_g")[:, n:n + 1]).then_inc(flag("conv_out"), 1)
        attention("at2", 4, yT[:, MT:KD, :])

        def layer_norm(name):
            after(ac, "vec", name + "_var")
            step(act(ln_r, ln_r, ACT.Sqrt))
            finish(ac, "act", name + "_std")

        def load_rows(a):
            for r in range(2):
                ac.dma_start(rows[:, r, :], ins["rows"][a + r:a + r + 1, :].partition_broadcast(P)).then_inc(flag(f"rows{a}"), 16)

        load_rows(1)
        layer_norm("ln21")
        after(ac, "vec", "e2_tok")
        load_rows(3)
        moe("e2")
        layer_norm("ln22")

        for n in range(3):
            src = full(ac, "mk", n)
            copy_out(("mk", n), kT3[:, 2 * n:2 * n + 2, :], src.rearrange("p (a t) -> p a t", a=2))
        for th in range(TH):
            src = full(ac, "mv0", th)
            copy_out(("mv0", th), v3[:, th, 0:512], src)
        for th in range(TH):
            src = full(ac, "mv1", th)
            copy_out(("mv1", th), v3[:, th, 512:768], src[:, 0:256])
        attention("at3", 12, yT[:, 0:MT, :])
        attention("at3m", 4, yT[:, MT:KD, :])
        load_rows(5)
        layer_norm("ln31")
        after(ac, "vec", "e3_tok")
        load_rows(7)
        moe("e3")
        layer_norm("ln32")

    @block.vector
    def _(ve):
        chain = flag("vec_chain")
        n_chain = [0]
        tt, ts, stt = ve.tensor_tensor, ve.tensor_scalar, ve.scalar_tensor_tensor

        def step(ins_):
            n_chain[0] += 1
            ins_.then_inc(chain, 1)
            ve.wait_ge(chain, n_chain[0])

        def counted(ins_):
            n_chain[0] += 1
            ins_.then_inc(chain, 1)
            return n_chain[0]

        def tell(name):
            finish(ve, "vec", name)

        def over(a, *shape):
            while len(a.shape) < len(shape):
                a = a.unsqueeze(len(a.shape))
            return a.broadcast_to(list(shape))

        def rows_over(a, n):
            return a.unsqueeze(1).broadcast_to([P, n, a.shape[1]])

        def take_T(name, scale=None):
            for n in range(4):
                th, kk = n // 2, n % 2
                src = full(ve, name, n).rearrange("p (k t) -> p k t", k=4)
                dst = (memT if name == "memT" else xT)[:, 4 * kk:4 * kk + 4, th * P:(th + 1) * P]
                if scale is None:
                    read_out(ve.tensor_copy(dst, src), name, n)
                else:
                    read_out(tt(dst, src, over(scale[:, 4 * kk:4 * kk + 4], P, 4, P), ALU.mult), name, n)

        def split_heads(name, dst, src, j0, s1, s2=None):
            nt = src.shape[1]
            d = dst.rearrange("p (j o) t -> p j o t", o=2)
            for o in range(2):
                r = slice(o * HD, (o + 1) * HD)
                sc = s1[r] if s1 is not None else 1.0
                last = ts(d[r, j0:j0 + nt, o, :], src[r], sc, s2 if s2 is not None else 1.0, ALU.mult, ALU.mult)
                if o == 0:
                    step(last)
            read_out(last, *name)

        def attention(name, heads, op, scalar, causal):
            N = 2 * heads

            def unit(n):
                p, th, j = n // 4, n // 2 % 2, n % 2
                return 2 * p + j, th, (P if causal and th == 0 else T)

            for n in range(N + 1):
                if n < N:
                    h, th, W = unit(n)
                    src = full(ve, name, "score", n)[:, 0:W]
                    if n >= NBUF:
                        full(ve, name, "pt", n - NBUF)
                    dst = P_buf[:, n % NBUF, 0:W]
                    if causal:
                        ins_ = stt(out=dst, in0=src, scalar=scalar(h, th), in1=mask[:, th, 0:W], op0=op, op1=ALU.add)
                    else:
                        ins_ = ts(dst, src, scalar(h, th), None, op)
                    read_out(ins_, name, "score", n)
                    evacuated(ve, name, "score", n)
                    ve.tensor_reduce(nmax(n), dst, AX.X, ALU.max, negate=True).then_inc(flag("attn_logits"), 1)
                if n >= 1:
                    m = n - 1
                    h, th, W = unit(m)
                    attn_wait(ve, name, "exp", m + 1)
                    step(ve.reciprocal(precip(m), psums(m)))
                    ts(P_buf[:, m % NBUF, 0:W], P_buf[:, m % NBUF, 0:W], precip(m), None, ALU.mult).then_inc(flag("attn_probs"), 1)

        def residual(name, alpha):
            for n in range(4):
                th, hf = n // 2, n % 2
                src = full(ve, name, n)
                dst = x_sb[:, th, hf * 512:(hf + 1) * 512]
                read_out(stt(out=dst, in0=dst, scalar=alpha, in1=src, op0=ALU.mult, op1=ALU.add), name, n)
            for n in range(4):
                evacuated(ve, name, n)

        def moe_sum(e, alpha):
            ve.wait_ge(flag("moe_sum_ready"), int(e[1]))
            for n in range(4):
                th, hf = n // 2, n % 2
                dst = x_sb[:, th, hf * 512:(hf + 1) * 512]
                step(stt(out=dst, in0=dst, scalar=alpha, in1=psum[:, n, :], op0=ALU.mult, op1=ALU.add))

        def layer_norm(name, a):
            for th in range(TH):
                for hf in range(2):
                    step(ve.bn_stats(bn6[:, th, hf, :], x_sb[:, th, hf * 512:(hf + 1) * 512]))
                step(ve.bn_aggr(bn2[:, th, :], bn6[:, th, :, :]))
            step(ts(ln_r, bn2[:, :, 1], 1e-5, None, ALU.add))
            tell(name + "_var")
            after(ve, "act", name + "_std")
            step(ve.reciprocal(ln_r, ln_r))
            for th in range(TH):
                step(ts(x_sb[:, th, :], x_sb[:, th, :], bn2[:, th, 0:1], ln_r[:, th:th + 1], ALU.subtract, ALU.mult))
            ve.wait_ge(flag(f"rows{a}"), 32)
            step(tt(x_sb[:, :, :], x_sb[:, :, :], rows_over(rows[:, 0, :], TH), ALU.mult))
            step(tt(x_sb[:, :, :], x_sb[:, :, :], rows_over(rows[:, 1, :], TH), ALU.add))

        def rms_norm(name, dst):
            after(ve, "act", name + "_sq")
            step(ts(rms_r, rms_ms, 1.0 / D, 1e-6, ALU.mult, ALU.add))
            tell(name + "_ms")
            after(ve, "act", name + "_rms")
            step(ve.reciprocal(rms_r, rms_r))
            for th in range(TH):
                step(ts(dst[:, th, :], x_sb[:, th, :], rms_r[:, th:th + 1], None, ALU.mult))

        def moe(e):
            F = 2 if e == "e1" else 4
            FW = F * P
            n_e = int(e[1]) - 1
            take_T(e + "xT")
            step(ve.memset(og[:, 0:512], 0.0))
            tell(e + "_zero")
            src = full(ve, e + "logits")[:, 0:TH * NR].rearrange("p (h n) -> p h n", h=TH)
            read_out(tt(r_L, src, rows_over(brow[:, 8 + n_e * NR:8 + (n_e + 1) * NR], TH), ALU.add), e + "logits")
            evacuated(ve, e + "logits")
            step(ve.tensor_reduce(r_gmax, r_L[:, :, 0:NG], AX.X, ALU.max))
            step(tt(r_gd, r_L[:, :, 0:NG], over(r_gmax, P, TH, NG), ALU.subtract))
            tell(e + "_gd")

            def first_max(x, top, eq, cand, first, onehot, n):
                step(tt(eq, x, over(top, P, TH, n), ALU.is_equal))
                step(stt(out=cand, in0=eq, scalar=-100.0, in1=rows_over(col_id[:, 0:n], TH), op0=ALU.mult, op1=ALU.add))
                step(ve.tensor_reduce(first, cand, AX.X, ALU.min))
                step(tt(onehot, cand, over(first, P, TH, n), ALU.is_equal))

            first_max(r_L[:, :, 0:NG], r_gmax, r_geq, r_gc, r_gfirst, r_goh, NG)
            step(ts(r_pen, r_goh, -1.0, 1e30, ALU.add, ALU.mult))
            step(tt(r_EL.rearrange("p h (g x) -> p h g x", g=NG), r_L[:, :, NG:NR].rearrange("p h (g x) -> p h g x", g=NG),
                    over(r_pen, P, TH, NG, EPG), ALU.add))
            step(ve.tensor_reduce(r_m1, r_EL, AX.X, ALU.max))
            first_max(r_EL, r_m1, r_eq, r_cand, r_f1, r_oh1, NE)
            step(stt(out=r_EL, in0=r_oh1, scalar=-3e38, in1=r_EL, op0=ALU.mult, op1=ALU.add))
            step(ve.tensor_reduce(r_m2, r_EL, AX.X, ALU.max))
            first_max(r_EL, r_m2, r_eq, r_cand, r_f2, r_oh2, NE)
            step(tt(sel, r_oh1, r_oh2, ALU.add))
            tell(e + "_sel")
            step(tt(r_d21, r_m2, r_m1, ALU.subtract))
            tell(e + "_d21")
            after(ve, "act", e + "_ge")
            step(ve.tensor_reduce(r_gs, r_ge, AX.X, ALU.add))
            step(ve.reciprocal(r_gw, r_gs))
            after(ve, "act", e + "_p2")
            step(ts(r_rd, r_p2, 1.0, None, ALU.add))
            step(ve.reciprocal(r_rd, r_rd))
            step(tt(r_w1, r_gw, r_rd, ALU.mult))
            step(tt(r_w2, r_w1, r_p2, ALU.mult))
            step(ve.memset(wcomb, 0.0))
            step(ve.memset(rank, -1.0))
            step(tt(r_t, r_oh1, over(r_w1, P, TH, NE), ALU.mult))
            step(tt(r_cand, r_oh2, over(r_w2, P, TH, NE), ALU.mult))
            step(tt(wcomb[:, :, 0:NE], r_t, r_cand, ALU.add))
            src = full(ve, e + "rank")
            step(stt(out=r_t, in0=src[:, 0:2 * NE].rearrange("p (h n) -> p h n", h=TH), scalar=1.0, in1=sel, op0=ALU.add, op1=ALU.mult))
            step(ts(rank[:, :, 0:NE], r_t, -1.0, None, ALU.add))
            read_out(ve.tensor_copy(r_cnt, src[:, 2 * NE:3 * NE]), e + "rank")

            def one_hot(par, j):
                s4 = S[:, par, :, :].rearrange("p h (x c) -> p h x c", x=2)
                sw4 = Sw[:, par, :, :].rearrange("p h (x c) -> p h x c", x=2)
                ids = col_id[:, 0:CAP].unsqueeze(1).unsqueeze(1).broadcast_to([P, TH, 2, CAP])
                tt(s4, ids, over(rank[:, :, bass.ds(j * 2, 2)], P, TH, 2, CAP), ALU.is_equal).then_inc(flag("moe_S"), 1)
                moe_wait(ve, e, "S", j * 2 + 1)
                tt(sw4, s4, over(wcomb[:, :, bass.ds(j * 2, 2)], P, TH, 2, CAP), ALU.mult).then_inc(flag("moe_S"), 1)

            def gathered(par):
                ve.tensor_copy(xg[:, par, 4:8, :], psum[:, 7, :].rearrange("p (k c) -> p k c", k=4)).then_inc(flag("moe_xgB"), 1)

            one_hot(0, 0)
            moe_wait(ve, e, "gathB", 1)
            gathered(0)
            evacuated(ve, e + "rank")
            for p in range(EXTRA):
                step(ts(r_over[:, p, :], r_cnt, float((p + 1) * CAP), None, ALU.is_gt))
                step(ve.tensor_copy(r_expert[:, p, :], col_id[:, 0:NE]))
                step(ts(rank3[:, :, p, :], rank[:, :, 0:NE], -float((p + 1) * CAP), None, ALU.add))
                step(ve.tensor_copy(wcomb3[:, :, p, :], wcomb[:, :, 0:NE]))
            over_flat = r_over.rearrange("p a b -> p (a b)")
            expert_flat = r_expert.rearrange("p a b -> p (a b)")
            step(ve.tensor_tensor_scan(r_pos, ones[:, 0:EXTRA * NE], over_flat, 0.0, ALU.mult, ALU.add))
            step(ve.tensor_copy(r_list[:, 2 * NOVF:2 * NOVF + 1], r_pos[:, EXTRA * NE - 1:EXTRA * NE]))
            step(tt(r_pos, r_pos, over_flat, ALU.mult))
            step(tt(item_eq, rows_over(r_pos, NOVF), over(col_id[:, 1:1 + NOVF], P, NOVF, EXTRA * NE), ALU.is_equal))
            step(tt(item_t, item_eq, rows_over(col_id[:, :], NOVF), ALU.mult))
            step(ve.tensor_reduce(r_list[:, 0:NOVF], item_t, AX.X, ALU.add))
            step(tt(item_t, item_eq, rows_over(expert_flat, NOVF), ALU.mult))
            step(ve.tensor_reduce(r_list[:, NOVF:2 * NOVF], item_t, AX.X, ALU.add))
            step(ve.tensor_copy(ovf[:, 0:2 * NOVF + 1], r_list[:, 0:2 * NOVF + 1]))
            tell(e + "_items")
            with ve.Fori(0, 8) as i:
                for u in range(2):
                    def c(k, per=1):
                        return i * (2 * per) + (u * per + k)

                    one_hot(1 - u, c(1))
                    hs, per, at_u = moe_slots(e, u)[3]
                    ve.wait_ge(used[hs], i * per + (moe_used[e][hs] + at_u + 1 + SEED))
                    moe_wait(ve, e, "silu", c(1))
                    tt(hh[:, 0:FW], sg[:, 0:FW], psum[:, 6, 0:FW], ALU.mult).then_inc(flag("moe_h"), 1)
                    moe_wait(ve, e, "gathB", c(2))
                    gathered(1 - u)
                    moe_wait(ve, e, "Sw", c(1))
                    ve.tensor_copy(SwT[:, :], psum[:, 6, 0:T]).then_inc(flag("moe_SwT"), 1)
                    hs, per, at_u = moe_slots(e, u)[5]
                    ve.wait_ge(used[hs], i * per + (moe_used[e][hs] + at_u + 1 + SEED))
                    ve.tensor_copy(og[:, 512:1024], psum[:, 7, :]).then_inc(flag("moe_outB"), 1)
            ovp, ovv = flag(e + "_ovf_pe"), flag(e + "_ovf_vec")
            n = ve.value_load(ovf[0:1, 2 * NOVF:2 * NOVF + 1], min_val=0, max_val=NOVF)
            with ve.If(n > 0):
                moe_wait(ve, e, "scattered", PAIRS)
                with ve.Fori(0, n) as k_:
                    item = ve.value_load(ovf[0:1, bass.ds(k_, 1)], min_val=0, max_val=EXTRA * NE - 1)
                    ve.wait_ge(ovp, k_ * OVF_PE + OVF_PE)
                    s3, sw3 = S[:, 0, :, 0:CAP], Sw[:, 0, :, 0:CAP]
                    rank_flat, w_flat = (a.rearrange("p h a b -> p h (a b)")[:, :, bass.ds(item, 1)].broadcast_to([P, TH, CAP])
                                         for a in (rank3, wcomb3))
                    tt(s3, rows_over(col_id[:, 0:CAP], TH), rank_flat, ALU.is_equal).then_inc(ovv, 1)
                    ve.wait_ge(ovv, k_ * OVF_VEC + 1)
                    tt(sw3, s3, w_flat, ALU.mult).then_inc(ovv, 1)
                    ve.wait_ge(ovp, k_ * OVF_PE + (OVF_PE + 1))
                    for half, b in enumerate((4, 7)):
                        ve.tensor_copy(xg[:, 0, 4 * half:4 * half + 4, 0:CAP], psum[:, b, 0:4 * CAP].rearrange("p (k c) -> p k c", k=4)).then_inc(ovv, 1)
                    ve.tensor_copy(SwT[0:CAP, :], psum[0:CAP, 6, 0:T]).then_inc(ovv, 1)
                    ve.wait_ge(flag(e + "_ovf_silu"), k_ + 1)
                    tt(hh[0:CAP, 0:FW], sg[0:CAP, 0:FW], psum[0:CAP, 6, 0:FW], ALU.mult).then_inc(ovv, 1)
                    ve.wait_ge(ovp, k_ * OVF_PE + (OVF_PE + 3))
                    ve.tensor_copy(hT[:, 0:F, 0:CAP], psum[:, 5, 0:FW].rearrange("p (f c) -> p f c", f=F)[:, :, 0:CAP]).then_inc(ovv, 1)
                    ve.wait_ge(ovp, k_ * OVF_PE + (OVF_PE + 4))
                    for half, b in enumerate((4, 7)):
                        ve.tensor_copy(og[0:CAP, half * 512:(half + 1) * 512], psum[0:CAP, b, :]).then_inc(ovv, 1)

        rms_norm("x", h_tok)
        tell("h_tok")
        after(ve, "act", "ssm_dt")
        sc = lambda n: ssm_s[:, n, :]
        step(tt(s_adt, V("a_re"), s_dt, ALU.mult))
        tell("ssm_adt")
        step(tt(s_th, V("a_im"), s_dt, ALU.mult))
        step(ts(sc(6), s_th, 1.0 / (2 * np.pi), ROUND, ALU.mult, ALU.add))
        step(ts(sc(6), sc(6), -ROUND, None, ALU.add))
        step(stt(out=sc(7), in0=sc(6), scalar=-TWO_PI_HI, in1=s_th, op0=ALU.mult, op1=ALU.add))
        step(stt(out=sc(7), in0=sc(6), scalar=-TWO_PI_LO, in1=sc(7), op0=ALU.mult, op1=ALU.add))
        step(ts(sc(5), sc(7), SIN_MAX, -SIN_MAX, ALU.min, ALU.max))
        step(stt(out=sc(6), in0=sc(5), scalar=-1.0, in1=sc(5), op0=ALU.mult, op1=ALU.min))
        step(ts(sc(4), sc(6), np.pi / 2, None, ALU.add))
        tell("ssm_angle")
        take_T("hT", V("mix_g"))
        after(ve, "act", "ssm_sin")
        for k in range(LEVELS):
            counted(tt(sc(6), e_pow(k, 0), e_pow(k, 0), ALU.mult))
            n = counted(tt(sc(7), e_pow(k, 1), e_pow(k, 1), ALU.mult))
            counted(stt(out=e_pow(k + 1, 1), in0=e_pow(k, 0), scalar=2.0, in1=e_pow(k, 1), op0=ALU.mult, op1=ALU.mult))
            ve.wait_ge(chain, n)
            step(tt(e_pow(k + 1, 0), sc(6), sc(7), ALU.subtract))
        tell("ssm_powers2")
        are, aim = V("a_re"), V("a_im")
        step(tt(sc(6), s_mag, e_pow(0, 0), ALU.mult))
        step(ts(sc(6), sc(6), -1.0, None, ALU.add))
        step(tt(sc(7), s_mag, e_pow(0, 1), ALU.mult))
        step(tt(sc(8), are, are, ALU.mult))
        step(tt(sc(9), aim, aim, ALU.mult))
        step(tt(sc(8), sc(8), sc(9), ALU.add))
        step(ve.reciprocal(sc(8), sc(8)))
        step(tt(sc(9), sc(6), are, ALU.mult))
        step(tt(sc(10), sc(7), aim, ALU.mult))
        step(tt(sc(9), sc(9), sc(10), ALU.add))
        step(tt(sc(9), sc(9), sc(8), ALU.mult))
        step(tt(sc(10), sc(7), are, ALU.mult))
        step(tt(sc(11), sc(6), aim, ALU.mult))
        step(tt(sc(10), sc(10), sc(11), ALU.subtract))
        step(tt(sc(10), sc(10), sc(8), ALU.mult))
        after(ve, "pool", "zeros")
        cr, ci = (V(n).rearrange("p (j c) -> p j c", j=NJ) for n in ("c_re", "c_im"))
        fr_, fi_ = over(sc(9), P, NJ, 16), over(sc(10), P, NJ, 16)
        t1, t2 = (at(4096 + 256 * n, NJ, 16) for n in range(2))
        for c_ in range(2):
            step(tt(t1, cr, (fr_, fi_)[c_], ALU.mult))
            step(tt(t2, ci, (fi_, fr_)[c_], ALU.mult))
            step(tt(t1, t1, t2, (ALU.subtract, ALU.add)[c_]))
            if c_:
                step(ts(t1, t1, -1.0, None, ALU.mult))
            t1q = t1.rearrange("p (q j) c -> p q j c", q=NQ)
            blk = c_blk[:, c_, :, :].rearrange("p (q j) s -> p q j s", q=NQ)
            for jj in range(4):
                for o in range(2):
                    r = slice(o * HD, (o + 1) * HD)
                    col = (2 * jj + o) * 16
                    n = counted(ve.tensor_copy(blk[r, :, jj, col:col + 16], t1q[r, :, jj, :]))
            ve.wait_ge(chain, n)

        carry = ssm_s[:, 12:16, 0:4]

        def ssm_states(q):
            js = slice(4 * q, 4 * q + 4)
            c_t, s_t = powers[:, 0, js, :], powers[:, 1, js, :]
            c_both = c_t.unsqueeze(1).broadcast_to([P, 2, 4, HALF_T])
            for b in range(2, 6):
                full(ve, "bu", q, b)
            bu = psum[:, 2:6, :].rearrange("p (c b) (a t) -> p c (b a) t", c=2, a=2)
            for half in range(2):
                b_in = bu[:, :, :, half * HALF_T:(half + 1) * HALF_T]
                w_ = ws[:, half, :, :, :]
                counted(tt(tmp, c_both, b_in, ALU.mult))
                n0 = counted(tt(zs[:, 0, :, :], s_t, b_in[:, 1, :, :], ALU.mult))
                n1 = counted(tt(zs[:, 1, :, :], s_t, b_in[:, 0, :, :], ALU.mult))
                if q:
                    ve.wait_ge(flag("ssm_y"), 2 * (q - 1) + half + 1)
                ve.wait_ge(chain, n0)
                counted(tt(w_[:, 0, :, :], tmp[:, 0, :, :], zs[:, 0, :, :], ALU.add))
                ve.wait_ge(chain, n1)
                step(tt(w_[:, 1, :, :], tmp[:, 1, :, :], zs[:, 1, :, :], ALU.subtract))
                if half:
                    for b in range(2, 6):
                        ve.sem_inc(bank_free[b], 1)
                for c_ in range(2):
                    for jj in range(4):
                        mag = s_mag[:, 4 * q + jj:4 * q + jj + 1].broadcast_to([P, HALF_T])
                        init = carry[:, c_, jj:jj + 1] if half else 0.0
                        n = counted(ve.tensor_tensor_scan(zs[:, c_, jj, :], mag, w_[:, c_, jj, :], init, ALU.mult, ALU.add))
                ve.wait_ge(chain, n)
                counted(tt(tmp, c_both, zs, ALU.mult))
                n0 = counted(tt(w_[:, 0, :, :], s_t, zs[:, 1, :, :], ALU.mult))
                n1 = counted(tt(w_[:, 1, :, :], s_t, zs[:, 0, :, :], ALU.mult))
                ve.wait_ge(chain, n0)
                counted(tt(w_[:, 0, :, :], tmp[:, 0, :, :], w_[:, 0, :, :], ALU.subtract))
                ve.wait_ge(chain, n1)
                step(tt(w_[:, 1, :, :], tmp[:, 1, :, :], w_[:, 1, :, :], ALU.add))
                tell(f"ssm_state{2 * q + half}")
                if half == 0:
                    c1, s1 = e_pow(LEVELS, 0)[:, js], e_pow(LEVELS, 1)[:, js]
                    zr, zi = zs[:, 0, :, HALF_T - 1], zs[:, 1, :, HALF_T - 1]
                    step(tt(carry[:, 2, :], c1, zr, ALU.mult))
                    step(tt(carry[:, 3, :], s1, zi, ALU.mult))
                    step(tt(carry[:, 0, :], carry[:, 2, :], carry[:, 3, :], ALU.subtract))
                    step(tt(carry[:, 2, :], c1, zi, ALU.mult))
                    step(tt(carry[:, 3, :], s1, zr, ALU.mult))
                    step(tt(carry[:, 1, :], carry[:, 2, :], carry[:, 3, :], ALU.add))

        def ssm_skip(q):
            src = full(ve, "y", q)
            read_out(stt(out=yg[:, q, :], in0=uT[:, q, :], scalar=V("d_skip")[:, q:q + 1], in1=src[:, 0:T],
                         op0=ALU.mult, op1=ALU.add), "y", q)

        def take_qk(w, c0):
            for th in range(TH):
                src = full(ve, w, th)
                read_out(ve.tensor_copy(qk_tok[:, th, c0:c0 + 512], src), w, th)

        take_qk("q", 0)
        after(ve, "pool", "powers")
        ssm_states(0)
        take_qk("k", 512)
        for w in "qk":
            for th in range(TH):
                evacuated(ve, w, th)
        for th in range(TH):
            step(tt(square_junk, qk_tok[:, th, :], qk_tok[:, th, :], ALU.mult))
            step(ve.tensor_reduce(qk_r[:, th * 16:(th + 1) * 16], square_junk.rearrange("p (h d) -> p h d", h=16), AX.X, ALU.add))
        step(ts(qk_r, qk_r, 1.0 / HD, 1e-6, ALU.mult, ALU.add))
        tell("qk_ms")
        src = full(ve, "f")[:, 0:16].rearrange("p (a h) -> p a h", a=2)
        fr = f_raw.rearrange("p (a h) -> p a h", a=2)
        read_out(tt(fr, src, rows_over(brow[:, 0:8], TH), ALU.add), "f")
        evacuated(ve, "f")
        step(stt(out=f_abs, in0=f_raw, scalar=-1.0, in1=f_raw, op0=ALU.mult, op1=ALU.max))
        tell("f_abs")
        after(ve, "act", "qk_rms")
        step(ve.reciprocal(qk_r, qk_r))
        for th in range(TH):
            v3_ = qk_tok[:, th, :].rearrange("p (h d) -> p h d", h=16)
            step(tt(v3_, v3_, over(qk_r[:, th * 16:(th + 1) * 16], P, 16, HD), ALU.mult))
        tell("qk_tok")
        after(ve, "act", "f_ln")
        lf_pos = lf[:, 0, :, :].rearrange("p a h -> p (a h)")
        lf_neg = lf[:, 1, :, :].rearrange("p a h -> p (a h)")
        step(stt(out=lf_pos, in0=f_raw, scalar=0.0, in1=f_l, op0=ALU.min, op1=ALU.subtract))
        step(ts(lf_neg, lf_pos, -1.0, None, ALU.mult))
        tell("logf")
        ssm_states(1)
        ssm_skip(0)
        for th in range(TH):
            src = full(ve, "qT", th).rearrange("p (j t) -> p j t", j=4)
            split_heads(("qT", th), qz1[:, :, th * P:(th + 1) * P], src, 0, V("qg"), HD ** -0.5)
        for th in range(TH):
            src = full(ve, "kT", th).rearrange("p (j t) -> p j t", j=4)
            read_out(ts(kT1[:, :, th * P:(th + 1) * P], src, V("kg"), None, ALU.mult), "kT", th)
        after(ve, "pool", "masks")
        src = full(ve, "F")
        step(ve.tensor_copy(Ft, src[:, 0:16].rearrange("p (a h) -> p a h", a=2)))
        read_out(ve.tensor_copy(nF[0:8, :], src[0:8, 128:128 + T]), "F")
        ssm_states(2)
        ssm_skip(1)
        ssm_states(3)
        ssm_skip(2)
        ssm_skip(3)
        attention("at1", 8, ALU.add, lambda h, th: Ft[:, th, h:h + 1], True)
        for n in range(2):
            evacuated(ve, "glu", n)
        step(tt(y_ssm, y_ssm, yg, ALU.mult))
        tell("y_ssm")
        for n in range(4):
            src = full(ve, "pa", n).rearrange("p (a t) -> p a t", a=2)
            read_out(tt(mixedT[:, 2 * n:2 * n + 2, :], src, gates[:, 2 * n:2 * n + 2, :], ALU.mult), "pa", n)
            src = full(ve, "ps", n).rearrange("p (a t) -> p a t", a=2)
            read_out(tt(mix_tmp, src, gates[:, 8 + 2 * n:10 + 2 * n, :], ALU.mult), "ps", n)
            evacuated(ve, "pa", n)
            evacuated(ve, "ps", n)
            tt(mixedT[:, 2 * n:2 * n + 2, :], mixedT[:, 2 * n:2 * n + 2, :], mix_tmp, ALU.add).then_inc(flag("mixed"), 1)
            ve.wait_ge(flag("mixed"), n + 1)
        take_T("memT")
        residual("res1", 1.0)
        tell("x1")
        rms_norm("x1", xh)
        ve.wait_ge(flag("gain_loaded"), 16)
        step(tt(xh, xh, rows_over(gain, TH), ALU.mult))
        tell("e1_tok")
        moe("e1")
        moe_sum("e1", 1.0)
        tell("x2")

        take_T("x2T")
        step(ve.memset(hpad, 0.0))
        step(ve.memset(qz2, 0.0))
        for n in range(MT):
            after(ve, "act", f"conv_gate{n}")
            src = full(ve, "conv", n)
            read_out(tt(hpad[:, n, PAD:PAD + T], src[:, 0:T], gatez[:, n % 2, :], ALU.mult), "conv", n)
            evacuated(ve, "conv", n)
            tell(f"glu_in{n}")
        src = full(ve, "qm2").rearrange("p (a t) -> p a t", a=2)
        split_heads(("qm2",), qz2, src, 0, None)
        tap = flag("conv_tap")
        dw = V("dw_w")
        for n in range(MT):
            ts(conv[:, n, :], hpad[:, n, 0:T], dw[:, n * TAPS:n * TAPS + 1], V("dw_b")[:, n:n + 1], ALU.mult, ALU.add).then_inc(tap, 1)
        with ve.Fori(1, TAPS) as k:
            for n in range(MT):
                ve.wait_ge(tap, k * MT + (n - MT + 1))
                stt(out=conv[:, n, :], in0=hpad[:, n, bass.ds(k, T)], scalar=dw[:, bass.ds(k + n * TAPS, 1)],
                    in1=conv[:, n, :], op0=ALU.mult, op1=ALU.add).then_inc(tap, 1)
        ve.wait_ge(tap, MT * TAPS)
        tell("conv_done")
        src = full(ve, "mean")
        read_out(ts(stat[:, 0, :], src[:, 0:T], 1.0 / MIX, None, ALU.mult), "mean")
        evacuated(ve, "mean")
        step(tt(conv, conv, rows_over(stat[:, 0, :], MT), ALU.subtract))
        step(tt(sq, conv, conv, ALU.mult))
        tell("conv_sq")
        src = full(ve, "var")
        read_out(ts(stat[:, 1, :], src[:, 0:T], 1.0 / MIX, 1e-5, ALU.mult, ALU.add), "var")
        evacuated(ve, "var")
        tell("conv_var")
        after(ve, "act", "conv_std")
        step(ve.reciprocal(stat[:, 1, :], stat[:, 1, :]))
        for n in range(MT):
            tt(conv[:, n, :], conv[:, n, :], stat[:, 1, :], ALU.mult).then_inc(flag("conv_norm"), 1)
        attention("at2", 4, ALU.mult, lambda h, th: HD ** -0.5, False)
        residual("res2", ALPHA)
        layer_norm("ln21", 1)
        tell("e2_tok")
        moe("e2")
        moe_sum("e2", ALPHA)
        layer_norm("ln22", 3)
        tell("x3")

        take_T("x3T")
        step(ve.memset(qz3, 0.0))
        step(ve.memset(qz3m, 0.0))
        for n in range(3):
            src = full(ve, "mq", n).rearrange("p (a t) -> p a t", a=2)
            split_heads(("mq", n), qz3, src, 2 * n, None)
        src = full(ve, "qm3").rearrange("p (a t) -> p a t", a=2)
        split_heads(("qm3",), qz3m, src, 0, None)
        attention("at3", 12, ALU.mult, lambda h, th: HD ** -0.5, True)
        attention("at3m", 4, ALU.mult, lambda h, th: HD ** -0.5, False)
        residual("res3", ALPHA)
        layer_norm("ln31", 5)
        tell("e3_tok")
        moe("e3")
        moe_sum("e3", ALPHA)
        layer_norm("ln32", 7)
        tell("x_final")


def _tiles(w, c0, c1, slot=True):
    w = w[:, c0:c1]
    k = w.shape[0] // P
    w = w.reshape(k, P, c1 - c0).transpose(1, 0, 2)
    if k * (c1 - c0) < SLOT:
        out = np.zeros((P, SLOT), np.float32)
        if k == KD:
            out.reshape(P, KD, 512)[:, :, :c1 - c0] = w
        else:
            out[:, :k * (c1 - c0)] = w.reshape(P, -1)
        return out
    return w.reshape(P, -1)


def _experts(w):
    e, r, c = w.shape
    return np.ascontiguousarray(w.reshape(e, r // P, P, c).transpose(0, 2, 1, 3).reshape(e, P, (r // P) * c))


def _layout(a):
    w_in = a["w_in"][0]
    chunks = {"u": _tiles(w_in, 1544, 2056), "q": _tiles(w_in, 0, 512), "k": _tiles(w_in, 512, 1024),
              "v": _tiles(w_in, 1024, 1536), "glu": _tiles(a["w_glu"][0], 0, 512),
              "pa": _tiles(a["w_proj_attn"][0], 0, D), "ps": _tiles(a["w_proj_ssm"][0], 0, D),
              "memkv": _tiles(a["w_mem_kv_2"], 0, 512)}
    for n in range(4):
        chunks[f"g{n}"] = _tiles(w_in, 2056 + 512 * n, 2568 + 512 * n)
    for name, w in (("wo", a["w_out"][0]), ("w2o", a["w_o_2"][0]), ("w3o", a["w_o_2"][1])):
        for n in range(2):
            chunks[f"{name}{n}"] = _tiles(w[512 * n:512 * (n + 1)], 0, D)
    cw = a["conv_w_in_2"][0]
    for n in range(3):
        cols = [cw[:, c + P * (2 * n + m):c + P * (2 * n + m + 1)] for m in range(2) for c in (0, MIX)]
        chunks[f"c{n}"] = _tiles(np.concatenate(cols, 1), 0, 512)
    chunks["c3"] = _tiles(cw, 2 * MIX, 2 * MIX + 256)
    mw = a["moba_w_in_2"][0]
    for n in range(5):
        chunks[f"m{n}"] = _tiles(mw, 512 * n, 512 * (n + 1))
    out = {"stream": np.stack([chunks[c] for c in CHUNKS])}

    by_part = lambda v: v.reshape(-1, P).T
    state = lambda v: v.reshape(NJ, 2 * HD).T
    cmat = lambda c: c.transpose(0, 2, 1).reshape(NJ, P, 16).transpose(1, 0, 2).reshape(P, NJ * 16)
    ldt = np.repeat(a["ssm_log_dt"][0][:, None], HD, axis=1)
    parts = {"mix_g": by_part(a["norm_mix_g"][0]), "qg": np.tile(a["q_norm_g"][0], 2)[:, None],
             "kg": np.tile(a["k_norm_g"][0], 2)[:, None], "a_re": state(a["ssm_A_re"][0]), "a_im": state(a["ssm_A_im"][0]),
             "log_dt": state(ldt), "d_skip": by_part(a["ssm_D"][0]), "dw_b": by_part(a["conv_dw_b_2"][0]),
             "ln_g": by_part(a["conv_ln_g_2"][0]), "ln_b": by_part(a["conv_ln_b_2"][0]),
             "dw_w": a["conv_dw_w_2"][0].T.reshape(MT, P, TAPS).transpose(1, 0, 2).reshape(P, MT * TAPS),
             "c_re": cmat(a["ssm_C_re"][0]), "c_im": cmat(a["ssm_C_im"][0])}
    out["vec"] = np.concatenate([parts[n] for n in VEC], 1)
    blk = np.zeros((2, P, NJ, P), np.float32)
    for c, name in enumerate(("ssm_B_re", "ssm_B_im")):
        b = a[name][0]
        for g in range(32):
            j, o = g // 2, g % 2
            r = (g % 8) * 16
            blk[c, r:r + 16, j, o * HD:(o + 1) * HD] = b[g].T
    out["b_blk"] = blk
    out["wf"] = w_in[:, 1536:1544].reshape(KD, P, 8).transpose(1, 0, 2)
    rg = [a["w_router_group"][0], a["w_rg_2"][0], a["w_rg_2"][1]]
    re = [a["w_router_expert"][0], a["w_re_2"][0], a["w_re_2"][1]]
    out["wr"] = np.stack([np.concatenate([g, e], 1).reshape(KD, P, NR).transpose(1, 0, 2) for g, e in zip(rg, re)])
    out["brow"] = np.concatenate([a["b_forget"][0], a["b_router_group"][0], a["b_router_expert"][0],
                                  a["b_rg_2"][0], a["b_re_2"][0], a["b_rg_2"][1], a["b_re_2"][1]])[None, :]
    rows = [a["norm_ffn_g"][0]]
    for n in range(2):
        rows += [a["ln1_g_2"][n], a["ln1_b_2"][n], a["ln2_g_2"][n], a["ln2_b_2"][n]]
    out["rows"] = np.stack(rows)
    out["x"] = a["x"][0]
    out["mem"] = a["mem_2"][0]
    for e, (g, u, d) in (("e1", (a["w_expert_gate"][0], a["w_expert_up"][0], a["w_expert_down"][0])),
                         ("e2", tuple(a[n][0].reshape(NE, *a[n].shape[3:]) for n in ("w_gate_2", "w_up_2", "w_down_2"))),
                         ("e3", tuple(a[n][1].reshape(NE, *a[n].shape[3:]) for n in ("w_gate_2", "w_up_2", "w_down_2")))):
        out[e + "_gate"], out[e + "_up"], out[e + "_down"] = _experts(g), _experts(u), _experts(d)
    return {n: np.ascontiguousarray(v) for n, v in out.items()}


def kernel(**inputs):
    import concourse.bacc as _bacc
    from concourse.bass_utils import run_bass_kernel_spmd as _run

    arrays = _layout({n: np.asarray(v) for n, v in inputs.items()})
    nc = _bacc.Bacc("TRN2", target_bir_lowering=False, num_devices=1)
    named = {n: nc.dram_tensor(f"in_{n}", v.shape, F32, kind="ExternalInput").ap() for n, v in arrays.items()}
    out = nc.dram_tensor("out_x", (T, D), F32, kind="ExternalOutput").ap()
    build(nc, named, out)
    r = _run(nc, [{f"in_{n}": v for n, v in arrays.items()}], core_ids=[0])
    return r.results[0]["out_x"].reshape(1, T, D)
```

```python
from contextlib import ExitStack

import numpy as np
import concourse.bass as bass
from concourse import mybir

ALU = mybir.AluOpType
ACT = mybir.ActivationFunctionType
AX = mybir.AxisListType
F32 = mybir.dt.float32
I32 = mybir.dt.int32

P = 128
D = 1024
KD = D // P
T = 256
TH = T // P
HD = 64
NE, NG, EPG = 32, 4, 8
NR = NG + NE
TOP_K = 2
CAP = 64
PAIRS = NE // 2
EXTRA = T // CAP - 1
NOVF = TOP_K * T // CAP
NO_ITEM = EXTRA * NE
NJ = 16
NQ = 4
HALF_T = 128
LEVELS = 7
TAPS = 31
MIX = 768
MT = MIX // P
PAD = TAPS - 1
TAP_STEP = 6
VEC_TILES = 4
SLOT = 4096
NSLOT = 6
NBUF = 6
NBUF1 = 4
ALPHA = (2 * 2) ** 0.25
MASKED = -1e30
TWO_PI_HI = 6.28125
TWO_PI_LO = 2 * np.pi - 6.28125
ROUND = 1.5 * 2 ** 23
SIN_MAX = 3.1415925

VEC = {}
_n = 0
for _name, _w in (("mix_g", KD), ("qg", 1), ("kg", 1), ("a_re", NJ), ("a_im", NJ), ("log_dt", NJ),
                  ("d_skip", NQ), ("dw_b", MT), ("ln_g", MT), ("ln_b", MT), ("dw_w", MT * TAPS),
                  ("c_re", NJ * 16), ("c_im", NJ * 16)):
    VEC[_name] = (_n, _n + _w)
    _n += _w
NVEC = _n

STREAM = (["u", "q", "k", "v", "g0", "g1", "g2", "g3", "glu", "pa", "ps", "wo0", "wo1", "memkv"],
          ["c3", "c0", "c1", "c2", "w2o0", "w2o1"],
          ["m4", "m0", "m1", "m2", "m3", "w3o0", "w3o1"])
CHUNKS = [n for part in STREAM for n in part]


def build(nc, ins, out):
    ctx = ExitStack()
    with ctx:
        _build(ctx, nc, ins, out)


def _build(ctx, nc, ins, out):
    def sb(name, shape, dt=F32):
        return ctx.enter_context(nc.sbuf_tensor(name, shape, dt))

    sems = {}

    def flag(name):
        if name not in sems:
            sems[name] = ctx.enter_context(nc.semaphore(name))
        return sems[name]

    ring = sb("ring", [P, NSLOT, SLOT])
    x_sb = sb("x_sb", [P, TH, D])
    xT = sb("xT", [P, KD, T])
    ident = sb("ident", [P, P])
    ones = sb("ones", [P, P])
    before = sb("before", [P, P])
    upto = sb("upto", [P, TH, T])
    mask = sb("mask", [P, TH, T])
    col_id = sb("col_id", [P, EXTRA * NE])
    vec = sb("vec", [P, NVEC])
    rows = sb("rows", [P, 2, D])
    head_sel = rows[:, 0, :].rearrange("p (h t) -> p h t", h=8)
    nF = sb("nF", [P, T])
    mem_k = sb("mem_k", [P, 2, T])
    mem_v = sb("mem_v", [P, TH, 256])
    wr = sb("wr", [P, KD, NR])
    brow = sb("brow", [P, 8 + 3 * NR])
    small = sb("small", [P, 256])
    ovf = sb("ovf", [P, 2 * NOVF + 2], I32)
    arena = sb("arena", [P, 15360])

    def at(off, *dims):
        n = int(np.prod(dims))
        a = arena[:, off:off + n]
        if len(dims) == 1:
            return a
        names = "abcd"[:len(dims)]
        return a.rearrange(f"p ({' '.join(names)}) -> p {' '.join(names)}",
                           **{c: d for c, d in zip(names[:-1], dims[:-1])})

    V = lambda name: vec[:, VEC[name][0]:VEC[name][1]]

    gates = at(0, 16, T)
    h_tok = at(0, TH, D)
    qk_tok = at(2048, TH, 1024)
    zs = at(4096, 2, 4, HALF_T)
    tmp = at(5120, 2, 4, HALF_T)
    mixedT = at(4096, KD, T)
    ws = at(6144, 2, 2, 4, HALF_T)
    y_ssm = at(6144, NQ, T)
    v_tok = at(8192, TH, 512)
    qz1 = at(9216, 8, T)
    kT1 = at(11264, 4, T)
    uT = at(12288, NQ, T)
    yg = at(13312, NQ, T)
    ya = at(14336, 4, T)
    powers = ring[:, 3, :].rearrange("p (c j t) -> p c j t", c=2, j=NJ)
    b_blk = ring[:, 4:6, 0:2048].rearrange("p c (j s) -> p c j s", j=NJ)
    c_blk = ring[:, 4:6, 2048:4096].rearrange("p c (j s) -> p c j s", j=NJ)
    P_buf = rows[:, :, :].rearrange("p a (b t) -> p (a b) t", b=4)
    PT_buf = sb("PT_buf", [P, 2, T])
    gatez = at(0, MT, T)
    hpad = at(2048, MT, PAD + T)
    conv = at(3840, MT, T)
    sq = at(5376, MT, T)
    stat = at(6912, 4, T)
    qz2 = at(8192, 4, T)
    yT = at(9216, KD, T)
    diag = at(11264, TAPS, P)
    qz3 = at(0, 12, T)
    kT3 = at(3072, MT, T)
    v3 = at(4608, TH, MIX)
    qz3m = at(6144, 4, T)
    xh = at(0, TH, D)
    S = at(2048, 2, TH, 2 * CAP)
    Sw = at(2560, 2, TH, 2 * CAP)
    SwT = at(3072, T)
    xg = at(3328, 2, KD, 2 * CAP)
    sg = at(5376, 512)
    hT = at(5888, 4, 2 * CAP)
    og = at(6400, D)
    rt = at(7424, 4096)
    rank = at(11520, TH, NE + 2)
    wcomb = at(11588, TH, NE + 2)
    sel = at(11656, TH, NE)
    hh = at(11720, 512)
    rank3 = at(12232, TH, NO_ITEM + 1)
    wcomb3 = at(12432, TH, NO_ITEM + 1)
    item_eq = at(12632, NOVF, EXTRA * NE)
    item_t = at(13400, NOVF, EXTRA * NE)
    junk = at(12288, D)

    gain = rows[:, 0, :]
    mem_tok = at(9216, TH, D)
    memT = at(13312, KD, T)
    wf = sb("wf", [P, KD, 8])
    lf = sb("lf", [P, 2, TH, 8])
    e_tab = sb("e_tab", [P, LEVELS + 1, 2, NJ])
    ssm_s = sb("ssm_s", [P, 16, NJ])

    def e_pow(k, c):
        return e_tab[:, k, c, :]

    rms_ms = small[:, 0:2]
    rms_r = small[:, 2:4]
    ln_r = small[:, 4:6]
    nmax, psums, precip = (small[:, 156 + 8 * n:164 + 8 * n] for n in range(3))

    def buffers(name):
        if name == "at1":
            return NBUF1, lambda n: 8 - NBUF1 + n % NBUF1
        return NBUF, lambda n: n % NBUF

    Ft = small[:, 16:32].rearrange("p (a h) -> p a h", a=2)
    qk_r = small[:, 32:64]
    f_raw, f_abs, f_e, f_l = (small[:, 64 + 16 * n:80 + 16 * n] for n in range(4))
    bn6 = small[:, 128:152].rearrange("p (a b c) -> p a b c", a=2, b=2)
    bn2 = small[:, 152:156].rearrange("p (a b) -> p a b", a=2)
    s_dt, s_adt, s_mag, s_th = (ssm_s[:, n, :] for n in range(4))
    s_ang = ssm_s[:, 4:6, :].rearrange("p c j -> p (c j)")
    mix_tmp = at(7168, 2, T)
    square_junk = at(14336, D)

    def rt_at(off, *dims):
        return at(7424 + off, *dims)

    r_L, r_gd, r_ge = rt_at(0, TH, NR), rt_at(72, TH, NG), rt_at(80, TH, NG)
    r_geq, r_gc, r_goh, r_pen = (rt_at(88 + 8 * n, TH, NG) for n in range(4))
    r_gmax, r_gfirst, r_gs, r_gw, r_m1, r_m2, r_f1, r_f2, r_d21, r_p2, r_rd, r_w1, r_w2 = (
        rt_at(120 + 2 * n, TH) for n in range(13))
    r_EL, r_eq, r_cand, r_oh1, r_oh2, r_t = (rt_at(160 + 64 * n, TH, NE) for n in range(6))
    r_cnt, r_over, r_pos = rt_at(600, NE), rt_at(632, EXTRA, NE), rt_at(728, EXTRA * NE)
    r_list = rt_at(824, 2 * NOVF + 2)
    r_expert = rt_at(848, EXTRA, NE)
    r_there, r_total = rt_at(944, NOVF), rt_at(952, 1)

    psum = ctx.enter_context(nc.psum_tensor("psum", [P, 8, 512], F32))

    bank_full = [flag(f"bank_full{b}") for b in range(8)]
    bank_free = [flag(f"bank_free{b}") for b in range(8)]
    plan, uses = {}, [0] * 8

    def use(name, bank):
        plan[name] = (bank, uses[bank])
        uses[bank] += 1

    turn = [0]

    def use2(*name):
        use(name, turn[0] % 2)
        turn[0] += 1

    def plan_attention(name, heads):
        for n in range(2 * heads):
            use((name, "score", n), 2 + n % 2)
            use((name, "pt", n), 4 + n % 2)
        for p in range(heads // 2):
            use((name, "pv", p), 6 + p % 2)

    def plan_turn(name, first=2):
        for n in range(4):
            use((name, n), first + n)

    plan_turn("hT")
    for n in range(2):
        use2("u", n)
    for q in range(NQ):
        for b in range(2, 6):
            use(("bu", q, b), b)
        use(("y", q), 6 + q % 2)
    for w in "qk":
        for th in range(TH):
            use2(w, th)
    use2("f")
    for th in range(TH):
        use2("v", th)
    use2("F")
    for n in range(2 * NQ):
        use2("gate", n)
    for th in range(TH):
        use(("qT", th), 2 + th)
        use(("kT", th), 4 + th)
    plan_attention("at1", 8)
    use2("glu", 0)
    use2("glu", 1)
    for n in range(4):
        use2("pa", n)
        use2("ps", n)
    plan_turn("memT")
    for n in range(4):
        use2("res1", n)
    use2("memk")
    for th in range(TH):
        use2("memv", th)

    def plan_moe(name):
        plan_turn(name + "xT")
        use((name + "logits",), 6)
        use((name + "rank",), 7)

    plan_moe("e1")
    before_moe = {"e1": list(uses)}
    plan_turn("x2T", 4)
    use(("qm2",), 4)
    for n in range(MT):
        use(("conv", n), (0, 1, 2, 3, 6, 7)[n])
    plan_attention("at2", 4)
    for n in range(VEC_TILES, MT):
        use2("depthwise", n)
    use2("mean")
    use2("var")
    for n in range(4):
        use(("res2", n), 2 + n)
    plan_moe("e2")
    before_moe["e2"] = list(uses)
    plan_turn("x3T", 4)
    use2("qm3")
    for th in range(TH):
        use2("mv1", th)
    for n in range(3):
        use2("mq", n)
    plan_attention("at3m", 4)
    for n in range(3):
        use2("mk", n)
    for th in range(TH):
        use2("mv0", th)
    plan_attention("at3", 12)
    for n in range(4):
        use(("res3", n), (0, 1, 2, 3)[n])
    plan_moe("e3")
    before_moe["e3"] = list(uses)

    def open_bank(pe, *name):
        b, m = plan[name]
        if m:
            pe.wait_ge(bank_free[b], m)
        return b

    def close_bank(ins, *name):
        ins.then_inc(bank_full[plan[name][0]], 1)

    def full(eng, *name):
        b, m = plan[name]
        eng.wait_ge(bank_full[b], m + 1)
        return psum[:, b, :]

    def read_out(ins, *name):
        ins.then_inc(bank_free[plan[name][0]], 1)

    def evacuated(eng, *name):
        b, m = plan[name]
        eng.wait_ge(bank_free[b], m + 1)

    last_use = {"u": ("u", 1), "q": ("q", 1), "k": ("k", 1), "v": ("v", 1), "glu": ("glu", 1), "pa": ("pa", 3),
                "ps": ("ps", 3), "wo0": ("res1", 3), "wo1": ("res1", 3), "memkv": ("memv", 1), "c3": ("qm2",),
                "w2o0": ("res2", 3), "w2o1": ("res2", 3), "m0": ("mq", 1), "m1": ("mk", 0), "m2": ("mk", 2),
                "m3": ("mv0", 1), "m4": ("mv1", 1), "w3o0": ("res3", 3), "w3o1": ("res3", 3)}
    for n in range(4):
        last_use[f"g{n}"] = ("gate", 2 * n + 1)
    for n in range(3):
        last_use[f"c{n}"] = ("conv", 2 * n + 1)
    loaded = [flag(f"loaded{s}") for s in range(2 * NSLOT)]
    used = [flag(f"used{s}") for s in range(2 * NSLOT)]
    loads, moe_uses = [0] * (2 * NSLOT), [0] * (2 * NSLOT)
    holder = [None] * NSLOT
    where, moe_loads, moe_used, moe_after = {}, {}, {}, {}
    for part, (names, width) in enumerate(zip(STREAM, (3, NSLOT, NSLOT))):
        for n, c in enumerate(names):
            s = n % width
            where[c] = (s, loads[2 * s], holder[s] or (moe_uses[2 * s], moe_uses[2 * s + 1]))
            loads[2 * s] += 1
            holder[s] = c
        e = f"e{part + 1}"
        moe_loads[e], moe_used[e], moe_after[e] = list(loads), list(moe_uses), list(holder)
        holder = [None] * NSLOT
        for s in range(2 * NSLOT):
            n = 8 if part == 0 else 16 * (s % 2 == 0)
            loads[s] += n
            moe_uses[s] += n

    def load_chunk(sp, c):
        s, _, prior = where[c]
        if isinstance(prior, str):
            full(sp, *last_use[prior])
        else:
            for half in range(2):
                if prior[half]:
                    sp.wait_ge(used[2 * s + half], prior[half] + SEED)
        sp.dma_start(ring[:, s, :], ins["stream"][CHUNKS.index(c)]).then_inc(loaded[2 * s], 16)

    def chunk(pe, c, inner):
        s, before_, _ = where[c]
        pe.wait_ge(loaded[2 * s], 16 * (before_ + 1))
        return ring[:, s, :].rearrange("p (k n) -> p k n", n=inner)

    def moe_slots(e, u):
        if e == "e1":
            return [(6 * u + w, 1, 0) for w in range(6)]
        return [(2 * w, 2, u) for w in range(6)]

    def moe_view(e, hs):
        return ring[:, hs // 2, (hs % 2) * 2048:(hs % 2) * 2048 + (2 if e == "e1" else 4) * 1024]

    def moe_steps(e):
        return [e + n for n in ("_tok0", "_tok", "_zero", "_gd", "_sel", "_d21", "_items")]

    milestones = {
        "vec": ["x_ms", "h_tok", "ssm_adt", "ssm_angle", "ssm_powers2", "ssm_state0", "ssm_state1", "qk_ms", "f_abs",
                "qk_tok", "logf"] + [f"ssm_state{n}" for n in range(2, 2 * NQ)] + ["y_ssm", "x1", "x1_ms"] + moe_steps("e1")
        + ["x2_0", "x2"] + [f"glu_in{n}" for n in range(MT)] + ["conv_done", "conv_off0", "conv_off2", "conv_off4", "conv_var", "ln21_var"]
        + moe_steps("e2") + ["ln22_var", "x3_0", "x3", "ln31_var"] + moe_steps("e3") + ["ln32_var", "x_final0", "x_final"],
        "act": ["x_sq", "x_rms", "ssm_dt", "ssm_mag", "ssm_sin", "qk_rms", "f_ln", "x1_sq", "x1_rms", "e1_ge", "e1_p2"]
        + [f"conv_gate{n}" for n in range(MT)] + ["conv_std", "ln21_std", "e2_ge", "e2_p2", "ln22_std", "ln31_std",
                                                  "e3_ge", "e3_p2", "ln32_std"],
        "pool": ["ident", "masks", "zeros", "powers"]}
    finished = {who: flag(who + "_finished") for who in milestones}
    said = {who: 0 for who in milestones}

    def finish(eng, who, name):
        assert milestones[who][said[who]] == name, (name, milestones[who][said[who]])
        said[who] += 1
        eng.sem_inc(finished[who], 1)

    def after(eng, who, name):
        eng.wait_ge(finished[who], milestones[who].index(name) + 1)

    per_layer = {"S": 2 * (PAIRS + 1), "gathA": PAIRS + 1, "gathB": PAIRS + 1, "xgA": PAIRS + 1, "xgB": PAIRS + 1,
                 "gate": PAIRS, "silu": PAIRS, "up": PAIRS, "h": PAIRS, "T": PAIRS, "hT": PAIRS, "Sw": PAIRS, "SwT": PAIRS,
                 "down": PAIRS, "outA": PAIRS, "outB": PAIRS,
                 "scattered": PAIRS}

    SEED = 1

    def moe_wait(eng, e, name, value):
        eng.wait_ge(flag("moe_" + name), value + ((int(e[1]) - 1) * per_layer[name] + SEED))

    heads_before = {"at1": 0, "at2": 8, "at3m": 12, "at3": 16}

    def attn_wait(eng, name, what, value):
        eng.wait_ge(flag("attn_" + what), value + 2 * heads_before[name])

    OVF_PE, OVF_VEC = 5, 11

    block = ctx.enter_context(nc.Block())
    small_sem = flag("constants_loaded")
    NSMALL = 3

    @block.sync
    def _(sp):
        sp.dma_start(x_sb[:, :, :], ins["x"].rearrange("(h p) d -> p h d", p=P)).then_inc(flag("x_loaded"), 16)
        sp.dma_start(vec[:, :], ins["vec"]).then_inc(small_sem, 16)
        sp.dma_start(wf[:, :, :], ins["wf"]).then_inc(small_sem, 16)
        sp.dma_start(brow[:, :], ins["brow"].partition_broadcast(P)).then_inc(small_sem, 16)
        load_chunk(sp, STREAM[0][0])
        for c_ in range(2):
            sp.dma_start(b_blk[:, c_, :, :], ins["b_blk"][c_]).then_inc(flag("b_loaded"), 16)
        sp.dma_start(wr[:, :, :], ins["wr"][0]).then_inc(flag("router_w"), 16)
        for c in STREAM[0][1:]:
            load_chunk(sp, c)
        for part, e in enumerate(("e1", "e2", "e3")):
            if part == 0:
                full(sp, "y", NQ - 1)
            base = moe_used[e]

            def load_pair(u, pair, i):
                for w, (hs, per, at_u) in enumerate(moe_slots(e, u)):
                    sp.wait_ge(used[hs], i * per + (base[hs] + at_u + SEED))
                    load_expert(w, hs, pair)

            def load_expert(w, hs, pair):
                expert = pair * 2 + w % 2
                sp.dma_start(moe_view(e, hs), ins[e + ("_gate", "_up", "_down")[w // 2]][expert, :, :]).then_inc(loaded[hs], 16)

            for w in ((0, 1, 2, 3, 4, 5) if part < 2 else (1, 2, 3, 4, 0, 5)):
                hs = moe_slots(e, 0)[w][0]
                full(sp, *last_use[moe_after[e][hs // 2]])
                load_expert(w, hs, 0)
            with sp.Fori(0, PAIRS // 2 - 1) as i:
                load_pair(1, i * 2 + 1, i)
                load_pair(0, i * 2 + 2, i + 1)
            load_pair(1, PAIRS - 1, PAIRS // 2 - 1)
            after(sp, "vec", e + "_items")
            n = sp.value_load(ovf[0:1, 2 * NOVF:2 * NOVF + 1], min_val=0, max_val=NOVF // 2)
            with sp.If(n > 0):
                with sp.Fori(0, n) as k:
                    for w, (hs, per, _) in enumerate(moe_slots(e, 0)):
                        expert = sp.value_load(ovf[0:1, bass.ds(k * 2 + (NOVF + w % 2), 1)], min_val=0, max_val=NE - 1)
                        sp.wait_ge(used[hs], moe_used[e][hs] + 8 * per + SEED)
                        sp.wait_ge(flag(e + "_ovf_pe"), k * OVF_PE + (2, 2, 4)[w // 2])
                        sp.dma_start(moe_view(e, hs), ins[e + ("_gate", "_up", "_down")[w // 2]][expert, :, :]).then_inc(
                            flag(e + f"_ovf_loaded{w // 2}"), 16)
                sp.wait_ge(flag("moe_sum_ready"), int(e[1]))
            if part < 2:
                for c in STREAM[part + 1]:
                    load_chunk(sp, c)
        for th, name in enumerate(("x_final0", "x_final")):
            after(sp, "vec", name)
            sp.dma_start(out[th * P:(th + 1) * P, :], x_sb[:, th, :]).then_inc(flag("stored"), 16)
        sp.wait_ge(flag("stored"), 32)

    @block.gpsimd
    def _(po):
        made = flag("pool_made")
        n = [0]

        def step(ins_):
            n[0] += 1
            ins_.then_inc(made, 1)
            po.wait_ge(made, n[0])

        step(po.memset(ident[:, :], 0.0))
        step(po.affine_select(out=ident[:, :], in_=ident[:, :], compare_op=ALU.not_equal, fill=1.0, base=0,
                              pattern=[[-1, P]], channel_multiplier=1))
        finish(po, "pool", "ident")
        step(po.memset(ones[:, :], 1.0))
        step(po.memset(before[:, :], 1.0))
        step(po.affine_select(out=before[:, :], in_=before[:, :], compare_op=ALU.is_gt, fill=0.0, base=0,
                              pattern=[[1, P]], channel_multiplier=-1))
        step(po.memset(upto[:, :, :], 1.0))
        step(po.memset(mask[:, :, :], 0.0))
        for h in range(TH):
            step(po.affine_select(out=upto[:, h, :], in_=upto[:, h, :], compare_op=ALU.is_ge, fill=0.0,
                                  base=-P * h, pattern=[[1, T]], channel_multiplier=-1))
            step(po.affine_select(out=mask[:, h, :], in_=mask[:, h, :], compare_op=ALU.is_ge, fill=MASKED,
                                  base=P * h, pattern=[[-1, T]], channel_multiplier=1))
        step(po.iota(col_id[:, :], pattern=[[1, EXTRA * NE]], base=0, channel_multiplier=0,
                     allow_small_or_imprecise_dtypes=True))
        step(po.memset(rows[:, 0, :], 1.0))
        step(po.affine_select(out=head_sel, in_=head_sel, compare_op=ALU.is_equal, fill=0.0, base=0,
                              pattern=[[-1, 8], [0, P]], channel_multiplier=1))
        step(po.memset(nF[:, :], 0.0))
        finish(po, "pool", "masks")
        step(po.memset(c_blk, 0.0))
        step(po.memset(qz1, 0.0))
        finish(po, "pool", "zeros")
        after(po, "vec", "ssm_powers2")
        pw = powers
        step(po.memset(pw[:, 0, :, 0:1], 1.0))
        step(po.memset(pw[:, 1, :, 0:1], 0.0))
        scratch = at(6144, 2, NJ * HALF_T // 2)
        for k in range(LEVELS):
            Lk = 1 << k
            er = e_pow(k, 0).unsqueeze(2).broadcast_to([P, NJ, Lk])
            ei = e_pow(k, 1).unsqueeze(2).broadcast_to([P, NJ, Lk])
            t1 = scratch[:, 0, 0:NJ * Lk].rearrange("p (j t) -> p j t", j=NJ)
            t2 = scratch[:, 1, 0:NJ * Lk].rearrange("p (j t) -> p j t", j=NJ)
            pr, pi = pw[:, 0, :, 0:Lk], pw[:, 1, :, 0:Lk]
            step(po.tensor_tensor(t1, pr, er, ALU.mult))
            step(po.tensor_tensor(t2, pi, ei, ALU.mult))
            step(po.tensor_tensor(pw[:, 0, :, Lk:2 * Lk], t1, t2, ALU.subtract))
            step(po.tensor_tensor(t1, pr, ei, ALU.mult))
            step(po.tensor_tensor(t2, pi, er, ALU.mult))
            step(po.tensor_tensor(pw[:, 1, :, Lk:2 * Lk], t1, t2, ALU.add))
        finish(po, "pool", "powers")

    @block.tensor
    def _(pe):
        mm = pe.matmul
        for name in per_layer:
            pe.sem_inc(flag("moe_" + name), SEED)
        for s in used:
            pe.sem_inc(s, SEED)
        for e in ("e1", "e2", "e3"):
            pe.sem_inc(flag(e + "_ovf_pe"), OVF_PE)

        def turn_to_T(name, src, ready=None):
            for n in range(4):
                th, kk = n // 2, n % 2
                if ready and kk == 0:
                    after(pe, "vec", ready[th])
                b = open_bank(pe, name, n)
                for k in range(4):
                    last = pe.transpose(psum[:, b, k * P:(k + 1) * P], src[:, th, (4 * kk + k) * P:(4 * kk + k + 1) * P], ident[:, :])
                close_bank(last, name, n)

        def wait_T(name):
            for n in range(4):
                evacuated(pe, name, n)

        def to_T(w, cols, name, rhs, K=KD):
            b = open_bank(pe, *name)
            for n, c in enumerate(cols):
                for k in range(K):
                    last = mm(psum[:, b, n * T:(n + 1) * T], w[:, k, c * P:(c + 1) * P], rhs[:, k, :],
                              start=(k == 0), stop=(k == K - 1))
            close_bank(last, *name)

        def to_tok(w, c0, c1, name, th, lhs, k0=0, K=KD, start=True, stop=True, close=True):
            b = open_bank(pe, *name) if start else plan[name][0]
            for k in range(K):
                last = mm(psum[:, b, 0:c1 - c0], lhs[:, k0 + k, th * P:(th + 1) * P], w[:, k, c0:c1],
                          start=(start and k == 0), stop=(stop and k == K - 1))
            if close:
                close_bank(last, *name)
            return last

        def attention(name, heads, qz, kT, v, causal, forget=False, between=iter(())):
            N = 2 * heads

            def unit(n):
                p, th, j = n // 4, n // 2 % 2, n % 2
                return 2 * p + j, th, (P if causal and th == 0 else T)

            nbuf, buf = buffers(name)
            LAG = nbuf - 1
            for n in range(N + LAG + 2):
                if n < N:
                    h, th, W = unit(n)
                    b = open_bank(pe, name, "score", n)
                    last = mm(psum[:, b, 0:W], qz[:, h, th * P:(th + 1) * P], kT(h)[:, 0:W], start=True, stop=not forget)
                    if forget:
                        last = mm(psum[:, b, 0:W], head_sel[:, h, :], nF[:, 0:W], start=False, stop=True)
                    close_bank(last, name, "score", n)
                for _ in range(2):
                    next(between, None)
                m = n - LAG - 2
                if m >= 0:
                    h, th, W = unit(m)
                    p = m // 4
                    evacuated(pe, name, "pt", m)
                    b = open_bank(pe, name, "pv", p) if m % 4 == 0 else plan[(name, "pv", p)][0]
                    for s in range(W // P):
                        last = mm(psum[(h % 2) * HD:(h % 2 + 1) * HD, b, th * P:(th + 1) * P], v(s, h),
                                  PT_buf[:, m % 2, s * P:(s + 1) * P], start=(s == 0), stop=(s == W // P - 1))
                    if m % 4 == 3:
                        close_bank(last, name, "pv", p)
                m = n - LAG
                if 0 <= m < N:
                    h, th, W = unit(m)
                    b = open_bank(pe, name, "pt", m)
                    attn_wait(pe, name, "probs", m + 1)
                    for s in range(W // P):
                        last = pe.transpose(psum[:, b, s * P:(s + 1) * P], P_buf[:, buf(m), s * P:(s + 1) * P], ident[:, :])
                    close_bank(last, name, "pt", m)
            for _ in between:
                pass

        def to_T_steps(w, cols, name, rhs):
            b = open_bank(pe, *name)
            for n, c in enumerate(cols):
                for k in range(KD):
                    last = mm(psum[:, b, n * T:(n + 1) * T], w[:, k, c * P:(c + 1) * P], rhs[:, k, :],
                              start=(k == 0), stop=(k == KD - 1))
                    if (n, k) == (len(cols) - 1, KD - 1):
                        close_bank(last, *name)
                    yield

        def residual(name, chunks, lhs):
            w = [chunk(pe, c, D) for c in chunks]
            for n in range(4):
                th, hf = n // 2, n % 2
                to_tok(w[0], hf * 512, hf * 512 + 512, (name, n), th, lhs, 0, 4, True, False, False)
                to_tok(w[1], hf * 512, hf * 512 + 512, (name, n), th, lhs, 4, 4, False, True, True)

        def moe(e, tok):
            F = 2 if e == "e1" else 4
            FW = F * P
            lbase = moe_loads[e]
            turn_to_T(e + "xT", tok, (e + "_tok0", e + "_tok"))
            pe.wait_ge(flag("router_w"), 16 * int(e[1]))
            b = open_bank(pe, e + "logits")
            for th in range(TH):
                evacuated(pe, e + "xT", 2 * th)
                evacuated(pe, e + "xT", 2 * th + 1)
                for k in range(KD):
                    last = mm(psum[:, b, th * NR:(th + 1) * NR], xT[:, k, th * P:(th + 1) * P], wr[:, k, :],
                              start=(k == 0), stop=(k == KD - 1))
            close_bank(last, e + "logits")
            after(pe, "vec", e + "_zero")
            for b in range(4):
                pe.wait_ge(bank_free[b], before_moe[e][b])
                mm(psum[:, b, :], ones[:, :], og[:, 0:512], start=True, stop=False, skip_group_check=True)
            b = open_bank(pe, e + "rank")
            after(pe, "vec", e + "_sel")
            mm(psum[:, b, 0:NE], before[:, :], sel[:, 0, :], start=True, stop=True)
            mm(psum[:, b, NE:2 * NE], ones[:, :], sel[:, 0, :], start=True, stop=False)
            mm(psum[:, b, NE:2 * NE], before[:, :], sel[:, 1, :], start=False, stop=True)
            mm(psum[:, b, 2 * NE:3 * NE], ones[:, :], sel[:, 0, :], start=True, stop=False)
            last = mm(psum[:, b, 2 * NE:3 * NE], ones[:, :], sel[:, 1, :], start=False, stop=True)
            close_bank(last, e + "rank")
            for b in range(4, 8):
                pe.wait_ge(bank_free[b], before_moe[e][b])

            def gather(par, half):
                for k in range(4):
                    for th in range(TH):
                        last = mm(psum[:, (4, 7)[half], k * 2 * CAP:(k + 1) * 2 * CAP], tok[:, th, (4 * half + k) * P:(4 * half + k + 1) * P],
                                  S[:, par, th, :], start=(th == 0), stop=(th == TH - 1))
                last.then_inc(flag(("moe_gathA", "moe_gathB")[half]), 1)

            moe_wait(pe, e, "S", 1)
            gather(0, 0)
            gather(0, 1)

            with pe.Fori(0, 8) as i:
                for u in range(2):
                    def c(k, per=1):
                        return i * (2 * per) + (u * per + k)

                    slots = moe_slots(e, u)
                    views = [moe_view(e, s[0]) for s in slots]

                    def arrived(w):
                        hs, per, at_u = slots[w]
                        pe.wait_ge(loaded[hs], i * (16 * per) + 16 * (lbase[hs] + at_u + 1))

                    moe_wait(pe, e, "xgA", c(1))
                    moe_wait(pe, e, "xgB", c(1))
                    for g in range(2):
                        if g == 0:
                            moe_wait(pe, e, "hT", c(0))
                        else:
                            moe_wait(pe, e, "SwT", c(0))
                        arrived(2 * g)
                        arrived(2 * g + 1)
                        wv = [views[2 * g + x].rearrange("p (k n) -> p k n", k=KD) for x in range(2)]
                        for k in range(KD):
                            for x in range(2):
                                last = mm(psum[x * CAP:(x + 1) * CAP, 5 + g, 0:FW], xg[:, u, k, x * CAP:(x + 1) * CAP], wv[x][:, k, :],
                                          start=(k == 0), stop=(k == KD - 1))
                                if k == KD - 1:
                                    last.then_inc(used[slots[2 * g + x][0]], 1)
                    moe_wait(pe, e, "S", c(4, 2))
                    moe_wait(pe, e, "outA", c(0))
                    gather(1 - u, 0)
                    moe_wait(pe, e, "h", c(1))
                    for f in range(F):
                        last = pe.transpose(psum[:, 5, f * P:(f + 1) * P], hh[:, f * P:(f + 1) * P], ident[:, :])
                    last.then_inc(flag("moe_T"), 1)
                    moe_wait(pe, e, "outB", c(0))
                    gather(1 - u, 1)
                    for th in range(TH):
                        last = pe.transpose(psum[:, 6, th * P:(th + 1) * P], Sw[:, u, th, :], ident[:, :])
                    last.then_inc(flag("moe_Sw"), 1)
                    moe_wait(pe, e, "hT", c(1))
                    arrived(4)
                    arrived(5)
                    wv = [views[4 + x].rearrange("p (k n) -> p k n", n=D) for x in range(2)]
                    for half in range(2):
                        moe_wait(pe, e, ("xgA", "xgB")[half], c(2))
                        for f in range(F):
                            for x in range(2):
                                last = mm(psum[x * CAP:(x + 1) * CAP, (4, 7)[half], :], hT[:, f, x * CAP:(x + 1) * CAP],
                                          wv[x][:, f, half * 512:(half + 1) * 512], start=(f == 0), stop=(f == F - 1))
                                if half and f == F - 1:
                                    last.then_inc(used[slots[4 + x][0]], 1)
                        if half == 0:
                            last.then_inc(flag("moe_down"), 1)
                    moe_wait(pe, e, "SwT", c(1))
                    moe_wait(pe, e, "outA", c(1))
                    for half in range(2):
                        if half:
                            moe_wait(pe, e, "outB", c(1))
                        for th in range(TH):
                            last = mm(psum[:, 2 * th + half, :], SwT[:, th * P:(th + 1) * P], og[:, half * 512:(half + 1) * 512],
                                      start=False, stop=False, skip_group_check=True)
                    last.then_inc(flag("moe_scattered"), 1)
            moe_wait(pe, e, "xgA", PAIRS + 1)
            moe_wait(pe, e, "xgB", PAIRS + 1)

            ovp, ovv = flag(e + "_ovf_pe"), flag(e + "_ovf_vec")
            after(pe, "vec", e + "_items")
            n = pe.value_load(ovf[0:1, 2 * NOVF:2 * NOVF + 1], min_val=0, max_val=NOVF // 2)
            with pe.If(n > 0):
                with pe.Fori(0, n) as k_:
                    pe.wait_ge(ovv, k_ * OVF_VEC + 4)
                    for half, b in enumerate((4, 7)):
                        for k in range(4):
                            for th in range(TH):
                                mm(psum[:, b, k * P:(k + 1) * P], tok[:, th, (4 * half + k) * P:(4 * half + k + 1) * P],
                                   S[:, 0, th, :], start=(th == 0), stop=(th == TH - 1))
                    for th in range(TH):
                        last = pe.transpose(psum[:, 6, th * P:(th + 1) * P], Sw[:, 0, th, :], ident[:, :])
                    last.then_inc(ovp, 1)
                    pe.wait_ge(ovv, k_ * OVF_VEC + 7)
                    for g in range(2):
                        pe.wait_ge(flag(e + f"_ovf_loaded{g}"), k_ * 32 + 32)
                        wv = [moe_view(e, moe_slots(e, 0)[2 * g + x][0]).rearrange("p (k n) -> p k n", k=KD) for x in range(2)]
                        for k in range(KD):
                            for x in range(2):
                                last = mm(psum[x * CAP:(x + 1) * CAP, 5 + g, 0:FW], xg[:, 0, k, x * CAP:(x + 1) * CAP], wv[x][:, k, :],
                                          start=(k == 0), stop=(k == KD - 1))
                    last.then_inc(ovp, 1)
                    pe.wait_ge(ovv, k_ * OVF_VEC + 8)
                    for f in range(F):
                        last = pe.transpose(psum[:, 5, f * P:(f + 1) * P], hh[:, f * P:(f + 1) * P], ident[:, :])
                    last.then_inc(ovp, 1)
                    pe.wait_ge(ovv, k_ * OVF_VEC + 9)
                    pe.wait_ge(flag(e + "_ovf_loaded2"), k_ * 32 + 32)
                    wv = [moe_view(e, moe_slots(e, 0)[4 + x][0]).rearrange("p (k n) -> p k n", n=D) for x in range(2)]
                    for half, b in enumerate((4, 7)):
                        for f in range(F):
                            for x in range(2):
                                last = mm(psum[x * CAP:(x + 1) * CAP, b, :], hT[:, f, x * CAP:(x + 1) * CAP],
                                          wv[x][:, f, half * 512:(half + 1) * 512], start=(f == 0), stop=(f == F - 1))
                    last.then_inc(ovp, 1)
                    pe.wait_ge(ovv, k_ * OVF_VEC + 11)
                    for half in range(2):
                        for th in range(TH):
                            last = mm(psum[:, 2 * th + half, :], SwT[:, th * P:(th + 1) * P], og[:, half * 512:(half + 1) * 512],
                                      start=False, stop=False, skip_group_check=True)
                    last.then_inc(ovp, 1)
                    pe.wait_ge(ovp, k_ * OVF_PE + 2 * OVF_PE)
            moe_wait(pe, e, "scattered", PAIRS)
            pe.sem_inc(flag("moe_sum_ready"), 1)

        after(pe, "pool", "ident")
        after(pe, "vec", "h_tok")
        turn_to_T("hT", h_tok)
        wait_T("hT")
        w = chunk(pe, "u", 512)
        to_T(w, (0, 1), ("u", 0), xT)
        to_T(w, (2, 3), ("u", 1), xT)

        def ssm_in(q):
            for c_ in range(2):
                for hb in range(2):
                    bank = 2 + 2 * c_ + hb
                    open_bank(pe, "bu", q, bank)
                    for jj in (2 * hb, 2 * hb + 1):
                        last = mm(psum[:, bank, (jj % 2) * T:(jj % 2 + 1) * T], b_blk[:, c_, 4 * q + jj, :], uT[:, q, :],
                                  start=True, stop=True)
                    close_bank(last, "bu", q, bank)

        def ssm_out(q):
            b = open_bank(pe, "y", q)
            for half in range(2):
                after(pe, "vec", f"ssm_state{2 * q + half}")
                for jj in range(4):
                    for c_ in range(2):
                        last = mm(psum[:, b, half * HALF_T:(half + 1) * HALF_T], c_blk[:, c_, 4 * q + jj, :], ws[:, half, c_, jj, :],
                                  start=(jj == 0 and c_ == 0), stop=(jj == 3 and c_ == 1))
                last.then_inc(flag("ssm_y"), 1)
            pe.wait_ge(flag("ssm_y"), 2 * q + 2)
            pe.sem_inc(bank_full[b], 1)

        def gate(n):
            w = chunk(pe, f"g{n // 2}", 512)
            to_T(w, (2 * (n % 2), 2 * (n % 2) + 1), ("gate", n), xT)

        def project(name):
            w = chunk(pe, name, 512)
            for th in range(TH):
                to_tok(w, 0, 512, (name, th), th, xT)

        pe.wait_ge(flag("b_loaded"), 32)
        evacuated(pe, "u", 0)
        ssm_in(0)
        evacuated(pe, "u", 1)
        project("q")
        project("k")
        ssm_in(1)
        ssm_out(0)
        pe.wait_ge(small_sem, 16 * NSMALL)
        b = open_bank(pe, "f")
        for th in range(TH):
            for k in range(KD):
                last = mm(psum[:, b, th * 8:(th + 1) * 8], xT[:, k, th * P:(th + 1) * P], wf[:, k, :],
                          start=(k == 0), stop=(k == KD - 1))
        close_bank(last, "f")
        project("v")
        after(pe, "pool", "masks")
        after(pe, "vec", "logf")
        b = open_bank(pe, "F")
        mm(psum[:, b, 0:8], upto[:, 0, 0:P], lf[:, 0, 0, :], start=True, stop=True)
        mm(psum[:, b, 8:16], upto[:, 0, P:T], lf[:, 0, 0, :], start=True, stop=False)
        mm(psum[:, b, 8:16], upto[:, 1, P:T], lf[:, 0, 1, :], start=False, stop=True)
        mm(psum[0:8, b, 128:128 + T], lf[:, 1, 0, :], upto[:, 0, :], start=True, stop=False)
        last = mm(psum[0:8, b, 128:128 + T], lf[:, 1, 1, :], upto[:, 1, :], start=False, stop=True)
        close_bank(last, "F")
        gate(0)
        ssm_in(2)
        ssm_out(1)
        gate(1)
        ssm_in(3)
        gate(2)
        ssm_out(2)
        gate(3)
        for w_, c0 in (("qT", 0), ("kT", 512)):
            after(pe, "vec", "qk_tok")
            for th in range(TH):
                b = open_bank(pe, w_, th)
                for k in range(4):
                    last = pe.transpose(psum[:, b, k * P:(k + 1) * P], qk_tok[:, th, c0 + k * P:c0 + (k + 1) * P], ident[:, :])
                close_bank(last, w_, th)
        gate(4)
        ssm_out(3)
        gate(5)

        def last_gates():
            w = chunk(pe, "g3", 512)
            for n in (6, 7):
                yield from to_T_steps(w, (2 * (n % 2), 2 * (n % 2) + 1), ("gate", n), xT)

        for name in ("qT", "kT"):
            for th in range(TH):
                evacuated(pe, name, th)
        evacuated(pe, "F")
        evacuated(pe, "v", 0)
        evacuated(pe, "v", 1)
        attention("at1", 8, qz1, lambda h: kT1[:, h // 2, :], lambda s, h: v_tok[:, s, h * HD:(h + 1) * HD], True, True,
                  between=last_gates())
        w = chunk(pe, "glu", 512)
        pe.wait_ge(flag("gelu"), NQ)
        to_T(w, (0, 1), ("glu", 0), yg, K=4)
        to_T(w, (2, 3), ("glu", 1), yg, K=4)
        for p in range(4):
            evacuated(pe, "at1", "pv", p)
        wa, ws_ = chunk(pe, "pa", D), chunk(pe, "ps", D)
        for n in range(4):
            to_T(wa, (2 * n, 2 * n + 1), ("pa", n), ya, K=4)
            if n == 0:
                after(pe, "vec", "y_ssm")
            to_T(ws_, (2 * n, 2 * n + 1), ("ps", n), y_ssm, K=4)
        pe.wait_ge(flag("mem_loaded"), 16)
        turn_to_T("memT", mem_tok)
        pe.wait_ge(flag("mixed"), 4)
        residual("res1", ("wo0", "wo1"), mixedT)
        wait_T("memT")
        w = chunk(pe, "memkv", 512)
        to_T(w, (0, 1), ("memk",), memT)
        for th in range(TH):
            to_tok(w, 256, 512, ("memv", th), th, memT)
        moe("e1", xh)

        turn_to_T("x2T", x_sb, ("x2_0", "x2"))
        wait_T("x2T")
        w = chunk(pe, "c3", 512)
        to_T(w, (0, 1), ("qm2",), xT)

        def conv_in(n):
            w = chunk(pe, f"c{n // 2}", 512)
            to_T(w, (2 * (n % 2), 2 * (n % 2) + 1), ("conv", n), xT)

        for n in range(MT):
            conv_in(n)
        evacuated(pe, "qm2")
        evacuated(pe, "memk")
        evacuated(pe, "memv", 0)
        evacuated(pe, "memv", 1)

        def depthwise(n):
            after(pe, "vec", f"glu_in{n}")
            b = open_bank(pe, "depthwise", n)
            for k in range(TAPS):
                pe.wait_ge(flag("diag_made"), (n - VEC_TILES) * TAPS + k + 1)
                last = mm(psum[:, b, 0:T], diag[:, k, :], hpad[:, n, k:k + T], start=(k == 0), stop=(k == TAPS - 1))
                if k == TAPS - 1:
                    close_bank(last, "depthwise", n)
                elif n < MT - 1:
                    last.then_inc(flag("diag_used"), 1)
                yield

        attention("at2", 4, qz2, lambda h: mem_k[:, h // 2, :], lambda s, h: mem_v[:, s, h * HD:(h + 1) * HD], False,
                  between=depthwise(VEC_TILES))
        for n in range(VEC_TILES + 1, MT):
            for _ in depthwise(n):
                pass

        for n in range(VEC_TILES, MT):
            evacuated(pe, "depthwise", n)
        after(pe, "vec", "conv_done")
        b = open_bank(pe, "mean")
        for k in range(MT):
            last = mm(psum[:, b, 0:T], ones[:, :], conv[:, k, :], start=(k == 0), stop=(k == MT - 1))
        close_bank(last, "mean")
        b = open_bank(pe, "var")
        for k in range(MT):
            if k % 2 == 0:
                pe.wait_ge(flag("conv_sq"), k // 2 + 1)
            last = mm(psum[:, b, 0:T], ones[:, :], sq[:, k, :], start=(k == 0), stop=(k == MT - 1))
        close_bank(last, "var")
        for p in range(2):
            evacuated(pe, "at2", "pv", p)
        w = [chunk(pe, c, D) for c in ("w2o0", "w2o1")]
        for ks in (range(MT, KD), range(MT)):
            for n in range(4):
                th, hf = n // 2, n % 2
                b = open_bank(pe, "res2", n) if ks[0] else plan[("res2", n)][0]
                for k in ks:
                    if ks[0] == 0 and n == 0:
                        pe.wait_ge(flag("conv_out"), k + 1)
                    last = mm(psum[:, b, :], yT[:, k, th * P:(th + 1) * P], w[k // 4][:, k % 4, hf * 512:(hf + 1) * 512],
                              start=(k == MT), stop=(k == MT - 1))
                if ks[0] == 0:
                    close_bank(last, "res2", n)
        moe("e2", x_sb)

        turn_to_T("x3T", x_sb, ("x3_0", "x3"))
        wait_T("x3T")
        w = chunk(pe, "m4", 512)
        to_T(w, (2, 3), ("qm3",), xT)
        for th in range(TH):
            to_tok(w, 0, 256, ("mv1", th), th, xT)
        w = chunk(pe, "m0", 512)
        to_T(w, (0, 1), ("mq", 0), xT)
        evacuated(pe, "qm3")

        def more_projections():
            yield from to_T_steps(chunk(pe, "m0", 512), (2, 3), ("mq", 1), xT)
            yield from to_T_steps(chunk(pe, "m1", 512), (0, 1), ("mq", 2), xT)

        attention("at3m", 4, qz3m, lambda h: mem_k[:, h // 2, :], lambda s, h: mem_v[:, s, h * HD:(h + 1) * HD], False,
                  between=more_projections())
        w = chunk(pe, "m1", 512)
        to_T(w, (2, 3), ("mk", 0), xT)
        w = chunk(pe, "m2", 512)
        to_T(w, (0, 1), ("mk", 1), xT)
        to_T(w, (2, 3), ("mk", 2), xT)
        w = chunk(pe, "m3", 512)
        for th in range(TH):
            to_tok(w, 0, 512, ("mv0", th), th, xT)
        for n in range(3):
            evacuated(pe, "mq", n)
            evacuated(pe, "mk", n)
        for th in range(TH):
            evacuated(pe, "mv0", th)
            evacuated(pe, "mv1", th)

        w3o = [chunk(pe, c, D) for c in ("w3o0", "w3o1")]

        def project_out(n, k, started):
            th, hf = n // 2, n % 2
            b = plan[("res3", n)][0] if started else open_bank(pe, "res3", n)
            return mm(psum[:, b, :], yT[:, k, th * P:(th + 1) * P], w3o[k // 4][:, k % 4, hf * 512:(hf + 1) * 512],
                      start=not started, stop=(k == MT - 1))

        def first_outputs():
            for p in range(2):
                evacuated(pe, "at3m", "pv", p)
            for k in (6, 7):
                for n in range(2):
                    project_out(n, k, k > 6)
                    yield
            for _ in range(2 * NBUF + 6):
                yield
            for k in range(MT):
                for _ in range(6 if k else 0):
                    yield
                evacuated(pe, "at3", "pv", k)
                for n in range(2):
                    last = project_out(n, k, True)
                    if k == MT - 1:
                        close_bank(last, "res3", n)
                    yield

        attention("at3", 12, qz3, lambda h: kT3[:, h // 2, :], lambda s, h: v3[:, s, h * HD:(h + 1) * HD], True,
                  between=first_outputs())
        for n in range(2, 4):
            for k in (6, 7, *range(MT)):
                last = project_out(n, k, k != 6)
            close_bank(last, "res3", n)
        moe("e3", x_sb)

    @block.scalar
    def _(ac):
        act = ac.activation
        chain = flag("act_chain")
        n_chain = [0]

        def step(ins_):
            n_chain[0] += 1
            ins_.then_inc(chain, 1)
            ac.wait_ge(chain, n_chain[0])

        def copy_out(name, dst, src):
            read_out(act(dst, src, ACT.Copy), *name)

        def attention(name, heads, out_T):
            N = 2 * heads

            def width(n):
                return P if name in ("at1", "at3") and n // 2 % 2 == 0 else T

            nbuf, buf = buffers(name)
            LAG = nbuf - 1
            for n in range(N + LAG + 2):
                if n < N:
                    W = width(n)
                    attn_wait(ac, name, "logits", n + 1)
                    act(P_buf[:, buf(n), 0:W], P_buf[:, buf(n), 0:W], ACT.Exp, bias=nmax[:, buf(n):buf(n) + 1],
                        accum_out=psums[:, buf(n):buf(n) + 1]).then_inc(flag("attn_exp"), 1)
                m = n - LAG
                if 0 <= m < N:
                    W = width(m)
                    src = full(ac, name, "pt", m)
                    copy_out((name, "pt", m), PT_buf[:, m % 2, 0:W], src[:, 0:W])
                m = n - LAG - 2
                if m >= 0 and m % 4 == 3:
                    p = m // 4
                    src = full(ac, name, "pv", p)
                    copy_out((name, "pv", p), out_T[:, p, :], src[:, 0:T])

        def moe(e):
            F = 2 if e == "e1" else 4
            FW = F * P

            def gathered(par):
                act(xg[:, par, 0:4, :], psum[:, 4, :].rearrange("p (k c) -> p k c", k=4), ACT.Copy).then_inc(flag("moe_xgA"), 1)

            take_T(e + "xT")
            after(ac, "vec", e + "_gd")
            step(act(r_ge, r_gd, ACT.Exp))
            finish(ac, "act", e + "_ge")
            after(ac, "vec", e + "_d21")
            step(act(r_p2, r_d21, ACT.Exp))
            finish(ac, "act", e + "_p2")
            if e != "e3":
                ac.dma_start(wr[:, :, :], ins["wr"][int(e[1])]).then_inc(flag("router_w"), 16)

            moe_wait(ac, e, "gathA", 1)
            gathered(0)
            with ac.Fori(0, 8) as i:
                for u in range(2):
                    def c(k, per=1):
                        return i * (2 * per) + (u * per + k)

                    hs, per, at_u = moe_slots(e, u)[1]
                    ac.wait_ge(used[hs], i * per + (moe_used[e][hs] + at_u + 1 + SEED))
                    act(sg[:, 0:FW], psum[:, 5, 0:FW], ACT.Silu).then_inc(flag("moe_silu"), 1)
                    moe_wait(ac, e, "gathA", c(2))
                    gathered(1 - u)
                    moe_wait(ac, e, "T", c(1))
                    act(hT[:, 0:F, :], psum[:, 5, 0:FW].rearrange("p (f c) -> p f c", f=F), ACT.Copy).then_inc(flag("moe_hT"), 1)
                    moe_wait(ac, e, "down", c(1))
                    act(og[:, 0:512], psum[:, 4, :], ACT.Copy).then_inc(flag("moe_outA"), 1)
            after(ac, "vec", e + "_items")
            n = ac.value_load(ovf[0:1, 2 * NOVF:2 * NOVF + 1], min_val=0, max_val=NOVF // 2)
            with ac.If(n > 0):
                with ac.Fori(0, n) as k_:
                    ac.wait_ge(flag(e + "_ovf_pe"), k_ * OVF_PE + (OVF_PE + 2))
                    act(sg[:, 0:FW], psum[:, 5, 0:FW], ACT.Silu).then_inc(flag(e + "_ovf_silu"), 1)

        def rms_norm(squares, got):
            for th in range(TH):
                step(act(squares, x_sb[:, th, :], ACT.Square, accum_out=rms_ms[:, th:th + 1]))
            finish(ac, "act", got + "_sq")
            after(ac, "vec", got + "_ms")
            step(act(rms_r, rms_r, ACT.Sqrt))
            finish(ac, "act", got + "_rms")

        ac.wait_ge(flag("x_loaded"), 16)
        rms_norm(square_junk, "x")
        def take_T(name):
            for n in (1, 3):
                src = full(ac, name, n).rearrange("p (k t) -> p k t", k=4)
                copy_out((name, n), xT[:, 4:8, (n // 2) * P:(n // 2 + 1) * P], src)

        ac.wait_ge(small_sem, 16 * NSMALL)
        step(act(s_dt, V("log_dt"), ACT.Exp))
        finish(ac, "act", "ssm_dt")
        after(ac, "vec", "ssm_adt")
        step(act(s_mag, s_adt, ACT.Exp))
        finish(ac, "act", "ssm_mag")
        after(ac, "vec", "ssm_angle")
        step(act(e_tab[:, 0, :, :].rearrange("p c j -> p (c j)"), s_ang, ACT.Sin))
        finish(ac, "act", "ssm_sin")

        for n in range(2):
            src = full(ac, "u", n)
            copy_out(("u", n), uT[:, 2 * n:2 * n + 2, :], src.rearrange("p (a t) -> p a t", a=2))
        after(ac, "vec", "qk_ms")
        step(act(qk_r, qk_r, ACT.Sqrt))
        finish(ac, "act", "qk_rms")
        after(ac, "vec", "f_abs")
        step(act(f_e, f_abs, ACT.Exp, scale=-1.0))
        step(act(f_l, f_e, ACT.Ln, bias=1.0))
        finish(ac, "act", "f_ln")
        for th in range(TH):
            src = full(ac, "v", th)
            copy_out(("v", th), v_tok[:, th, :], src)
        def take_gate(n):
            src = full(ac, "gate", n)
            read_out(act(gates[:, 2 * n:2 * n + 2, :], src.rearrange("p (a t) -> p a t", a=2), ACT.Sigmoid), "gate", n)

        for n in range(6):
            if n == 4:
                full(ac, "kT", TH - 1)
            take_gate(n)
        for q in range(NQ):
            evacuated(ac, "y", q)
            act(yg[:, q, :], yg[:, q, :], ACT.Gelu_apprx_tanh).then_inc(flag("gelu"), 1)
        attention("at1", 8, ya)
        take_gate(6)
        take_gate(7)
        ac.dma_start(gain, ins["rows"][0:1, :].partition_broadcast(P)).then_inc(flag("gain_loaded"), 16)
        for n in range(2):
            src = full(ac, "glu", n)
            read_out(act(y_ssm[:, 2 * n:2 * n + 2, :], src.rearrange("p (a t) -> p a t", a=2), ACT.Sigmoid), "glu", n)
        ac.dma_start(mem_tok, ins["mem"].rearrange("(h p) d -> p h d", p=P)).then_inc(flag("mem_loaded"), 16)
        after(ac, "vec", "x1")
        rms_norm(junk, "x1")
        src = full(ac, "memk")
        copy_out(("memk",), mem_k[:, :, :], src.rearrange("p (a t) -> p a t", a=2))
        for th in range(TH):
            src = full(ac, "memv", th)
            copy_out(("memv", th), mem_v[:, th, :], src[:, 0:256])
        moe("e1")

        def load_rows(a):
            for r in range(2):
                ac.dma_start(rows[:, r, :], ins["rows"][a + r:a + r + 1, :].partition_broadcast(P)).then_inc(flag(f"rows{a}"), 16)

        take_T("x2T")
        def make_diag(n, k):
            w = V("dw_w")[:, n * TAPS + k:n * TAPS + k + 1]
            act(diag[:, k, :], ident[:, :], ACT.Copy, scale=w).then_inc(flag("diag_made"), 1)

        for k in range(TAPS):
            make_diag(VEC_TILES, k)
        for n in range(MT):
            full(ac, "conv", n)
            step(act(gatez[:, n, :], psum[:, plan[("conv", n)][0], T:2 * T], ACT.Sigmoid))
            finish(ac, "act", f"conv_gate{n}")
        attention("at2", 4, yT[:, MT:KD, :])
        load_rows(1)
        for n in range(VEC_TILES, MT):
            if n > VEC_TILES:
                for k in range(TAPS):
                    if k < TAPS - 1:
                        ac.wait_ge(flag("diag_used"), (n - VEC_TILES - 1) * (TAPS - 1) + k + 1)
                    else:
                        full(ac, "depthwise", n - 1)
                    make_diag(n, k)
        for n in range(VEC_TILES, MT):
            src = full(ac, "depthwise", n)
            read_out(act(conv[:, n, :], src[:, 0:T], ACT.Identity, bias=V("dw_b")[:, n:n + 1]), "depthwise", n)
        for n in range(0, MT, 2):
            after(ac, "vec", f"conv_off{n}")
            act(sq[:, n:n + 2, :], conv[:, n:n + 2, :], ACT.Square).then_inc(flag("conv_sq"), 1)
        after(ac, "vec", "conv_var")
        step(act(stat[:, 1, :], stat[:, 1, :], ACT.Sqrt))
        finish(ac, "act", "conv_std")
        for n in range(MT):
            ac.wait_ge(flag("conv_norm"), n + 1)
            act(yT[:, n, :], conv[:, n, :], ACT.Silu, bias=V("ln_b")[:, n:n + 1], scale=V("ln_g")[:, n:n + 1]).then_inc(flag("conv_out"), 1)

        def layer_norm(name):
            after(ac, "vec", name + "_var")
            step(act(ln_r, ln_r, ACT.Sqrt))
            finish(ac, "act", name + "_std")

        layer_norm("ln21")
        after(ac, "vec", "e2_tok")
        load_rows(3)
        moe("e2")
        layer_norm("ln22")

        take_T("x3T")
        for th in range(TH):
            src = full(ac, "mv1", th)
            copy_out(("mv1", th), v3[:, th, 512:768], src[:, 0:256])
        attention("at3m", 4, yT[:, MT:KD, :])
        for n in range(3):
            src = full(ac, "mk", n)
            copy_out(("mk", n), kT3[:, 2 * n:2 * n + 2, :], src.rearrange("p (a t) -> p a t", a=2))
        for th in range(TH):
            src = full(ac, "mv0", th)
            copy_out(("mv0", th), v3[:, th, 0:512], src)
        attention("at3", 12, yT[:, 0:MT, :])
        load_rows(5)
        layer_norm("ln31")
        after(ac, "vec", "e3_tok")
        load_rows(7)
        moe("e3")
        layer_norm("ln32")

    @block.vector
    def _(ve):
        chain = flag("vec_chain")
        n_chain = [0]
        tt, ts, stt = ve.tensor_tensor, ve.tensor_scalar, ve.scalar_tensor_tensor

        def step(ins_):
            n_chain[0] += 1
            ins_.then_inc(chain, 1)
            ve.wait_ge(chain, n_chain[0])

        def counted(ins_):
            n_chain[0] += 1
            ins_.then_inc(chain, 1)
            return n_chain[0]

        def tell(name):
            finish(ve, "vec", name)

        def over(a, *shape):
            while len(a.shape) < len(shape):
                a = a.unsqueeze(len(a.shape))
            return a.broadcast_to(list(shape))

        def rows_over(a, n):
            return a.unsqueeze(1).broadcast_to([P, n, a.shape[1]])

        def take_T(name, scale=None):
            for n in range(4):
                th, kk = n // 2, n % 2
                if kk and name not in ("hT", "memT"):
                    continue
                src = full(ve, name, n).rearrange("p (k t) -> p k t", k=4)
                dst = (memT if name == "memT" else xT)[:, 4 * kk:4 * kk + 4, th * P:(th + 1) * P]
                if scale is None:
                    read_out(ve.tensor_copy(dst, src), name, n)
                else:
                    read_out(tt(dst, src, over(scale[:, 4 * kk:4 * kk + 4], P, 4, P), ALU.mult), name, n)

        def split_heads(name, dst, src, j0, s1, s2=None):
            nt = src.shape[1]
            d = dst.rearrange("p (j o) t -> p j o t", o=2)
            for o in range(2):
                r = slice(o * HD, (o + 1) * HD)
                sc = s1[r] if s1 is not None else 1.0
                last = ts(d[r, j0:j0 + nt, o, :], src[r], sc, s2 if s2 is not None else 1.0, ALU.mult, ALU.mult)
                if o == 0:
                    step(last)
            read_out(last, *name)

        def attention(name, heads, op, scalar, causal):
            N = 2 * heads

            def unit(n):
                p, th, j = n // 4, n // 2 % 2, n % 2
                return 2 * p + j, th, (P if causal and th == 0 else T)

            nbuf, buf = buffers(name)
            for n in range(N + 2):
                if n < N:
                    h, th, W = unit(n)
                    src = full(ve, name, "score", n)[:, 0:W]
                    if n >= nbuf:
                        full(ve, name, "pt", n - nbuf)
                    dst = P_buf[:, buf(n), 0:W]
                    if causal:
                        ins_ = stt(out=dst, in0=src, scalar=scalar(h, th), in1=mask[:, th, 0:W], op0=op, op1=ALU.add)
                    else:
                        ins_ = ts(dst, src, scalar(h, th), None, op)
                    read_out(ins_, name, "score", n)
                m = n - 2
                if m >= 0:
                    attn_wait(ve, name, "exp", m + 1)
                    inverted = counted(ve.reciprocal(precip[:, buf(m):buf(m) + 1], psums[:, buf(m):buf(m) + 1]))
                if n < N:
                    evacuated(ve, name, "score", n)
                    ve.tensor_reduce(nmax[:, buf(n):buf(n) + 1], dst, AX.X, ALU.max, negate=True).then_inc(flag("attn_logits"), 1)
                if m >= 0:
                    Wm = unit(m)[2]
                    ve.wait_ge(chain, inverted)
                    ts(P_buf[:, buf(m), 0:Wm], P_buf[:, buf(m), 0:Wm], precip[:, buf(m):buf(m) + 1], None, ALU.mult).then_inc(flag("attn_probs"), 1)

        def stats(n):
            th, hf = n // 2, n % 2
            step(ve.bn_stats(bn6[:, th, hf, :], x_sb[:, th, hf * 512:(hf + 1) * 512]))

        def residual(name, alpha, normed):
            for n in range(4):
                th, hf = n // 2, n % 2
                src = full(ve, name, n)
                dst = x_sb[:, th, hf * 512:(hf + 1) * 512]
                read_out(stt(out=dst, in0=dst, scalar=alpha, in1=src, op0=ALU.mult, op1=ALU.add), name, n)
                evacuated(ve, name, n)
                if normed:
                    stats(n)

        def moe_sum(e, alpha, normed):
            ve.wait_ge(flag("moe_sum_ready"), int(e[1]))
            for n in range(4):
                th, hf = n // 2, n % 2
                dst = x_sb[:, th, hf * 512:(hf + 1) * 512]
                step(stt(out=dst, in0=dst, scalar=alpha, in1=psum[:, n, :], op0=ALU.mult, op1=ALU.add))
                if normed:
                    stats(n)
                elif hf:
                    tell(("x2_0", "x2")[th])

        def layer_norm(name, a, results):
            for th in range(TH):
                n = counted(ve.bn_aggr(bn2[:, th, :], bn6[:, th, :, :]))
            ve.wait_ge(chain, n)
            step(ts(ln_r, bn2[:, :, 1], 1e-5, None, ALU.add))
            tell(name + "_var")
            after(ve, "act", name + "_std")
            step(ve.reciprocal(ln_r, ln_r))
            ve.wait_ge(flag(f"rows{a}"), 32)
            for th in range(TH):
                xh_ = x_sb[:, th, :]
                step(stt(out=xh_, in0=xh_, scalar=bn2[:, th, 0:1], in1=rows[:, 0, :], op0=ALU.subtract, op1=ALU.mult))
                step(stt(out=xh_, in0=xh_, scalar=ln_r[:, th:th + 1], in1=rows[:, 1, :], op0=ALU.mult, op1=ALU.add))
                tell(results[th])

        def rms_norm(name, dst, by=None, results=None):
            after(ve, "act", name + "_sq")
            step(ts(rms_r, rms_ms, 1.0 / D, 1e-6, ALU.mult, ALU.add))
            tell(name + "_ms")
            after(ve, "act", name + "_rms")
            step(ve.reciprocal(rms_r, rms_r))
            for th in range(TH):
                r_ = rms_r[:, th:th + 1]
                if by is None:
                    step(ts(dst[:, th, :], x_sb[:, th, :], r_, None, ALU.mult))
                else:
                    step(stt(out=dst[:, th, :], in0=x_sb[:, th, :], scalar=r_, in1=by, op0=ALU.mult, op1=ALU.mult))
                    tell(results[th])

        def moe(e):
            F = 2 if e == "e1" else 4
            FW = F * P
            n_e = int(e[1]) - 1
            step(ve.memset(og[:, 0:512], 0.0))
            tell(e + "_zero")
            take_T(e + "xT")
            src = full(ve, e + "logits")[:, 0:TH * NR].rearrange("p (h n) -> p h n", h=TH)
            read_out(tt(r_L, src, rows_over(brow[:, 8 + n_e * NR:8 + (n_e + 1) * NR], TH), ALU.add), e + "logits")
            evacuated(ve, e + "logits")
            step(ve.tensor_reduce(r_gmax, r_L[:, :, 0:NG], AX.X, ALU.max))
            step(tt(r_gd, r_L[:, :, 0:NG], over(r_gmax, P, TH, NG), ALU.subtract))
            tell(e + "_gd")

            def first_max(x, top, eq, cand, first, onehot, n):
                step(tt(eq, x, over(top, P, TH, n), ALU.is_equal))
                step(stt(out=cand, in0=eq, scalar=-100.0, in1=rows_over(col_id[:, 0:n], TH), op0=ALU.mult, op1=ALU.add))
                step(ve.tensor_reduce(first, cand, AX.X, ALU.min))
                step(tt(onehot, cand, over(first, P, TH, n), ALU.is_equal))

            first_max(r_L[:, :, 0:NG], r_gmax, r_geq, r_gc, r_gfirst, r_goh, NG)
            step(ts(r_pen, r_goh, -1.0, 1e30, ALU.add, ALU.mult))
            step(tt(r_EL.rearrange("p h (g x) -> p h g x", g=NG), r_L[:, :, NG:NR].rearrange("p h (g x) -> p h g x", g=NG),
                    over(r_pen, P, TH, NG, EPG), ALU.add))
            step(ve.tensor_reduce(r_m1, r_EL, AX.X, ALU.max))
            first_max(r_EL, r_m1, r_eq, r_cand, r_f1, r_oh1, NE)
            step(stt(out=r_EL, in0=r_oh1, scalar=-3e38, in1=r_EL, op0=ALU.mult, op1=ALU.add))
            step(ve.tensor_reduce(r_m2, r_EL, AX.X, ALU.max))
            first_max(r_EL, r_m2, r_eq, r_cand, r_f2, r_oh2, NE)
            step(tt(sel, r_oh1, r_oh2, ALU.add))
            tell(e + "_sel")
            step(tt(r_d21, r_m2, r_m1, ALU.subtract))
            tell(e + "_d21")
            after(ve, "act", e + "_ge")
            step(ve.tensor_reduce(r_gs, r_ge, AX.X, ALU.add))
            step(ve.reciprocal(r_gw, r_gs))
            after(ve, "act", e + "_p2")
            step(ts(r_rd, r_p2, 1.0, None, ALU.add))
            step(ve.reciprocal(r_rd, r_rd))
            step(tt(r_w1, r_gw, r_rd, ALU.mult))
            step(tt(r_w2, r_w1, r_p2, ALU.mult))
            step(ve.memset(wcomb, 0.0))
            step(ve.memset(rank, -1.0))
            step(tt(r_t, r_oh1, over(r_w1, P, TH, NE), ALU.mult))
            step(tt(r_cand, r_oh2, over(r_w2, P, TH, NE), ALU.mult))
            step(tt(wcomb[:, :, 0:NE], r_t, r_cand, ALU.add))
            src = full(ve, e + "rank")
            step(stt(out=r_t, in0=src[:, 0:2 * NE].rearrange("p (h n) -> p h n", h=TH), scalar=1.0, in1=sel, op0=ALU.add, op1=ALU.mult))
            step(ts(rank[:, :, 0:NE], r_t, -1.0, None, ALU.add))
            read_out(ve.tensor_copy(r_cnt, src[:, 2 * NE:3 * NE]), e + "rank")

            def one_hot(par, j):
                s4 = S[:, par, :, :].rearrange("p h (x c) -> p h x c", x=2)
                sw4 = Sw[:, par, :, :].rearrange("p h (x c) -> p h x c", x=2)
                ids = col_id[:, 0:CAP].unsqueeze(1).unsqueeze(1).broadcast_to([P, TH, 2, CAP])
                tt(s4, ids, over(rank[:, :, bass.ds(j * 2, 2)], P, TH, 2, CAP), ALU.is_equal).then_inc(flag("moe_S"), 1)
                moe_wait(ve, e, "S", j * 2 + 1)
                tt(sw4, s4, over(wcomb[:, :, bass.ds(j * 2, 2)], P, TH, 2, CAP), ALU.mult).then_inc(flag("moe_S"), 1)

            def gathered(par):
                ve.tensor_copy(xg[:, par, 4:8, :], psum[:, 7, :].rearrange("p (k c) -> p k c", k=4)).then_inc(flag("moe_xgB"), 1)

            one_hot(0, 0)
            moe_wait(ve, e, "gathB", 1)
            gathered(0)

            def pair_(u, pair, i):
                one_hot(1 - u, pair + 1)
                hs, per, at_u = moe_slots(e, u)[3]
                ve.wait_ge(used[hs], i * per + (moe_used[e][hs] + at_u + 1 + SEED))
                moe_wait(ve, e, "silu", pair + 1)
                tt(hh[:, 0:FW], sg[:, 0:FW], psum[:, 6, 0:FW], ALU.mult).then_inc(flag("moe_h"), 1)
                moe_wait(ve, e, "gathB", pair + 2)
                gathered(1 - u)
                moe_wait(ve, e, "Sw", pair + 1)
                ve.tensor_copy(SwT[:, :], psum[:, 6, 0:T]).then_inc(flag("moe_SwT"), 1)
                hs, per, at_u = moe_slots(e, u)[5]
                ve.wait_ge(used[hs], i * per + (moe_used[e][hs] + at_u + 1 + SEED))
                ve.tensor_copy(og[:, 512:1024], psum[:, 7, :]).then_inc(flag("moe_outB"), 1)

            pair_(0, 0, 0)
            evacuated(ve, e + "rank")
            step(ve.memset(rank3, -1.0))
            step(ve.memset(wcomb3, 0.0))
            for p in range(EXTRA):
                step(ts(r_over[:, p, :], r_cnt, float((p + 1) * CAP), None, ALU.is_gt))
                step(ve.tensor_copy(r_expert[:, p, :], col_id[:, 0:NE]))
                step(ts(rank3[:, :, p * NE:(p + 1) * NE], rank[:, :, 0:NE], -float((p + 1) * CAP), None, ALU.add))
                step(ve.tensor_copy(wcomb3[:, :, p * NE:(p + 1) * NE], wcomb[:, :, 0:NE]))
            over_flat = r_over.rearrange("p a b -> p (a b)")
            expert_flat = r_expert.rearrange("p a b -> p (a b)")
            step(ve.tensor_tensor_scan(r_pos, ones[:, 0:EXTRA * NE], over_flat, 0.0, ALU.mult, ALU.add))
            step(ve.tensor_copy(r_total, r_pos[:, EXTRA * NE - 1:EXTRA * NE]))
            step(tt(r_pos, r_pos, over_flat, ALU.mult))
            step(tt(item_eq, rows_over(r_pos, NOVF), over(col_id[:, 1:1 + NOVF], P, NOVF, EXTRA * NE), ALU.is_equal))
            step(tt(item_t, item_eq, rows_over(col_id[:, :], NOVF), ALU.mult))
            step(ve.tensor_reduce(r_list[:, 0:NOVF], item_t, AX.X, ALU.add))
            step(tt(item_t, item_eq, rows_over(expert_flat, NOVF), ALU.mult))
            step(ve.tensor_reduce(r_list[:, NOVF:2 * NOVF], item_t, AX.X, ALU.add))
            step(tt(r_there, r_total.broadcast_to([P, NOVF]), col_id[:, 0:NOVF], ALU.is_gt))
            step(stt(out=r_list[:, 0:NOVF], in0=r_there, scalar=-float(NO_ITEM), in1=r_list[:, 0:NOVF], op0=ALU.mult, op1=ALU.add))
            step(ts(r_list[:, 0:NOVF], r_list[:, 0:NOVF], float(NO_ITEM), None, ALU.add))
            first = r_there.rearrange("p (a b) -> p a b", b=2)[:, :, 0]
            step(ve.tensor_reduce(r_list[:, 2 * NOVF:2 * NOVF + 1], first, AX.X, ALU.add))
            step(ve.tensor_copy(ovf[:, 0:2 * NOVF + 1], r_list[:, 0:2 * NOVF + 1]))
            tell(e + "_items")
            with ve.Fori(0, PAIRS // 2 - 1) as i:
                pair_(1, i * 2 + 1, i)
                pair_(0, i * 2 + 2, i + 1)
            pair_(1, PAIRS - 1, PAIRS // 2 - 1)
            ovp, ovv = flag(e + "_ovf_pe"), flag(e + "_ovf_vec")
            n = ve.value_load(ovf[0:1, 2 * NOVF:2 * NOVF + 1], min_val=0, max_val=NOVF // 2)
            with ve.If(n > 0):
                moe_wait(ve, e, "scattered", PAIRS)
                with ve.Fori(0, n) as k_:
                    ve.wait_ge(ovp, k_ * OVF_PE + OVF_PE)
                    for x in range(2):
                        item = ve.value_load(ovf[0:1, bass.ds(k_ * 2 + x, 1)], min_val=0, max_val=NO_ITEM)
                        s3, sw3 = (a[:, 0, :, x * CAP:(x + 1) * CAP] for a in (S, Sw))
                        rank_x, w_x = (a[:, :, bass.ds(item, 1)].broadcast_to([P, TH, CAP]) for a in (rank3, wcomb3))
                        tt(s3, rows_over(col_id[:, 0:CAP], TH), rank_x, ALU.is_equal).then_inc(ovv, 1)
                        ve.wait_ge(ovv, k_ * OVF_VEC + (2 * x + 1))
                        tt(sw3, s3, w_x, ALU.mult).then_inc(ovv, 1)
                    ve.wait_ge(ovp, k_ * OVF_PE + (OVF_PE + 1))
                    for half, b in enumerate((4, 7)):
                        ve.tensor_copy(xg[:, 0, 4 * half:4 * half + 4, :], psum[:, b, :].rearrange("p (k c) -> p k c", k=4)).then_inc(ovv, 1)
                    ve.tensor_copy(SwT[:, :], psum[:, 6, 0:T]).then_inc(ovv, 1)
                    ve.wait_ge(flag(e + "_ovf_silu"), k_ + 1)
                    tt(hh[:, 0:FW], sg[:, 0:FW], psum[:, 6, 0:FW], ALU.mult).then_inc(ovv, 1)
                    ve.wait_ge(ovp, k_ * OVF_PE + (OVF_PE + 3))
                    ve.tensor_copy(hT[:, 0:F, :], psum[:, 5, 0:FW].rearrange("p (f c) -> p f c", f=F)).then_inc(ovv, 1)
                    ve.wait_ge(ovp, k_ * OVF_PE + (OVF_PE + 4))
                    for half, b in enumerate((4, 7)):
                        ve.tensor_copy(og[:, half * 512:(half + 1) * 512], psum[:, b, :]).then_inc(ovv, 1)

        rms_norm("x", h_tok)
        tell("h_tok")
        after(ve, "act", "ssm_dt")
        sc = lambda n: ssm_s[:, n, :]
        step(tt(s_adt, V("a_re"), s_dt, ALU.mult))
        tell("ssm_adt")
        step(tt(s_th, V("a_im"), s_dt, ALU.mult))
        step(ts(sc(6), s_th, 1.0 / (2 * np.pi), ROUND, ALU.mult, ALU.add))
        step(ts(sc(6), sc(6), -ROUND, None, ALU.add))
        step(stt(out=sc(7), in0=sc(6), scalar=-TWO_PI_HI, in1=s_th, op0=ALU.mult, op1=ALU.add))
        step(stt(out=sc(7), in0=sc(6), scalar=-TWO_PI_LO, in1=sc(7), op0=ALU.mult, op1=ALU.add))
        step(ts(sc(5), sc(7), SIN_MAX, -SIN_MAX, ALU.min, ALU.max))
        step(stt(out=sc(6), in0=sc(5), scalar=-1.0, in1=sc(5), op0=ALU.mult, op1=ALU.min))
        step(ts(sc(4), sc(6), np.pi / 2, None, ALU.add))
        tell("ssm_angle")
        take_T("hT", V("mix_g"))
        after(ve, "act", "ssm_sin")
        for k in range(LEVELS):
            counted(tt(sc(6), e_pow(k, 0), e_pow(k, 0), ALU.mult))
            n = counted(tt(sc(7), e_pow(k, 1), e_pow(k, 1), ALU.mult))
            counted(stt(out=e_pow(k + 1, 1), in0=e_pow(k, 0), scalar=2.0, in1=e_pow(k, 1), op0=ALU.mult, op1=ALU.mult))
            ve.wait_ge(chain, n)
            step(tt(e_pow(k + 1, 0), sc(6), sc(7), ALU.subtract))
        tell("ssm_powers2")
        are, aim = V("a_re"), V("a_im")
        step(tt(sc(6), s_mag, e_pow(0, 0), ALU.mult))
        step(ts(sc(6), sc(6), -1.0, None, ALU.add))
        step(tt(sc(7), s_mag, e_pow(0, 1), ALU.mult))
        step(tt(sc(8), are, are, ALU.mult))
        step(tt(sc(9), aim, aim, ALU.mult))
        step(tt(sc(8), sc(8), sc(9), ALU.add))
        step(ve.reciprocal(sc(8), sc(8)))
        step(tt(sc(9), sc(6), are, ALU.mult))
        step(tt(sc(10), sc(7), aim, ALU.mult))
        step(tt(sc(9), sc(9), sc(10), ALU.add))
        step(tt(sc(9), sc(9), sc(8), ALU.mult))
        step(tt(sc(10), sc(7), are, ALU.mult))
        step(tt(sc(11), sc(6), aim, ALU.mult))
        step(tt(sc(10), sc(10), sc(11), ALU.subtract))
        step(tt(sc(10), sc(10), sc(8), ALU.mult))
        after(ve, "pool", "zeros")
        cr, ci = (V(n).rearrange("p (j c) -> p j c", j=NJ) for n in ("c_re", "c_im"))
        fr_, fi_ = over(sc(9), P, NJ, 16), over(sc(10), P, NJ, 16)
        t1, t2 = (at(4096 + 256 * n, NJ, 16) for n in range(2))
        for c_ in range(2):
            step(tt(t1, cr, (fr_, fi_)[c_], ALU.mult))
            step(tt(t2, ci, (fi_, fr_)[c_], ALU.mult))
            step(tt(t1, t1, t2, (ALU.subtract, ALU.add)[c_]))
            if c_:
                step(ts(t1, t1, -1.0, None, ALU.mult))
            t1q = t1.rearrange("p (q j) c -> p q j c", q=NQ)
            blk = c_blk[:, c_, :, :].rearrange("p (q j) s -> p q j s", q=NQ)
            for jj in range(4):
                for o in range(2):
                    r = slice(o * HD, (o + 1) * HD)
                    col = (2 * jj + o) * 16
                    n = counted(ve.tensor_copy(blk[r, :, jj, col:col + 16], t1q[r, :, jj, :]))
            ve.wait_ge(chain, n)

        carry = ssm_s[:, 12:16, 0:4]

        def ssm_states(q):
            js = slice(4 * q, 4 * q + 4)
            c_t, s_t = powers[:, 0, js, :], powers[:, 1, js, :]
            c_both = c_t.unsqueeze(1).broadcast_to([P, 2, 4, HALF_T])
            for b in range(2, 6):
                full(ve, "bu", q, b)
            bu = psum[:, 2:6, :].rearrange("p (c b) (a t) -> p c (b a) t", c=2, a=2)
            for half in range(2):
                b_in = bu[:, :, :, half * HALF_T:(half + 1) * HALF_T]
                w_ = ws[:, half, :, :, :]
                counted(tt(tmp, c_both, b_in, ALU.mult))
                n0 = counted(tt(zs[:, 0, :, :], s_t, b_in[:, 1, :, :], ALU.mult))
                n1 = counted(tt(zs[:, 1, :, :], s_t, b_in[:, 0, :, :], ALU.mult))
                if q:
                    ve.wait_ge(flag("ssm_y"), 2 * (q - 1) + half + 1)
                ve.wait_ge(chain, n0)
                counted(tt(w_[:, 0, :, :], tmp[:, 0, :, :], zs[:, 0, :, :], ALU.add))
                ve.wait_ge(chain, n1)
                step(tt(w_[:, 1, :, :], tmp[:, 1, :, :], zs[:, 1, :, :], ALU.subtract))
                if half:
                    for b in range(2, 6):
                        ve.sem_inc(bank_free[b], 1)
                for c_ in range(2):
                    for jj in range(4):
                        mag = s_mag[:, 4 * q + jj:4 * q + jj + 1].broadcast_to([P, HALF_T])
                        init = carry[:, c_, jj:jj + 1] if half else 0.0
                        n = counted(ve.tensor_tensor_scan(zs[:, c_, jj, :], mag, w_[:, c_, jj, :], init, ALU.mult, ALU.add))
                ve.wait_ge(chain, n)
                counted(tt(tmp, c_both, zs, ALU.mult))
                n0 = counted(tt(w_[:, 0, :, :], s_t, zs[:, 1, :, :], ALU.mult))
                n1 = counted(tt(w_[:, 1, :, :], s_t, zs[:, 0, :, :], ALU.mult))
                ve.wait_ge(chain, n0)
                counted(tt(w_[:, 0, :, :], tmp[:, 0, :, :], w_[:, 0, :, :], ALU.subtract))
                ve.wait_ge(chain, n1)
                step(tt(w_[:, 1, :, :], tmp[:, 1, :, :], w_[:, 1, :, :], ALU.add))
                tell(f"ssm_state{2 * q + half}")
                if half == 0:
                    c1, s1 = e_pow(LEVELS, 0)[:, js], e_pow(LEVELS, 1)[:, js]
                    zr, zi = zs[:, 0, :, HALF_T - 1], zs[:, 1, :, HALF_T - 1]
                    step(tt(carry[:, 2, :], c1, zr, ALU.mult))
                    step(tt(carry[:, 3, :], s1, zi, ALU.mult))
                    step(tt(carry[:, 0, :], carry[:, 2, :], carry[:, 3, :], ALU.subtract))
                    step(tt(carry[:, 2, :], c1, zi, ALU.mult))
                    step(tt(carry[:, 3, :], s1, zr, ALU.mult))
                    step(tt(carry[:, 1, :], carry[:, 2, :], carry[:, 3, :], ALU.add))

        def ssm_skip(q):
            src = full(ve, "y", q)
            read_out(stt(out=yg[:, q, :], in0=uT[:, q, :], scalar=V("d_skip")[:, q:q + 1], in1=src[:, 0:T],
                         op0=ALU.mult, op1=ALU.add), "y", q)

        def take_qk(w, c0):
            for th in range(TH):
                src = full(ve, w, th)
                read_out(ve.tensor_copy(qk_tok[:, th, c0:c0 + 512], src), w, th)

        take_qk("q", 0)
        after(ve, "pool", "powers")
        ssm_states(0)
        take_qk("k", 512)
        for w in "qk":
            for th in range(TH):
                evacuated(ve, w, th)
        for th in range(TH):
            step(tt(square_junk, qk_tok[:, th, :], qk_tok[:, th, :], ALU.mult))
            step(ve.tensor_reduce(qk_r[:, th * 16:(th + 1) * 16], square_junk.rearrange("p (h d) -> p h d", h=16), AX.X, ALU.add))
        step(ts(qk_r, qk_r, 1.0 / HD, 1e-6, ALU.mult, ALU.add))
        tell("qk_ms")
        src = full(ve, "f")[:, 0:16].rearrange("p (a h) -> p a h", a=2)
        fr = f_raw.rearrange("p (a h) -> p a h", a=2)
        read_out(tt(fr, src, rows_over(brow[:, 0:8], TH), ALU.add), "f")
        evacuated(ve, "f")
        step(stt(out=f_abs, in0=f_raw, scalar=-1.0, in1=f_raw, op0=ALU.mult, op1=ALU.max))
        tell("f_abs")
        after(ve, "act", "qk_rms")
        step(ve.reciprocal(qk_r, qk_r))
        for th in range(TH):
            v3_ = qk_tok[:, th, :].rearrange("p (h d) -> p h d", h=16)
            step(tt(v3_, v3_, over(qk_r[:, th * 16:(th + 1) * 16], P, 16, HD), ALU.mult))
        tell("qk_tok")
        after(ve, "act", "f_ln")
        lf_pos = lf[:, 0, :, :].rearrange("p a h -> p (a h)")
        lf_neg = lf[:, 1, :, :].rearrange("p a h -> p (a h)")
        step(stt(out=lf_pos, in0=f_raw, scalar=0.0, in1=f_l, op0=ALU.min, op1=ALU.subtract))
        step(ts(lf_neg, lf_pos, -1.0, None, ALU.mult))
        tell("logf")
        ssm_states(1)
        ssm_skip(0)
        after(ve, "pool", "masks")
        src = full(ve, "F")
        step(ve.tensor_copy(Ft, src[:, 0:16].rearrange("p (a h) -> p a h", a=2)))
        read_out(ve.tensor_copy(nF[0:8, :], src[0:8, 128:128 + T]), "F")
        ssm_states(2)
        ssm_skip(1)
        ssm_states(3)
        ssm_skip(2)
        for th in range(TH):
            src = full(ve, "qT", th).rearrange("p (j t) -> p j t", j=4)
            split_heads(("qT", th), qz1[:, :, th * P:(th + 1) * P], src, 0, V("qg"), HD ** -0.5)
        for th in range(TH):
            src = full(ve, "kT", th).rearrange("p (j t) -> p j t", j=4)
            read_out(ts(kT1[:, :, th * P:(th + 1) * P], src, V("kg"), None, ALU.mult), "kT", th)
        ssm_skip(3)
        attention("at1", 8, ALU.add, lambda h, th: Ft[:, th, h:h + 1], True)
        for n in range(2):
            evacuated(ve, "glu", n)
        step(tt(y_ssm, y_ssm, yg, ALU.mult))
        tell("y_ssm")
        for n in range(4):
            src = full(ve, "pa", n).rearrange("p (a t) -> p a t", a=2)
            read_out(tt(mixedT[:, 2 * n:2 * n + 2, :], src, gates[:, 2 * n:2 * n + 2, :], ALU.mult), "pa", n)
            src = full(ve, "ps", n).rearrange("p (a t) -> p a t", a=2)
            read_out(tt(mix_tmp, src, gates[:, 8 + 2 * n:10 + 2 * n, :], ALU.mult), "ps", n)
            evacuated(ve, "pa", n)
            evacuated(ve, "ps", n)
            tt(mixedT[:, 2 * n:2 * n + 2, :], mixedT[:, 2 * n:2 * n + 2, :], mix_tmp, ALU.add).then_inc(flag("mixed"), 1)
            ve.wait_ge(flag("mixed"), n + 1)
        take_T("memT")
        residual("res1", 1.0, False)
        tell("x1")
        ve.wait_ge(flag("gain_loaded"), 16)
        rms_norm("x1", xh, gain, ("e1_tok0", "e1_tok"))
        moe("e1")
        moe_sum("e1", 1.0, False)

        take_T("x2T")
        ve.memset(hpad[:, :, 0:PAD], 0.0)
        step(ve.memset(qz2, 0.0))
        src = full(ve, "qm2").rearrange("p (a t) -> p a t", a=2)
        split_heads(("qm2",), qz2, src, 0, None)
        tap = flag("conv_tap")
        dw = V("dw_w")

        def glu_in(n):
            after(ve, "act", f"conv_gate{n}")
            src = full(ve, "conv", n)
            read_out(tt(hpad[:, n, PAD:PAD + T], src[:, 0:T], gatez[:, n, :], ALU.mult), "conv", n)
            evacuated(ve, "conv", n)
            tell(f"glu_in{n}")

        def depthwise(n0):
            taps_before = n0 * TAPS
            for n in (n0, n0 + 1):
                ts(conv[:, n, :], hpad[:, n, 0:T], dw[:, n * TAPS:n * TAPS + 1], V("dw_b")[:, n:n + 1], ALU.mult, ALU.add).then_inc(tap, 1)
            with ve.Fori(0, PAD // TAP_STEP) as i:
                for d in range(TAP_STEP):
                    for n in (n0, n0 + 1):
                        ve.wait_ge(tap, i * (2 * TAP_STEP) + (taps_before + 2 * d + n - n0 + 1))
                        stt(out=conv[:, n, :], in0=hpad[:, n, bass.ds(i * TAP_STEP + (d + 1), T)],
                            scalar=dw[:, bass.ds(i * TAP_STEP + (d + 1 + n * TAPS), 1)],
                            in1=conv[:, n, :], op0=ALU.mult, op1=ALU.add).then_inc(tap, 1)

        glu_in(0)
        glu_in(1)
        depthwise(0)
        for n in range(2, MT):
            glu_in(n)
        attention("at2", 4, ALU.mult, lambda h, th: HD ** -0.5, False)
        depthwise(2)
        ve.wait_ge(tap, VEC_TILES * TAPS)
        tell("conv_done")
        src = full(ve, "mean")
        read_out(ts(stat[:, 0, :], src[:, 0:T], 1.0 / MIX, None, ALU.mult), "mean")
        evacuated(ve, "mean")
        for n in range(0, MT, 2):
            step(tt(conv[:, n:n + 2, :], conv[:, n:n + 2, :], rows_over(stat[:, 0, :], 2), ALU.subtract))
            tell(f"conv_off{n}")
        src = full(ve, "var")
        read_out(ts(stat[:, 1, :], src[:, 0:T], 1.0 / MIX, 1e-5, ALU.mult, ALU.add), "var")
        evacuated(ve, "var")
        tell("conv_var")
        after(ve, "act", "conv_std")
        step(ve.reciprocal(stat[:, 1, :], stat[:, 1, :]))
        for n in range(MT):
            tt(conv[:, n, :], conv[:, n, :], stat[:, 1, :], ALU.mult).then_inc(flag("conv_norm"), 1)
        residual("res2", ALPHA, True)
        layer_norm("ln21", 1, ("e2_tok0", "e2_tok"))
        moe("e2")
        moe_sum("e2", ALPHA, True)
        layer_norm("ln22", 3, ("x3_0", "x3"))

        take_T("x3T")
        step(ve.memset(qz3m, 0.0))
        src = full(ve, "qm3").rearrange("p (a t) -> p a t", a=2)
        split_heads(("qm3",), qz3m, src, 0, None)
        step(ve.memset(qz3, 0.0))

        def take_queries(n):
            src = full(ve, "mq", n).rearrange("p (a t) -> p a t", a=2)
            split_heads(("mq", n), qz3, src, 2 * n, None)

        take_queries(0)
        attention("at3m", 4, ALU.mult, lambda h, th: HD ** -0.5, False)
        take_queries(1)
        take_queries(2)
        attention("at3", 12, ALU.mult, lambda h, th: HD ** -0.5, True)
        residual("res3", ALPHA, True)
        layer_norm("ln31", 5, ("e3_tok0", "e3_tok"))
        moe("e3")
        moe_sum("e3", ALPHA, True)
        layer_norm("ln32", 7, ("x_final0", "x_final"))


def _tiles(w, c0, c1, slot=True):
    w = w[:, c0:c1]
    k = w.shape[0] // P
    w = w.reshape(k, P, c1 - c0).transpose(1, 0, 2)
    if k * (c1 - c0) < SLOT:
        out = np.zeros((P, SLOT), np.float32)
        if k == KD:
            out.reshape(P, KD, 512)[:, :, :c1 - c0] = w
        else:
            out[:, :k * (c1 - c0)] = w.reshape(P, -1)
        return out
    return w.reshape(P, -1)


def _experts(w):
    e, r, c = w.shape
    return np.ascontiguousarray(w.reshape(e, r // P, P, c).transpose(0, 2, 1, 3).reshape(e, P, (r // P) * c))


def _layout(a):
    w_in = a["w_in"][0]
    chunks = {"u": _tiles(w_in, 1544, 2056), "q": _tiles(w_in, 0, 512), "k": _tiles(w_in, 512, 1024),
              "v": _tiles(w_in, 1024, 1536), "glu": _tiles(a["w_glu"][0], 0, 512),
              "pa": _tiles(a["w_proj_attn"][0], 0, D), "ps": _tiles(a["w_proj_ssm"][0], 0, D),
              "memkv": _tiles(a["w_mem_kv_2"], 0, 512)}
    for n in range(4):
        chunks[f"g{n}"] = _tiles(w_in, 2056 + 512 * n, 2568 + 512 * n)
    for name, w in (("wo", a["w_out"][0]), ("w2o", a["w_o_2"][0]), ("w3o", a["w_o_2"][1])):
        for n in range(2):
            chunks[f"{name}{n}"] = _tiles(w[512 * n:512 * (n + 1)], 0, D)
    cw = a["conv_w_in_2"][0]
    for n in range(3):
        cols = [cw[:, c + P * (2 * n + m):c + P * (2 * n + m + 1)] for m in range(2) for c in (0, MIX)]
        chunks[f"c{n}"] = _tiles(np.concatenate(cols, 1), 0, 512)
    chunks["c3"] = _tiles(cw, 2 * MIX, 2 * MIX + 256)
    mw = a["moba_w_in_2"][0]
    for n in range(5):
        chunks[f"m{n}"] = _tiles(mw, 512 * n, 512 * (n + 1))
    out = {"stream": np.stack([chunks[c] for c in CHUNKS])}

    by_part = lambda v: v.reshape(-1, P).T
    state = lambda v: v.reshape(NJ, 2 * HD).T
    cmat = lambda c: c.transpose(0, 2, 1).reshape(NJ, P, 16).transpose(1, 0, 2).reshape(P, NJ * 16)
    ldt = np.repeat(a["ssm_log_dt"][0][:, None], HD, axis=1)
    parts = {"mix_g": by_part(a["norm_mix_g"][0]), "qg": np.tile(a["q_norm_g"][0], 2)[:, None],
             "kg": np.tile(a["k_norm_g"][0], 2)[:, None], "a_re": state(a["ssm_A_re"][0]), "a_im": state(a["ssm_A_im"][0]),
             "log_dt": state(ldt), "d_skip": by_part(a["ssm_D"][0]), "dw_b": by_part(a["conv_dw_b_2"][0]),
             "ln_g": by_part(a["conv_ln_g_2"][0]), "ln_b": by_part(a["conv_ln_b_2"][0]),
             "dw_w": a["conv_dw_w_2"][0].T.reshape(MT, P, TAPS).transpose(1, 0, 2).reshape(P, MT * TAPS),
             "c_re": cmat(a["ssm_C_re"][0]), "c_im": cmat(a["ssm_C_im"][0])}
    out["vec"] = np.concatenate([parts[n] for n in VEC], 1)
    blk = np.zeros((2, P, NJ, P), np.float32)
    for c, name in enumerate(("ssm_B_re", "ssm_B_im")):
        b = a[name][0]
        for g in range(32):
            j, o = g // 2, g % 2
            r = (g % 8) * 16
            blk[c, r:r + 16, j, o * HD:(o + 1) * HD] = b[g].T
    out["b_blk"] = blk
    out["wf"] = w_in[:, 1536:1544].reshape(KD, P, 8).transpose(1, 0, 2)
    rg = [a["w_router_group"][0], a["w_rg_2"][0], a["w_rg_2"][1]]
    re = [a["w_router_expert"][0], a["w_re_2"][0], a["w_re_2"][1]]
    out["wr"] = np.stack([np.concatenate([g, e], 1).reshape(KD, P, NR).transpose(1, 0, 2) for g, e in zip(rg, re)])
    out["brow"] = np.concatenate([a["b_forget"][0], a["b_router_group"][0], a["b_router_expert"][0],
                                  a["b_rg_2"][0], a["b_re_2"][0], a["b_rg_2"][1], a["b_re_2"][1]])[None, :]
    rows = [a["norm_ffn_g"][0]]
    for n in range(2):
        rows += [a["ln1_g_2"][n], a["ln1_b_2"][n], a["ln2_g_2"][n], a["ln2_b_2"][n]]
    out["rows"] = np.stack(rows)
    out["x"] = a["x"][0]
    out["mem"] = a["mem_2"][0]
    for e, (g, u, d) in (("e1", (a["w_expert_gate"][0], a["w_expert_up"][0], a["w_expert_down"][0])),
                         ("e2", tuple(a[n][0].reshape(NE, *a[n].shape[3:]) for n in ("w_gate_2", "w_up_2", "w_down_2"))),
                         ("e3", tuple(a[n][1].reshape(NE, *a[n].shape[3:]) for n in ("w_gate_2", "w_up_2", "w_down_2")))):
        out[e + "_gate"], out[e + "_up"], out[e + "_down"] = _experts(g), _experts(u), _experts(d)
    return {n: np.ascontiguousarray(v) for n, v in out.items()}


def kernel(**inputs):
    import concourse.bacc as _bacc
    from concourse.bass_utils import run_bass_kernel_spmd as _run

    arrays = _layout({n: np.asarray(v) for n, v in inputs.items()})
    nc = _bacc.Bacc("TRN2", target_bir_lowering=False, num_devices=1)
    named = {n: nc.dram_tensor(f"in_{n}", v.shape, F32, kind="ExternalInput").ap() for n, v in arrays.items()}
    out = nc.dram_tensor("out_x", (T, D), F32, kind="ExternalOutput").ap()
    build(nc, named, out)
    r = _run(nc, [{f"in_{n}": v for n, v in arrays.items()}], core_ids=[0])
    return r.results[0]["out_x"].reshape(1, T, D)
```
